# Optimizing a Trainium2 kernel written in Bass

```python
import jax, jax.numpy as jnp
from jax import lax
import numpy as np

D_MODEL = 1024
BATCH = 1
SEQ = 1024
DEPTH = 1

CHUNK = 64
D_MIX = D_MODEL
D_MLSTM = D_MIX // 2
D_POOL = D_MIX - D_MLSTM
N_MLSTM_HEADS = 4
HEAD_DIM = D_MLSTM // N_MLSTM_HEADS
POOL_WINDOWS = (2, 4, 8, 16)
N_POOL_GROUPS = len(POOL_WINDOWS)
POOL_GROUP_DIM = D_POOL // N_POOL_GROUPS
CONV_WIDTH = 4
D_FF = 4 * D_MODEL
OFF_Q = 0
OFF_K = OFF_Q + D_MLSTM
OFF_V = OFF_K + D_MLSTM
OFF_G = OFF_V + D_MLSTM
OFF_O = OFF_G + 2 * N_MLSTM_HEADS
OFF_P = OFF_O + D_MLSTM
D_IN = OFF_P + D_POOL
ALPHA = (2.0 * DEPTH) ** 0.25
BETA = (8.0 * DEPTH) ** -0.25
LN_EPS = 1e-5


def layer_norm(x, g, b):
    xf = x.astype(jnp.float32)
    mu = xf.mean(-1, keepdims=True)
    var = jnp.square(xf - mu).mean(-1, keepdims=True)
    return ((xf - mu) * lax.rsqrt(var + LN_EPS) * g.astype(jnp.float32) + b.astype(jnp.float32)).astype(x.dtype)

def causal_conv(x, w):
    S = x.shape[1]
    xp = jnp.pad(x, ((0, 0), (CONV_WIDTH - 1, 0), (0, 0)))
    y = w[0] * xp[:, 0:S]
    for j in range(1, CONV_WIDTH):
        y = y + w[j] * xp[:, j:j + S]
    return y

def mlstm_chunkwise(q, k, v, i_pre, f_pre):
    B, S, H, Dh = q.shape
    NC = S // CHUNK

    def to_chunks(t):
        t = t.reshape((B, NC, CHUNK, H) + t.shape[3:])
        return jnp.moveaxis(t, 3, 1)

    q, k, v = to_chunks(q), to_chunks(k), to_chunks(v)
    i_pre = to_chunks(i_pre)
    logf = to_chunks(jax.nn.log_sigmoid(f_pre))
    a = jnp.cumsum(logf, axis=-1)
    g = a[..., -1]

    w = g[..., None] - a + i_pre
    m_loc = w.max(-1)
    e = jnp.exp(w - m_loc[..., None])
    C_loc = jnp.einsum('bhnl,bhnlv,bhnlk->bhnvk', e, v, k)
    n_loc = jnp.einsum('bhnl,bhnlk->bhnk', e, k)

    def step(carry, inp):
        C, n, m = carry
        g_c, m_c, C_c, n_c = inp
        m_new = jnp.maximum(g_c + m, m_c)
        s_old = jnp.exp(g_c + m - m_new)
        s_new = jnp.exp(m_c - m_new)
        C_new = s_old[..., None, None] * C + s_new[..., None, None] * C_c
        n_new = s_old[..., None] * n + s_new[..., None] * n_c
        return (C_new, n_new, m_new), (C, n, m)

    init = (jnp.zeros((B, H, Dh, Dh), jnp.float32),
            jnp.zeros((B, H, Dh), jnp.float32),
            jnp.zeros((B, H), jnp.float32))
    xs = (jnp.moveaxis(g, 2, 0), jnp.moveaxis(m_loc, 2, 0),
          jnp.moveaxis(C_loc, 2, 0), jnp.moveaxis(n_loc, 2, 0))
    _, (C_prev, n_prev, m_prev) = lax.scan(step, init, xs)
    C_prev = jnp.moveaxis(C_prev, 0, 2)
    n_prev = jnp.moveaxis(n_prev, 0, 2)
    m_prev = jnp.moveaxis(m_prev, 0, 2)

    causal = jnp.tril(jnp.ones((CHUNK, CHUNK), dtype=bool))
    Dlog = a[..., :, None] - a[..., None, :] + i_pre[..., None, :]
    Dlog = jnp.where(causal, Dlog, -jnp.inf)
    m_inter = a + m_prev[..., None]
    m_t = jnp.maximum(m_inter, Dlog.max(-1))
    P = jnp.exp(Dlog - m_t[..., None])
    s_inter = jnp.exp(m_inter - m_t)
    qk = jnp.einsum('bhnld,bhnsd->bhnls', q, k) * P
    num = (jnp.einsum('bhnls,bhnsv->bhnlv', qk, v)
           + s_inter[..., None] * jnp.einsum('bhnvk,bhnlk->bhnlv', C_prev, q))
    den = qk.sum(-1) + s_inter * jnp.einsum('bhnk,bhnlk->bhnl', n_prev, q)
    h = num / jnp.maximum(jnp.abs(den), jnp.exp(-m_t))[..., None]
    return jnp.moveaxis(h, 1, 3).reshape(B, S, H * Dh)

def multiscale_pool(p, w_pool, scale):
    B, S, _ = p.shape
    pf = p.astype(jnp.float32)
    cs = jnp.cumsum(pf, axis=1)
    count = jnp.arange(1, S + 1, dtype=jnp.float32)[:, None]
    outs = []
    for gi, win in enumerate(POOL_WINDOWS):
        lo, hi = gi * POOL_GROUP_DIM, (gi + 1) * POOL_GROUP_DIM
        c = cs[..., lo:hi]
        lagged = jnp.pad(c[:, :S - win], ((0, 0), (win, 0), (0, 0)))
        mean = (c - lagged) / jnp.minimum(count, float(win))
        outs.append(mean - pf[..., lo:hi])
    d = jnp.stack(outs, axis=2)
    y = jnp.einsum('bsgc,gcd->bsgd', d, w_pool.astype(jnp.float32)).reshape(B, S, D_POOL)
    return (y * scale.astype(jnp.float32)).astype(p.dtype)

def hybrid_mixer(x, w_in, b_gate, w_conv, hn_g, w_pool, pool_scale, w_out):
    B, S, _ = x.shape
    u = x @ w_in
    qk = jax.nn.silu(causal_conv(u[..., OFF_Q:OFF_V], w_conv)).astype(jnp.float32)
    q = qk[..., :D_MLSTM].reshape(B, S, N_MLSTM_HEADS, HEAD_DIM)
    k = qk[..., D_MLSTM:].reshape(B, S, N_MLSTM_HEADS, HEAD_DIM) * (HEAD_DIM ** -0.5)
    v = u[..., OFF_V:OFF_G].astype(jnp.float32).reshape(B, S, N_MLSTM_HEADS, HEAD_DIM)
    gates = (u[..., OFF_G:OFF_O] + b_gate).astype(jnp.float32)
    i_pre = gates[..., :N_MLSTM_HEADS]
    f_pre = gates[..., N_MLSTM_HEADS:]
    h = mlstm_chunkwise(q, k, v, i_pre, f_pre).reshape(B, S, N_MLSTM_HEADS, HEAD_DIM)
    mu = h.mean(-1, keepdims=True)
    var = jnp.square(h - mu).mean(-1, keepdims=True)
    h = ((h - mu) * lax.rsqrt(var + LN_EPS)).reshape(B, S, D_MLSTM) * hn_g.astype(jnp.float32)
    y_m = (jax.nn.sigmoid(u[..., OFF_O:OFF_P].astype(jnp.float32)) * h).astype(x.dtype)
    y_p = multiscale_pool(u[..., OFF_P:D_IN], w_pool, pool_scale)
    return jnp.concatenate([y_m, y_p], axis=-1) @ w_out

def squared_relu_mlp(x, w1, w2):
    return jnp.square(jax.nn.relu(x @ w1)) @ w2

def first_inputs(seed: int = 0) -> dict:
    key = jax.random.key(seed)
    ks = jax.random.split(key, 16)
    L = DEPTH
    nrm = jax.random.normal
    x = nrm(ks[0], (BATCH, SEQ, D_MODEL), jnp.float32)
    w_in = nrm(ks[1], (L, D_MODEL, D_IN), jnp.float32) * D_MODEL ** -0.5
    b_i = 0.1 * nrm(ks[2], (L, N_MLSTM_HEADS), jnp.float32)
    b_f = jnp.linspace(3.0, 6.0, N_MLSTM_HEADS, dtype=jnp.float32)[None] + 0.1 * nrm(ks[3], (L, N_MLSTM_HEADS), jnp.float32)
    b_gate = jnp.concatenate([b_i, b_f], axis=-1)
    w_conv = nrm(ks[4], (L, CONV_WIDTH, 2 * D_MLSTM), jnp.float32) * CONV_WIDTH ** -0.5
    hn_g = 1.0 + 0.02 * nrm(ks[5], (L, D_MLSTM), jnp.float32)
    w_pool = nrm(ks[6], (L, N_POOL_GROUPS, POOL_GROUP_DIM, POOL_GROUP_DIM), jnp.float32) * POOL_GROUP_DIM ** -0.5
    pool_scale = 1.0 + 0.02 * nrm(ks[7], (L, D_POOL), jnp.float32)
    w_out = nrm(ks[8], (L, D_MIX, D_MODEL), jnp.float32) * (D_MIX ** -0.5) * BETA
    ln1_g = 1.0 + 0.02 * nrm(ks[9], (L, D_MODEL), jnp.float32)
    ln1_b = 0.02 * nrm(ks[10], (L, D_MODEL), jnp.float32)
    w_ff1 = nrm(ks[11], (L, D_MODEL, D_FF), jnp.float32) * D_MODEL ** -0.5
    w_ff2 = nrm(ks[12], (L, D_FF, D_MODEL), jnp.float32) * (D_FF ** -0.5) * BETA
    ln2_g = 1.0 + 0.02 * nrm(ks[13], (L, D_MODEL), jnp.float32)
    ln2_b = 0.02 * nrm(ks[14], (L, D_MODEL), jnp.float32)
    return {"x": x, "w_in": w_in, "b_gate": b_gate, "w_conv": w_conv, "hn_g": hn_g,
            "w_pool": w_pool, "pool_scale": pool_scale, "w_out": w_out,
            "ln1_g": ln1_g, "ln1_b": ln1_b, "w_ff1": w_ff1, "w_ff2": w_ff2,
            "ln2_g": ln2_g, "ln2_b": ln2_b}

def first_block(x, w_in, b_gate, w_conv, hn_g, w_pool, pool_scale, w_out,
              ln1_g, ln1_b, w_ff1, w_ff2, ln2_g, ln2_b):
    for l in range(DEPTH):
        mix = hybrid_mixer(x, w_in[l], b_gate[l], w_conv[l], hn_g[l], w_pool[l], pool_scale[l], w_out[l])
        x = layer_norm(ALPHA * x + mix, ln1_g[l], ln1_b[l])
        x = layer_norm(ALPHA * x + squared_relu_mlp(x, w_ff1[l], w_ff2[l]), ln2_g[l], ln2_b[l])
    return x


_first_inputs = first_inputs


def first_inputs(seed=0):
    import zlib

    import numpy as np

    out = dict(_first_inputs(seed))
    spreads = {}
    factors = {'hn_g': 8.0,
     'pool_scale': 8.0,
     'ln1_g': 2.729,
     'ln1_b': 2.761,
     'ln2_g': 2.741,
     'ln2_b': 2.873}
    for name, (base, spread) in spreads.items():
        noise = np.random.default_rng([zlib.crc32(name.encode()), seed]).standard_normal(out[name].shape)
        drawn = base * np.exp(spread * noise) if base else spread * noise
        out[name] = __import__('jax').numpy.asarray(drawn.astype(out[name].dtype))
    for name, factor in factors.items():
        out[name] = (out[name] * factor).astype(out[name].dtype)
    return out


_narrow_inputs = first_inputs


def first_inputs(seed=0):

    out = dict(_narrow_inputs(seed))
    wider = {'hn_g': 5.59, 'pool_scale': 3.61, 'ln2_g': 3.07, 'ln2_b': 3.08}
    for name, times in wider.items():
        mean = out[name].mean()
        out[name] = (mean + times * (out[name] - mean)).astype(out[name].dtype)
    return out


N_META = 16
Q_BLOCK = 128
D_CONV = 512
CONV_WIDTH_2 = 31
N_HEADS = 8
QK_NOPE = 64
QK_ROPE = 32
V_HEAD = 64
D_ATTN = N_HEADS * V_HEAD
Q_LORA = 384
KV_LORA = 256
ROPE_THETA = 10000.0
D_MIX_2 = D_CONV + D_ATTN
D_IN_2 = 2 * D_CONV + Q_LORA + KV_LORA + QK_ROPE
D_FF_2 = 2816
FFN_CONV_WIDTH = 3
EPS = 1e-6
NEG = -1e30


def rms_norm(x, g):
    xf = x.astype(jnp.float32)
    y = xf * lax.rsqrt(jnp.mean(xf * xf, axis=-1, keepdims=True) + EPS)
    return (y * g.astype(jnp.float32)).astype(x.dtype)

def layer_norm_2(x, g, b):
    xf = x.astype(jnp.float32)
    mu = jnp.mean(xf, axis=-1, keepdims=True)
    var = jnp.mean(jnp.square(xf - mu), axis=-1, keepdims=True)
    y = (xf - mu) * lax.rsqrt(var + EPS)
    return (y * g.astype(jnp.float32) + b.astype(jnp.float32)).astype(x.dtype)

def causal_depthwise_conv(x, w, b):
    k = w.shape[0]
    y = lax.conv_general_dilated(
        x, w[:, None, :].astype(x.dtype), window_strides=(1,), padding=[(k - 1, 0)],
        dimension_numbers=('NWC', 'WIO', 'NWC'), feature_group_count=x.shape[-1])
    return y + b.astype(x.dtype)

def rope(x, cos, sin):
    half = x.shape[-1] // 2
    x1, x2 = x[..., :half], x[..., half:]
    return jnp.concatenate([x1 * cos - x2 * sin, x2 * cos + x1 * sin], axis=-1)

def block_causal_attention(q, k, v, chunk_id):
    b, l, h, dqk = q.shape
    dv = v.shape[-1]
    nblk = l // Q_BLOCK
    qb = q.reshape(b, nblk, Q_BLOCK, h, dqk).transpose(1, 0, 2, 3, 4)
    cb = chunk_id.reshape(nblk, Q_BLOCK)
    scale = dqk ** -0.5

    def one_block(args):
        qi, ci = args
        s = jnp.einsum('bqhd,bkhd->bhqk', qi, k, preferred_element_type=jnp.float32) * scale
        visible = ci[:, None] >= chunk_id[None, :]
        s = jnp.where(visible[None, None], s, NEG)
        p = jax.nn.softmax(s, axis=-1)
        return jnp.einsum('bhqk,bkhd->bqhd', p.astype(v.dtype), v)

    o = lax.map(one_block, (qb, cb))
    return o.transpose(1, 0, 2, 3, 4).reshape(b, l, h * dv)

def hybrid_layer(h, cos, sin, chunk_id, mix_norm_g, w_in, q_norm_g, w_uq, kv_norm_g, w_ukv,
                 conv_w, conv_b, conv_ln_g, conv_ln_b, conv_out_g, attn_out_g, w_out,
                 ffn_norm_g, w_ffn_up, ffn_conv_w, ffn_conv_b, w_ffn_down):
    b, l, _ = h.shape
    n = rms_norm(h, mix_norm_g)
    z = n @ w_in.astype(h.dtype)
    a, gate, c_q, c_kv, k_r = jnp.split(
        z, [D_CONV, 2 * D_CONV, 2 * D_CONV + Q_LORA, 2 * D_CONV + Q_LORA + KV_LORA], axis=-1)

    u = a * jax.nn.sigmoid(gate)
    u = causal_depthwise_conv(u, conv_w, conv_b)
    u = jax.nn.silu(layer_norm_2(u, conv_ln_g, conv_ln_b))

    q = (rms_norm(c_q, q_norm_g) @ w_uq.astype(h.dtype)).reshape(b, l, N_HEADS, QK_NOPE + QK_ROPE)
    kv = (rms_norm(c_kv, kv_norm_g) @ w_ukv.astype(h.dtype)).reshape(b, l, N_HEADS, QK_NOPE + V_HEAD)
    q_nope, q_rot = q[..., :QK_NOPE], q[..., QK_NOPE:]
    k_nope, v = kv[..., :QK_NOPE], kv[..., QK_NOPE:]
    q_rot = rope(q_rot, cos[:, None, :], sin[:, None, :])
    k_rot = rope(k_r, cos, sin)
    qf = jnp.concatenate([q_nope, q_rot], axis=-1)
    kf = jnp.concatenate(
        [k_nope, jnp.broadcast_to(k_rot[:, :, None, :], (b, l, N_HEADS, QK_ROPE))], axis=-1)
    o = block_causal_attention(qf, kf, v, chunk_id)

    mix = jnp.concatenate([rms_norm(u, conv_out_g), rms_norm(o, attn_out_g)], axis=-1)
    h = h + mix @ w_out.astype(h.dtype)

    n2 = rms_norm(h, ffn_norm_g)
    up = causal_depthwise_conv(n2 @ w_ffn_up.astype(h.dtype), ffn_conv_w, ffn_conv_b)
    g, val = up[..., :D_FF_2], up[..., D_FF_2:]
    return h + (jax.nn.silu(g) * val) @ w_ffn_down.astype(h.dtype)

def second_inputs(seed: int = 0) -> dict:
    key = jax.random.key(seed)
    ks = jax.random.split(key, 24)
    f32 = jnp.float32

    def nrm(k, shape, scale):
        return jax.random.normal(k, shape, f32) * scale

    def gain(k, shape):
        return 1.0 + 0.02 * jax.random.normal(k, shape, f32)

    L = DEPTH
    return {
        'x': jax.random.normal(ks[0], (BATCH, SEQ, D_MODEL), f32),
        'meta_tokens': nrm(ks[1], (N_META, D_MODEL), 1.0),
        'mix_norm_g': gain(ks[2], (L, D_MODEL)),
        'w_in': nrm(ks[3], (L, D_MODEL, D_IN_2), D_MODEL ** -0.5),
        'q_norm_g': gain(ks[4], (L, Q_LORA)),
        'w_uq': nrm(ks[5], (L, Q_LORA, N_HEADS * (QK_NOPE + QK_ROPE)), Q_LORA ** -0.5),
        'kv_norm_g': gain(ks[6], (L, KV_LORA)),
        'w_ukv': nrm(ks[7], (L, KV_LORA, N_HEADS * (QK_NOPE + V_HEAD)), KV_LORA ** -0.5),
        'conv_w': nrm(ks[8], (L, CONV_WIDTH_2, D_CONV), CONV_WIDTH_2 ** -0.5),
        'conv_b': nrm(ks[9], (L, D_CONV), 0.02),
        'conv_ln_g': gain(ks[10], (L, D_CONV)),
        'conv_ln_b': nrm(ks[11], (L, D_CONV), 0.02),
        'conv_out_g': gain(ks[12], (L, D_CONV)),
        'attn_out_g': gain(ks[13], (L, D_ATTN)),
        'w_out': nrm(ks[14], (L, D_MIX_2, D_MODEL), D_MIX_2 ** -0.5),
        'ffn_norm_g': gain(ks[15], (L, D_MODEL)),
        'w_ffn_up': nrm(ks[16], (L, D_MODEL, 2 * D_FF_2), D_MODEL ** -0.5),
        'ffn_conv_w': nrm(ks[17], (L, FFN_CONV_WIDTH, 2 * D_FF_2), FFN_CONV_WIDTH ** -0.5),
        'ffn_conv_b': nrm(ks[18], (L, 2 * D_FF_2), 0.02),
        'w_ffn_down': nrm(ks[19], (L, D_FF_2, D_MODEL), D_FF_2 ** -0.5),
        'final_norm_g': gain(ks[20], (D_MODEL,)),
    }

def second_block(x, meta_tokens, mix_norm_g, w_in, q_norm_g, w_uq, kv_norm_g, w_ukv,
              conv_w, conv_b, conv_ln_g, conv_ln_b, conv_out_g, attn_out_g, w_out,
              ffn_norm_g, w_ffn_up, ffn_conv_w, ffn_conv_b, w_ffn_down, final_norm_g):
    b, s, d = x.shape
    l_real = N_META + s
    l_pad = ((l_real + Q_BLOCK - 1) // Q_BLOCK) * Q_BLOCK
    meta = jnp.broadcast_to(meta_tokens[None].astype(x.dtype), (b, N_META, d))
    pad = jnp.zeros((b, l_pad - l_real, d), x.dtype)
    h = jnp.concatenate([meta, x, pad], axis=1)

    pos = jnp.arange(l_pad, dtype=jnp.int32)
    chunk_id = jnp.where(pos < N_META, 0, 1 + (pos - N_META) // CHUNK).astype(jnp.int32)
    inv_freq = 1.0 / (ROPE_THETA ** (jnp.arange(0, QK_ROPE, 2, dtype=jnp.float32) / QK_ROPE))
    ang = pos.astype(jnp.float32)[:, None] * inv_freq[None, :]
    cos = jnp.cos(ang).astype(x.dtype)
    sin = jnp.sin(ang).astype(x.dtype)

    for i in range(DEPTH):
        h = hybrid_layer(h, cos, sin, chunk_id, mix_norm_g[i], w_in[i], q_norm_g[i], w_uq[i],
                         kv_norm_g[i], w_ukv[i], conv_w[i], conv_b[i], conv_ln_g[i], conv_ln_b[i],
                         conv_out_g[i], attn_out_g[i], w_out[i], ffn_norm_g[i], w_ffn_up[i],
                         ffn_conv_w[i], ffn_conv_b[i], w_ffn_down[i])

    h = rms_norm(h, final_norm_g)
    return h[:, N_META:N_META + s]


_first_inputs_2 = second_inputs


def second_inputs(seed=0):
    import zlib

    import numpy as np

    out = dict(_first_inputs_2(seed))
    spreads = {}
    factors = {'q_norm_g': 5.335,
     'kv_norm_g': 3.26,
     'conv_b': 2.718,
     'conv_ln_g': 4.178,
     'conv_ln_b': 4.823,
     'conv_out_g': 5.347,
     'attn_out_g': 5.254,
     'ffn_norm_g': 5.017,
     'ffn_conv_b': 5.115,
     'final_norm_g': 2.947}
    for name, (base, spread) in spreads.items():
        noise = np.random.default_rng([zlib.crc32(name.encode()), seed]).standard_normal(out[name].shape)
        drawn = base * np.exp(spread * noise) if base else spread * noise
        out[name] = __import__('jax').numpy.asarray(drawn.astype(out[name].dtype))
    for name, factor in factors.items():
        out[name] = (out[name] * factor).astype(out[name].dtype)
    return out


_narrow_inputs_2 = second_inputs


def second_inputs(seed=0):

    out = dict(_narrow_inputs_2(seed))
    wider = {'conv_ln_g': 3.04, 'conv_out_g': 3.29, 'attn_out_g': 3.32, 'final_norm_g': 3.31}
    for name, times in wider.items():
        mean = out[name].mean()
        out[name] = (mean + times * (out[name] - mean)).astype(out[name].dtype)
    return out


D_MIX_3 = 2 * D_MODEL
D_A = D_MIX_3 // 2
D_B = D_MIX_3 - D_A
A_GROUPS = 8
A_GROUP_DIM = D_A // A_GROUPS
A_CHUNK = 128
B_HEADS = 4
B_DK = D_B // 2 // B_HEADS
B_DV = D_B // B_HEADS
B_GATE_RANK = 16
B_GATE_TAU = 16.0
B_CHUNK = 64
D_IN_3 = 3 * D_A + 2 * B_HEADS * B_DK + 2 * D_B + B_GATE_RANK


def rmsnorm(x, g):
    xf = x.astype(jnp.float32)
    y = xf * lax.rsqrt(jnp.mean(xf * xf, axis=-1, keepdims=True) + EPS)
    return (y * g.astype(jnp.float32)).astype(x.dtype)

def layernorm(x, g, b):
    xf = x.astype(jnp.float32)
    mu = jnp.mean(xf, axis=-1, keepdims=True)
    xc = xf - mu
    y = xc * lax.rsqrt(jnp.mean(xc * xc, axis=-1, keepdims=True) + EPS)
    return (y * g.astype(jnp.float32) + b.astype(jnp.float32)).astype(x.dtype)

def chunked_sgu(u, v, ln_g, ln_b, w_s, b_s):
    bsz, s = u.shape[:2]
    n = s // A_CHUNK
    vn = layernorm(v, ln_g, ln_b).reshape(bsz, n, A_CHUNK, A_GROUPS, A_GROUP_DIM)
    causal = jnp.tril(jnp.ones((A_CHUNK, A_CHUNK), dtype=bool))
    w = jnp.where(causal[None], w_s, jnp.zeros_like(w_s))
    sp = jnp.einsum('gts,bnsgc->bntgc', w, vn) + b_s.T[None, None, :, :, None]
    return u * sp.reshape(bsz, s, D_A).astype(u.dtype)

def gla_chunked(q, k, v, log_a):
    bsz, s = q.shape[:2]
    n = s // B_CHUNK
    f32 = jnp.float32

    def blk(t, d):
        return t.astype(f32).reshape(bsz, n, B_CHUNK, B_HEADS, d).transpose(0, 3, 1, 2, 4)

    q = blk(q, B_DK) * (B_DK ** -0.5)
    k = blk(k, B_DK)
    v = blk(v, B_DV)
    b = jnp.cumsum(blk(log_a, B_DK), axis=3)
    b_last = b[:, :, :, -1:, :]
    b_ref = b[:, :, :, B_CHUNK // 2 - 1:B_CHUNK // 2, :]

    qe = q * jnp.exp(b - b_ref)
    ke = k * jnp.exp(b_ref - b)
    scores = jnp.einsum('bhncd,bhnsd->bhncs', qe, ke)
    causal = jnp.tril(jnp.ones((B_CHUNK, B_CHUNK), dtype=bool))
    scores = jnp.where(causal, scores, 0.0)
    o_intra = jnp.einsum('bhncs,bhnsv->bhncv', scores, v)

    chunk_kv = jnp.einsum('bhncd,bhncv->bhndv', k * jnp.exp(b_last - b), v)
    decay = jnp.exp(b_last[:, :, :, 0, :])

    def step(state, inp):
        dec, kv = inp
        return dec[..., None] * state + kv, state

    s0 = jnp.zeros((bsz, B_HEADS, B_DK, B_DV), f32)
    _, s_prev = lax.scan(step, s0, (decay.transpose(2, 0, 1, 3), chunk_kv.transpose(2, 0, 1, 3, 4)))
    s_prev = s_prev.transpose(1, 2, 0, 3, 4)
    o_inter = jnp.einsum('bhncd,bhndv->bhncv', q * jnp.exp(b), s_prev)

    o = o_intra + o_inter
    return o.transpose(0, 2, 3, 1, 4).reshape(bsz, s, B_HEADS, B_DV)

def hybrid_layer_3(x, pre_g, w_in, w_a2, b_a2, a_ln_g, a_ln_b, a_w_s, a_b_s, b_norm_g, w_out, post_g):
    bsz, s, _ = x.shape
    h = rmsnorm(x, pre_g)
    z = jnp.einsum('bsd,de->bse', h, w_in)
    sizes = [D_A, D_A, D_A, B_HEADS * B_DK, B_HEADS * B_DK, D_B, D_B, B_GATE_RANK]
    cuts = np.cumsum(sizes)[:-1].tolist()
    a_u, a_v, a_gate, b_q, b_k, b_v, b_gate, b_lr = jnp.split(z, cuts, axis=-1)

    a_out = chunked_sgu(jax.nn.gelu(a_u, approximate=False), jax.nn.gelu(a_v, approximate=False),
                        a_ln_g, a_ln_b, a_w_s, a_b_s)
    a_out = a_out * jax.nn.silu(a_gate)

    gate_logit = jnp.einsum('bsr,re->bse', b_lr.astype(jnp.float32), w_a2.astype(jnp.float32)) + b_a2.astype(jnp.float32)
    log_a = jax.nn.log_sigmoid(gate_logit) / B_GATE_TAU
    o = gla_chunked(b_q.reshape(bsz, s, B_HEADS, B_DK), b_k.reshape(bsz, s, B_HEADS, B_DK),
                    b_v.reshape(bsz, s, B_HEADS, B_DV), log_a.reshape(bsz, s, B_HEADS, B_DK))
    o = rmsnorm(o, b_norm_g.reshape(B_HEADS, B_DV)).reshape(bsz, s, D_B).astype(x.dtype)
    b_out = o * jax.nn.silu(b_gate)

    mixed = jnp.concatenate([a_out, b_out], axis=-1)
    y = jnp.einsum('bse,ed->bsd', mixed, w_out)
    return x + rmsnorm(y, post_g)

def third_inputs(seed: int = 0) -> dict:
    key = jax.random.key(seed)
    ks = jax.random.split(key, 13)
    f32 = jnp.float32
    nrm = lambda k, shp, sc: jax.random.normal(k, shp, f32) * sc
    return {
        "x": jax.random.normal(ks[0], (BATCH, SEQ, D_MODEL), f32),
        "pre_norm_g": 1.0 + nrm(ks[1], (DEPTH, D_MODEL), 0.02),
        "w_in": nrm(ks[2], (DEPTH, D_MODEL, D_IN_3), D_MODEL ** -0.5),
        "w_a2": nrm(ks[3], (DEPTH, B_GATE_RANK, B_HEADS * B_DK), B_GATE_RANK ** -0.5),
        "b_a2": nrm(ks[4], (DEPTH, B_HEADS * B_DK), 0.1),
        "a_ln_g": 1.0 + nrm(ks[5], (DEPTH, D_A), 0.02),
        "a_ln_b": nrm(ks[6], (DEPTH, D_A), 0.02),
        "a_w_s": nrm(ks[7], (DEPTH, A_GROUPS, A_CHUNK, A_CHUNK), A_CHUNK ** -0.5),
        "a_b_s": 1.0 + nrm(ks[8], (DEPTH, A_GROUPS, A_CHUNK), 0.02),
        "b_norm_g": 1.0 + nrm(ks[9], (DEPTH, D_B), 0.02),
        "w_out": nrm(ks[10], (DEPTH, D_MIX_3, D_MODEL), D_MIX_3 ** -0.5),
        "post_norm_g": 1.0 + nrm(ks[11], (DEPTH, D_MODEL), 0.02),
    }

def third_block(x, pre_norm_g, w_in, w_a2, b_a2, a_ln_g, a_ln_b, a_w_s, a_b_s, b_norm_g, w_out, post_norm_g):
    for l in range(DEPTH):
        x = hybrid_layer_3(x, pre_norm_g[l], w_in[l], w_a2[l], b_a2[l], a_ln_g[l], a_ln_b[l],
                         a_w_s[l], a_b_s[l], b_norm_g[l], w_out[l], post_norm_g[l])
    return x


_first_inputs_3 = third_inputs


def third_inputs(seed=0):
    import zlib

    import numpy as np

    out = dict(_first_inputs_3(seed))
    spreads = {}
    factors = {}
    for name, (base, spread) in spreads.items():
        noise = np.random.default_rng([zlib.crc32(name.encode()), seed]).standard_normal(out[name].shape)
        drawn = base * np.exp(spread * noise) if base else spread * noise
        out[name] = __import__('jax').numpy.asarray(drawn.astype(out[name].dtype))
    for name, factor in factors.items():
        out[name] = (out[name] * factor).astype(out[name].dtype)
    return out


_narrow_inputs_3 = third_inputs


def third_inputs(seed=0):

    out = dict(_narrow_inputs_3(seed))
    wider = {'a_ln_g': 12.0, 'a_ln_b': 12.0, 'a_b_s': 9.49, 'b_norm_g': 5.78, 'post_norm_g': 4.5}
    for name, times in wider.items():
        mean = out[name].mean()
        out[name] = (mean + times * (out[name] - mean)).astype(out[name].dtype)
    return out


def setup_inputs(seed=0):
    out = dict(first_inputs(seed))
    for name, value in second_inputs(seed + 1).items():
        if name != "x":
            out[name + "_2"] = value
    for name, value in third_inputs(seed + 2).items():
        if name != "x":
            out[name + "_3"] = value
    return out


def reference(
    x, w_in, b_gate, w_conv, hn_g, w_pool, pool_scale, w_out, ln1_g, ln1_b, w_ff1, w_ff2, ln2_g,
    ln2_b, meta_tokens_2, mix_norm_g_2, w_in_2, q_norm_g_2, w_uq_2, kv_norm_g_2, w_ukv_2,
    conv_w_2, conv_b_2, conv_ln_g_2, conv_ln_b_2, conv_out_g_2, attn_out_g_2, w_out_2,
    ffn_norm_g_2, w_ffn_up_2, ffn_conv_w_2, ffn_conv_b_2, w_ffn_down_2, final_norm_g_2,
    pre_norm_g_3, w_in_3, w_a2_3, b_a2_3, a_ln_g_3, a_ln_b_3, a_w_s_3, a_b_s_3, b_norm_g_3,
    w_out_3, post_norm_g_3,
):
    x = first_block(
        x, w_in, b_gate, w_conv, hn_g, w_pool, pool_scale, w_out, ln1_g, ln1_b, w_ff1, w_ff2,
        ln2_g, ln2_b,
    )
    x = second_block(
        x, meta_tokens_2, mix_norm_g_2, w_in_2, q_norm_g_2, w_uq_2, kv_norm_g_2, w_ukv_2,
        conv_w_2, conv_b_2, conv_ln_g_2, conv_ln_b_2, conv_out_g_2, attn_out_g_2, w_out_2,
        ffn_norm_g_2, w_ffn_up_2, ffn_conv_w_2, ffn_conv_b_2, w_ffn_down_2, final_norm_g_2,
    )
    return third_block(
        x, pre_norm_g_3, w_in_3, w_a2_3, b_a2_3, a_ln_g_3, a_ln_b_3, a_w_s_3, a_b_s_3,
        b_norm_g_3, w_out_3, post_norm_g_3,
    )


_drawn_inputs = setup_inputs


def setup_inputs(seed=0):
    import zlib

    import numpy as np

    out = dict(_drawn_inputs(seed))
    spreads = {}
    factors = {}
    for name, (base, spread) in spreads.items():
        noise = np.random.default_rng([zlib.crc32(name.encode()), seed]).standard_normal(out[name].shape)
        drawn = base * np.exp(spread * noise) if base else spread * noise
        out[name] = __import__('jax').numpy.asarray(drawn.astype(out[name].dtype))
    for name, factor in factors.items():
        out[name] = (out[name] * factor).astype(out[name].dtype)
    return out
```

```python
from contextlib import ExitStack

import numpy as np

import concourse.bass as bass
from concourse import mybir

P = 128
S = 1024
D = 1024
DC = D // P
META = 16
WIDE = 1044
F32, F32R = mybir.dt.float32, mybir.dt.float32r
ACT, ALU, AX = mybir.ActivationFunctionType, mybir.AluOpType, mybir.AxisListType
ALPHA = 2.0 ** 0.25
LN_EPS, EPS = 1e-5, 1e-6
BLOCKS = 8

TWO = [(0, 512), (512, 512)]
THREE = [(0, 348), (348, 348), (696, 348)]
FFN2 = [(14, 342), (356, 342), (698, 342)]

H1, FF1 = 4, 32
OFF_G, OFF_O, OFF_P = 1536, 1544, 2056
CONV1 = 4
H2, QK, NOPE, ROPE = 8, 96, 64, 32
CONV2, FF2, CONV3 = 31, 22, 3
H3, CHUNK = 4, 64
OFF3 = dict(u=0, v=1024, gate=2048, q=3072, k=3584, bv=4096, bgate=5120, lr=6144)

N_BLOCKS = (
    8 * (1 + 4 * 4 + 4) + 8 * 8 + 2 * 8 * 32
    + 8 * 14 + 4 * 2 * 2 + 8 * 3 + 8 * 8 + 3 * 8 * 22
    + 8 * (8 * 3 + 1 + 4 * 6) + 16 * 8
)
N_TILES = -(-N_BLOCKS // BLOCKS)

VECTORS = [
    ("w_conv", CONV1 * 8), ("hn_g", 4), ("pool_scale", 4), ("ln1_g", 8), ("ln1_b", 8), ("ln2_g", 8), ("ln2_b", 8),
    ("mix_norm_g_2", 8), ("q_norm_g_2", 3), ("kv_norm_g_2", 2), ("conv_w_2", CONV2 * 4), ("conv_b_2", 4),
    ("conv_ln_g_2", 4), ("conv_ln_b_2", 4), ("conv_out_g_2", 4), ("attn_out_g_2", 4), ("ffn_norm_g_2", 8),
    ("ffn_conv_w_2", CONV3 * 44), ("ffn_conv_b_2", 44), ("final_norm_g_2", 8), ("pre_norm_g_3", 8), ("b_a2_3", 4),
    ("a_ln_g_3", 8), ("a_ln_b_3", 8), ("b_norm_g_3", 8), ("post_norm_g_3", 8),
]
VCOL = {}
for _name, _n in VECTORS:
    VCOL[_name] = sum(n for _, n in VECTORS[:len(VCOL)])
N_VEC = sum(n for _, n in VECTORS)


class Engine:

    def __init__(self, sem):
        self.sem, self.count, self.steps, self.waited = sem, 0, [], {}

    def wait(self, after):
        for token in after:
            if token is None:
                continue
            if isinstance(token, list):
                self.wait(token)
                continue
            sem, value = token
            if self.waited.get(sem.name, 0) < value:
                self.waited[sem.name] = value
                self.steps.append(lambda e, sem=sem, value=value: e.wait_ge(sem, value))

    def run(self, step, after=()):
        self.wait(after)
        self.steps.append(step)

    def do(self, step, after=()):
        self.wait(after)
        self.count += 1
        self.steps.append(lambda e: step(e).then_inc(self.sem, 1))
        return (self.sem, self.count)

    def last(self):
        return (self.sem, self.count) if self.count else None

    def emit(self, e):
        for step in self.steps:
            step(e)


class Dma:

    def __init__(self, engine, sem):
        self.engine, self.sem, self.count = engine, sem, 0

    def start(self, out, in_, after=()):
        self.count += 16
        self.engine.run(lambda e: e.dma_start(out() if callable(out) else out,
                                              in_() if callable(in_) else in_).then_inc(self.sem, 16), after)
        return (self.sem, self.count)


class Program:
    def __init__(self, nc, ctx, dram):
        self.nc, self.ctx, self.dram = nc, ctx, dram
        self.n_sem = 0
        self.pe, self.dve, self.act, self.pool, self.sp = (
            Engine(self.sem(n)) for n in ("pe_done", "dve_done", "act_done", "pool_done", "sp_done"))
        sb = self.sbuf
        self.w_raw = [sb(f"w_raw{i}", [P, BLOCKS, P]) for i in range(3)]
        self.w_hi = [sb(f"w_hi{i}", [P, BLOCKS, P], F32R) for i in range(3)]
        self.w_lo = [sb(f"w_lo{i}", [P, BLOCKS, P], F32R) for i in range(3)]
        self.w_dma = [Dma(self.sp, self.sem(f"w_landed{i}")) for i in range(3)]
        self.w_landed, self.w_ready, self.w_used = [], [], []
        self.blocks = []
        self.x_hi = sb("x_hi", [P, DC, WIDE], F32R)
        self.x_lo = sb("x_lo", [P, DC, WIDE], F32R)
        self.res = sb("res", [P, DC, WIDE])
        self.vec = sb("vectors", [P, N_VEC])
        self.ident = sb("identity", [P, P])
        self.upper = sb("upper", [P, P])
        self.ones = sb("ones", [P, P])
        self.head_row = sb("head_row", [H1, H1, P])
        self.tiny = sb("tiny", [P, 4])
        self.ps = ctx.enter_context(nc.psum_tensor("psum", [P, 8, 512], F32))
        self.bank_free = [None] * 8
        self.slot = 0

        once = Dma(self.sp, self.sem("constants_landed"))
        once.start(self.vec[:, :], dram["vectors"])
        once.start(self.ident[:, :], dram["identity"])
        once.start(self.upper[:, :], dram["upper"])
        self.const = [once.start(self.head_row[:, :, :], dram["head_row"])]
        self.const.append(self.dve.do(lambda e: e.memset(self.ones[:, :], 1.0)))
        for i, value in enumerate((LN_EPS, EPS, 1.0)):
            self.const.append(self.dve.do(lambda e, i=i, value=value: e.memset(self.tiny[:, i:i + 1], value)))

    def sem(self, name):
        return self.ctx.enter_context(self.nc.semaphore(name))

    def sbuf(self, name, shape, dt=F32, ctx=None):
        return (ctx or self.ctx).enter_context(self.nc.sbuf_tensor(name, shape, dt))

    def everything(self):
        return [e.last() for e in (self.pe, self.dve, self.act, self.pool)]

    def column(self, name, i):
        c = VCOL[name] + i
        return self.vec[:, c:c + 1]

    def activation(self, out, in_, func, after, bias=0.0, scale=1.0, accum=None):
        if accum is None:
            return self.act.do(lambda e: e.activation(out, in_, func, bias=bias, scale=scale), after)
        return self.act.do(lambda e: e.activation(out, in_, func, bias=bias, scale=scale, accum_out=accum), after)

    def copy(self, out, in_, after):
        return self.act.do(lambda e: e.copy(out, in_), after)

    def tt(self, out, a, b, op, after, eng=None):
        return (eng or self.dve).do(lambda e: e.tensor_tensor(out, a, b, op), after)

    def ts(self, out, a, s1, s2, op0, op1, after):
        if s2 is None:
            return self.dve.do(lambda e: e.tensor_scalar(out, a, s1, None, op0), after)
        return self.dve.do(lambda e: e.tensor_scalar(out, a, s1, s2, op0, op1), after)

    def stt(self, out, a, s, b, op0, op1, after):
        return self.dve.do(lambda e: e.scalar_tensor_tensor(out, a, s, b, op0, op1), after)

    def dcopy(self, out, in_, after):
        return self.dve.do(lambda e: e.tensor_copy(out, in_), after)

    def memset(self, out, value, after=()):
        return self.dve.do(lambda e: e.memset(out, value), after)

    def mm(self, products, after, transpose=False):
        def step(e):
            for out, lhsT, rhs, start, stop in products:
                if transpose:
                    ins = e.transpose(out, lhsT, rhs)
                else:
                    ins = e.matmul(out, lhsT, rhs, start=start, stop=stop, skip_group_check=True)
            return ins
        return self.pe.do(step, after)

    def prefetch(self, tile):
        for n in range(len(self.w_ready), min(tile + 3, N_TILES)):
            self.load_tile(n)
            raw, hi, lo = self.w_raw[n % 3], self.w_hi[n % 3], self.w_lo[n % 3]
            used = self.w_used[n - 3] if n >= 3 else None
            high = self.copy(hi[:, :, :], raw[:, :, :], [self.w_landed[n], used])
            low = self.tt(lo[:, :, :], raw[:, :, :], hi[:, :, :].bitcast(F32), ALU.subtract,
                          [high, self.w_landed[n], used], self.pool)
            self.w_ready.append(low)
        for n in range(len(self.w_landed), min(tile + 6, N_TILES)):
            self.load_tile(n)

    def load_tile(self, n):
        if n < len(self.w_landed):
            return
        freed = self.w_ready[n - 3] if n >= 3 else None
        self.w_landed.append(self.w_dma[n % 3].start(self.w_raw[n % 3][:, :, :], lambda n=n: self.dram["w"][n], [freed]))

    def product(self, chunks, hi, lo, pieces, x_ready, slots=2):
        width = len(pieces)
        first = self.slot * (2 if width == 2 else 3)
        banks = range(first, first + width)
        self.slot = (self.slot + 1) % slots
        n = pieces[0][1]
        wait_banks = [self.bank_free[b] for b in banks]
        token = None
        for k, spec in enumerate(chunks):
            index = len(self.blocks)
            self.blocks.append(spec)
            tile, at = divmod(index, BLOCKS)
            if at == 0 or k == 0:
                self.prefetch(tile)
            whi, wlo = self.w_hi[tile % 3][:, at, :], self.w_lo[tile % 3][:, at, :]
            first_k, last_k = k == 0, k == len(chunks) - 1

            def step(e, whi=whi, wlo=wlo, k=k, first_k=first_k, last_k=last_k):
                for i, (t0, m) in enumerate(pieces):
                    e.matmul(self.ps[:, first + i, 0:m], whi, hi(k)[:, t0:t0 + m], start=first_k, stop=False, skip_group_check=True)
                for i, (t0, m) in enumerate(pieces):
                    e.matmul(self.ps[:, first + i, 0:m], whi, lo(k)[:, t0:t0 + m], start=False, stop=False, skip_group_check=True)
                for i, (t0, m) in enumerate(pieces):
                    ins = e.matmul(self.ps[:, first + i, 0:m], wlo, hi(k)[:, t0:t0 + m], start=False, stop=last_k, skip_group_check=True)
                return ins
            after = [self.w_ready[tile], x_ready[k]] + (wait_banks if first_k else [])
            if at == BLOCKS - 1 or last_k or index == N_BLOCKS - 1:
                token = self.pe.do(step, after)
                if at == BLOCKS - 1 or index == N_BLOCKS - 1:
                    self.w_used.append(token)
            else:
                self.pe.run(step, after)
        return self.ps[:, first:first + width, 0:n], list(banks), token

    def free(self, banks, token):
        for b in banks:
            self.bank_free[b] = token

    def x_parts(self):
        return (lambda k: self.x_hi[:, k, :]), (lambda k: self.x_lo[:, k, :])

    def split(self, src, k, t0, t1, after, hi=None, lo=None):
        hi, lo = self.x_hi if hi is None else hi, self.x_lo if lo is None else lo
        high = self.copy(hi[:, k, t0:t1], src, after)
        return self.tt(lo[:, k, t0:t1], src, hi[:, k, t0:t1].bitcast(F32), ALU.subtract, [high, after])

    def feature_sums(self, sources, pieces, banks, after):
        token = None
        for i, (view, ready) in enumerate(sources):
            token = self.mm([(self.ps[:, b, 0:m], self.ones[:, :], view[:, t0:t0 + m], i == 0, i == len(sources) - 1)
                             for b, (t0, m) in zip(banks, pieces)],
                            [ready, self.const] + ([after, [self.bank_free[b] for b in banks]] if i == 0 else []))
        return token

    def inverse_root(self, out, scratch, sums, n, eps, after):
        eps_col = self.tiny[:, 0:1] if eps == LN_EPS else self.tiny[:, 1:2]
        a = self.activation(out, sums, ACT.Ln, [after, self.const], bias=eps_col, scale=1.0 / n)
        b = self.activation(out, out, ACT.Exp, [a], scale=-0.5)
        c = self.tt(scratch, out, out, ALU.mult, [b])
        d = self.stt(scratch, sums, n * eps, scratch, ALU.add, ALU.mult, [c])
        e = self.ts(scratch, scratch, -0.5 / n, 1.5, ALU.mult, ALU.add, [d])
        return self.tt(out, out, scratch, ALU.mult, [e])

    def norm(self, xs, ready, pieces, n, eps, scratch, squares, banks=(0, 1, 2), center=False, after=None):
        view = lambda t: t[:, pieces[0][0]:pieces[-1][0] + pieces[-1][1]]
        grid = lambda t: view(t).rearrange("p (a b) -> p a b", a=len(pieces))
        banks = list(banks)[:len(pieces)]
        sums = self.ps[:, banks[0]:banks[0] + len(pieces), 0:pieces[0][1]]
        rstd, mean, tmp = scratch
        if center:
            s = self.feature_sums(list(zip(xs, ready)), pieces, banks, None)
            m = self.activation(grid(mean), sums, ACT.Copy, [s, self.dve.last(), after], scale=1.0 / n)
            self.free(banks, m)
            ready = [self.tt(view(x), view(x), view(mean), ALU.subtract, [m, r]) for x, r in zip(xs, ready)]
        sq = []
        source_done = [None, None]
        token = None
        for i, (x, r) in enumerate(zip(xs, ready)):
            q = self.activation(view(squares[i % 2]), view(x), ACT.Square, [r, source_done[i % 2], [self.dve.last(), after] if i < 2 else None])
            token = self.mm([(self.ps[:, b, 0:m], self.ones[:, :], squares[i % 2][:, t0:t0 + m], i == 0, i == len(xs) - 1)
                             for b, (t0, m) in zip(banks, pieces)],
                            [q, self.const] + ([[self.bank_free[b] for b in banks]] if i == 0 else []))
            source_done[i % 2] = token
        rs = self.inverse_root(grid(rstd), grid(tmp), sums, n, eps, [token, self.dve.last(), after])
        self.free(banks, rs)
        return rs, ready


def block_of(name, k, cols):
    return (name, k * P, P, [(0, cols, P)] if isinstance(cols, int) else cols)


def layer_1(p):
    nc, dram, ps = p.nc, p.dram, p.ps
    hi, lo = p.x_parts()
    ctx = ExitStack()
    mix = p.sbuf("mix_1", [P, 8, WIDE], ctx=ctx)
    work = p.sbuf("work_1", [P, 7, WIDE], ctx=ctx)
    w_pool = p.sbuf("w_pool", [P, 4, P], ctx=ctx)
    gate_bias = p.sbuf("gate_bias", [P, 1], ctx=ctx)
    pool_fix = p.sbuf("pool_fix", [P, 4, 16], ctx=ctx)
    b_cols = p.sbuf("b_cols", [P, 8, H1], ctx=ctx)

    xin = [Dma(p.sp, p.sem(f"x_landed{k % 4}")) if k < 4 else None for k in range(8)]
    x_ready = []
    for k in range(8):
        landed = xin[k % 4].start(p.res[:, k, 0:S], dram["x"][k], [x_ready[k - 4] if k >= 4 else None])
        if k == 0:
            p.prefetch(0)
        x_ready.append(p.split(p.res[:, k, 0:S], k, 0, S, [landed]))
    small = Dma(p.sp, p.sem("small_1_landed"))
    small.start(gate_bias[:, :], dram["gate_bias"])
    small.start(pool_fix[:, :, :], dram["pool_fix"])
    const = p.const + [small.start(w_pool[:, :, :], dram["w_pool"])]

    T = [p.res[:, i, :] for i in range(8)] + [work[:, i, :] for i in range(7)]
    row_b, row_m, row_am, row_t, row_u = T[0], T[1], T[2], T[3], T[4]
    q_in, k_in, q_t, k_t = T[3], T[4], T[5], T[6]
    v_f, v_t, m_bc, floor, prob = T[7], T[8], T[9], T[10], T[11]
    o_sig = [T[12], T[13]]
    hbuf = T[14]
    tmp = v_f
    res_free = x_ready[-1]

    view, banks, tok = p.product([block_of("w_in", k, [(0, OFF_G, 4), (32, OFF_G + 4, 4)]) for k in range(8)], hi, lo, TWO, x_ready)
    gts = work[:, 5, 0:S]
    a = p.ts(gts[0:36, :], ps[0:36, banks[0]:banks[0] + 2, :], gate_bias[0:36, :], None, ALU.add, None, [tok, const])
    p.free(banks, a)
    i_row, f_row, l_row, e_row = work[0:4, 5, 0:S], work[0:4, 6, 0:S], work[0:4, 0, 0:S], work[0:4, 1, 0:S]
    one_row = work[0:4, 2, 0:S]
    b = p.dcopy(f_row, gts[32:36, :], [a])
    c = p.stt(e_row, f_row, -1.0, f_row, ALU.mult, ALU.max, [b])
    c = p.activation(e_row, e_row, ACT.Exp, [c], scale=-1.0)
    c = p.activation(e_row, e_row, ACT.Ln, [c, const], bias=p.tiny[0:4, 2:3])
    c = p.stt(l_row, f_row, 0.0, e_row, ALU.min, ALU.subtract, [c])
    one = p.memset(one_row, 1.0)
    A, B, M, AM = work[0:4, 3, 0:S], row_b[0:4, 0:S], row_m[0:4, 0:S], row_am[0:4, 0:S]
    c = p.dve.do(lambda e: e.tensor_tensor_scan(A, one_row, l_row, 0.0, ALU.mult, ALU.add), [c, one])
    bt = p.tt(B, i_row, A, ALU.subtract, [c, res_free])
    mt = p.dve.do(lambda e: e.tensor_tensor_scan(M, one_row, B, 0.0, ALU.mult, ALU.max), [bt])
    amt = p.tt(AM, A, M, ALU.add, [mt])
    t = p.mm([(ps[:, 4, 4 * j:4 * j + 4], row_b[0:4, j * P:(j + 1) * P], p.ident[0:4, 0:4], True, True) for j in range(8)],
             [bt, const], transpose=True)
    cols = p.dcopy(b_cols[:, :, :], ps[:, 4, 0:32], [t])
    p.free([4], cols)
    pads = [p.memset(x[:, 0:3], 0.0, [res_free]) for x in (q_in, k_in)]

    state = dict(q_in=None, v_f=None, q=None, v=None, o=[None, None], m_bc=None, prob=[None, None], h=None)

    def products_of_head(h):
        out = {}
        for n, off in (("q", 0), ("k", 512), ("v", 1024), ("o", OFF_O)):
            view, banks, tok = p.product([block_of("w_in", k, off + h * P) for k in range(8)], hi, lo, TWO, x_ready)
            if n == "o":
                e = p.activation(o_sig[h % 2][:, 0:S], view, ACT.Sigmoid, [tok, state["o"][h % 2]])
            elif n == "v":
                e = p.copy(v_f[:, 0:S], view, [tok, state["v_f"], res_free])
            else:
                e = p.copy((q_in if n == "q" else k_in)[:, 3:3 + S], view, [tok, state["q_in"], res_free])
            p.free(banks, e)
            out[n] = e
        return out

    def prepare(h, got):
        ready = []
        for n, src, dst in (("q", q_in, q_t), ("k", k_in, k_t)):
            chunk = h + (4 if n == "k" else 0)
            acc = dst[:, 0:S]
            w = lambda j: p.column("w_conv", j * 8 + chunk)
            c = p.ts(acc, src[:, 0:S], w(0), None, ALU.mult, None, [got[n], pads, state["q"], const, res_free])
            for j in range(1, CONV1):
                c = p.stt(acc, src[:, j:j + S], w(j), acc, ALU.mult, ALU.add, [c])
            state["q_in"] = c
            c = p.activation(acc, acc, ACT.Silu, [c])
            if n == "k":
                c = p.ts(acc, acc, P ** -0.5, None, ALU.mult, None, [c])
            ready.append(c)
        for g in range(2):
            t = p.mm([(ps[:, 4 + g, j * P:(j + 1) * P], v_f[:, (4 * g + j) * P:(4 * g + j + 1) * P], p.ident[:, :], True, True)
                      for j in range(4)], [got["v"], const, p.bank_free[4 + g]], transpose=True)
            state["v_f"] = t
            e = p.copy(v_t[:, g * 512:(g + 1) * 512], ps[:, 4 + g, :], [t, state["v"]])
            p.free([4 + g], e)
            ready.append(e)
        return ready

    def attend(h, ready, got):
        for row, dst, tok in ((M, m_bc, mt), (AM, floor, amt)):
            for g in range(2):
                t = p.mm([(ps[:, 4 + g, :], p.head_row[:, h, :], row[:, g * 512:(g + 1) * 512], True, True)],
                         [tok, const, p.bank_free[4 + g]])
                half = dst[:, g * 512:(g + 1) * 512]
                if row is M:
                    e = p.copy(half, ps[:, 4 + g, :], [t, state["m_bc"]])
                    m_tok = e
                else:
                    e = p.activation(half, ps[:, 4 + g, :], ACT.Exp, [t, state["m_bc"]], scale=-1.0)
                    floor_tok = e
                p.free([4 + g], e)
        n = 0
        for half in range(2):
            blocks = []
            for j in range(4 * half + 4):
                t0 = max(half * 512, j * P)
                blocks.append((j, t0, (half + 1) * 512 - t0))

            def scores(i):
                j, t0, w = blocks[i]
                bank = 4 + i % 2
                return p.mm([(ps[:, bank, 0:w], k_t[:, j * P:(j + 1) * P], q_t[:, t0:t0 + w], True, True)],
                            [ready, p.bank_free[bank]])

            s_tok = {0: scores(0)}
            for i, (j, t0, w) in enumerate(blocks):
                if i + 1 < len(blocks):
                    s_tok[i + 1] = scores(i + 1)
                bank = 4 + i % 2
                pr = prob[:, (n % 2) * 512:(n % 2) * 512 + w]
                c = p.ts(pr, m_bc[:, t0:t0 + w], b_cols[:, j, h:h + 1], 0.0, ALU.subtract, ALU.max, [m_tok, cols, state["prob"][n % 2]])
                c = p.activation(pr, pr, ACT.Exp, [c], scale=-1.0)
                if t0 == j * P:
                    c = p.tt(pr[:, 0:P], pr[:, 0:P], p.upper[:, :], ALU.mult, [c, const])
                c = p.tt(pr, pr, ps[:, bank, 0:w], ALU.mult, [c, s_tok[i]])
                p.free([bank], c)
                o0 = t0 - half * 512
                last = i == len(blocks) - 1
                t = p.mm([(ps[:, 6, o0:o0 + w], v_t[:, j * P:(j + 1) * P], pr, i == 0, last),
                          (ps[:, 7, o0:o0 + w], p.ones[:, :], pr, i == 0, last)],
                         [c, ready] + ([p.bank_free[6], p.bank_free[7]] if i == 0 else []))
                state["prob"][n % 2] = t
                n += 1
            sl = slice(half * 512, (half + 1) * 512)
            c = p.activation(hbuf[:, sl], ps[:, 7, :], ACT.Abs, [t, state["h"]])
            c = p.tt(floor[:, sl], hbuf[:, sl], floor[:, sl], ALU.max, [c, floor_tok])
            c = p.dve.do(lambda e, sl=sl: e.reciprocal(floor[:, sl], floor[:, sl]), [c])
            c = p.tt(hbuf[:, sl], ps[:, 6, :], floor[:, sl], ALU.mult, [c, state["h"]])
            p.free([6, 7], c)
        state["q"] = state["v"] = t
        rs, (r,) = p.norm([hbuf], [c], TWO, P, LN_EPS, (m_bc, floor, prob), (k_t, q_t), banks=(6, 7), center=True)
        state["q"] = [state["q"], p.pe.last()]
        c = p.stt(hbuf[:, 0:S], hbuf[:, 0:S], p.column("hn_g", h), m_bc[:, 0:S], ALU.mult, ALU.mult, [rs, const])
        c = p.tt(mix[:, h, 0:S], hbuf[:, 0:S], o_sig[h % 2][:, 0:S], ALU.mult, [c, got["o"]])
        state["o"][h % 2] = state["m_bc"] = state["h"] = c
        state["prob"] = [c, c]
        return c

    mix_ready = [None] * 8
    got = products_of_head(0)
    ready = prepare(0, got)
    for h in range(H1):
        following = products_of_head(h + 1) if h + 1 < H1 else None
        mix_ready[h] = attend(h, ready, got)
        if following:
            got = following
            ready = prepare(h + 1, got)

    p_in, p_sum, p_two, d_t = T[3], T[4], T[5], T[6]
    done = p.dve.last()
    pe_done = p.pe.last()
    for g in range(4):
        view, banks, tok = p.product([block_of("w_in", k, OFF_P + g * P) for k in range(8)], hi, lo, TWO, x_ready)
        e = p.copy(p_in[:, 0:S], view, [tok, done, pe_done])
        p.free(banks, e)
        src, dst = p_in, p_sum
        c = e
        for step in range(g + 1):
            shift = 1 << step
            c1 = p.tt(dst[:, shift:S], src[:, shift:S], src[:, 0:S - shift], ALU.add, [c, done, pe_done])
            c2 = p.dcopy(dst[:, 0:shift], src[:, 0:shift], [c, done])
            c = [c1, c2]
            src, dst = dst, (p_two if dst is p_sum else p_sum)
        win = 2 << g
        c = p.tt(src[:, 0:16], src[:, 0:16], pool_fix[:, g, :], ALU.mult, [c, const])
        c = p.stt(d_t[:, 0:S], src[:, 0:S], 1.0 / win, p_in[:, 0:S], ALU.mult, ALU.subtract, [c, pe_done])
        done = c
        t = p.mm([(ps[:, 4 + i, :], w_pool[:, g, :], d_t[:, i * 512:(i + 1) * 512], True, True) for i in range(2)],
                 [c, const, p.bank_free[4], p.bank_free[5]])
        pe_done = t
        e = p.activation(mix[:, 4 + g, 0:S], ps[:, 4:6, :], ACT.Copy, [t, const], scale=p.column("pool_scale", g))
        p.free([4, 5], e)
        mix_ready[4 + g] = e

    back = Dma(p.sp, p.sem("x_again_landed"))
    x_back = back.start(p.res[:, :, META:META + S], dram["x"].rearrange("k p t -> p k t"), p.everything())
    old = p.pe.last()
    real = lambda k: p.res[:, k, META:META + S]
    m_ready = [p.split(mix[:, k, 0:S], k, 0, S, [mix_ready[k], old]) for k in range(8)]
    r_ready = []
    for m in range(8):
        view, banks, tok = p.product([block_of("w_out", k, m * P) for k in range(8)], hi, lo, TWO, m_ready)
        c = p.stt(real(m), real(m), ALPHA, view, ALU.mult, ALU.add, [tok, x_back])
        p.free(banks, c)
        r_ready.append(c)
    xs = [real(k) for k in range(8)]
    rs, r_ready = p.norm(xs, r_ready, TWO, D, LN_EPS, (T[8], T[9], T[10]), (T[11], T[12]), banks=(4, 5), center=True)
    x1 = []
    for k in range(8):
        c = p.stt(real(k), real(k), p.column("ln1_g", k), T[8][:, 0:S], ALU.mult, ALU.mult, [rs, r_ready[k]])
        c = p.ts(real(k), real(k), p.column("ln1_b", k), None, ALU.add, None, [c])
        x1.append(p.split(real(k), k, 0, S, [c, old]))
    switch = p.everything()
    ctx.close()

    ctx = ExitStack()
    h_hi = p.sbuf("h1_hi", [P, 6, S], F32R, ctx=ctx)
    h_lo = p.sbuf("h1_lo", [P, 6, S], F32R, ctx=ctx)
    tmp = p.sbuf("h1_tmp", [P, 2, S], ctx=ctx)
    h_used = [switch] * 6
    t_used = [switch] * 2
    h_ready = {}
    acc = [None] * 8

    def hidden(j):
        view, banks, tok = p.product([block_of("w_ff1", k, j * P) for k in range(8)], hi, lo, TWO, x1)
        r = tmp[:, j % 2, :]
        c = p.activation(r, view, ACT.Relu, [tok, t_used[j % 2]])
        p.free(banks, c)
        c = p.tt(r, r, r, ALU.mult, [c])
        c = p.split(r, j % 6, 0, S, [c, h_used[j % 6]], h_hi, h_lo)
        h_ready[j] = t_used[j % 2] = c

    def project(g):
        ks = range(4 * g, 4 * g + 4)
        for m in range(8):
            view, banks, tok = p.product([block_of("w_ff2", k, m * P) for k in ks],
                                         lambda i: h_hi[:, (4 * g + i) % 6, :], lambda i: h_lo[:, (4 * g + i) % 6, :],
                                         TWO, [h_ready[k] for k in ks])
            out = real(m)
            c = p.stt(out, out, ALPHA if g == 0 else 1.0, view, ALU.mult, ALU.add, [tok, acc[m], x1[m]])
            p.free(banks, c)
            acc[m] = c
        for k in ks:
            h_used[k % 6] = tok

    for g in range(FF1 // 4):
        for j in range(4):
            if g == 0 or j >= 2:
                hidden(4 * g + j)
        if g + 1 < FF1 // 4:
            hidden(4 * g + 4)
            hidden(4 * g + 5)
        project(g)
    switch = p.everything()
    ctx.close()
    return acc, switch


def layer_2(p, acc, switch):
    nc, dram, ps = p.nc, p.dram, p.ps
    hi, lo = p.x_parts()
    real = lambda k: p.res[:, k, META:META + S]
    ctx = ExitStack()
    mix = p.sbuf("mix_2", [P, 8, WIDE], ctx=ctx)
    u_pad = p.sbuf("u_padded", [P, 4, CONV2 - 1 + WIDE], ctx=ctx)
    work = p.sbuf("work_2", [P, 4, WIDE], ctx=ctx)
    small = p.sbuf("v_and_probs_of_meta", [P, 2, P], ctx=ctx)
    col = p.sbuf("softmax_columns", [P, 2, 4], ctx=ctx)
    M = [mix[:, i, :] for i in range(8)]

    meta_dma = Dma(p.sp, p.sem("meta_landed"))
    meta = meta_dma.start(p.res[:, :, 0:META], dram["meta"], switch)
    pad = p.memset(p.res[:, :, META + S:WIDE], 0.0, switch)
    rs, ready = p.norm([real(k) for k in range(8)], acc, TWO, D, LN_EPS, (M[0], M[1], M[2]), (M[3], M[4]), center=True, after=switch)
    h0 = []
    for k in range(8):
        c = p.stt(real(k), real(k), p.column("ln2_g", k), M[0][:, 0:S], ALU.mult, ALU.mult, [rs, ready[k]])
        c = p.ts(real(k), real(k), p.column("ln2_b", k), None, ALU.add, None, [c])
        h0.append([c, meta, pad])
    spill = Dma(p.sp, p.sem("h0_spilled"))
    spilled = spill.start(dram["spill_2"], p.res[:, :, :], h0)

    rs, _ = p.norm([p.res[:, k, :] for k in range(8)], h0, THREE, D, EPS, (M[0], M[1], M[2]), (M[3], M[4]))
    old = p.pe.last()
    x_ready = []
    for k in range(8):
        t = M[5 + k % 2]
        c = p.stt(t, p.res[:, k, :], p.column("mix_norm_g_2", k), M[0], ALU.mult, ALU.mult, [rs, x_ready[k - 2] if k >= 2 else None])
        x_ready.append(p.split(t, k, 0, WIDE, [c, old]))
    free = [spilled, x_ready[-1]]

    T = [p.res[:, i, :] for i in range(8)] + [work[:, i, :] for i in range(4)]
    grid = lambda t: t.rearrange("p (a b) -> p a b", a=3)
    rope_dma = Dma(p.sp, p.sem("rope_landed"))
    rope_t = T[6]
    rope = rope_dma.start(rope_t, dram["rope"], free)
    sig = T[7]
    zeros = p.memset(u_pad[:, :, 0:CONV2 - 1], 0.0, switch)

    conv_steps = []
    conv_token = [None] * 4

    def conv_step(c, j, u_ready):
        src = u_pad[:, c, j:j + WIDE]
        w = p.column("conv_w_2", j * 4 + c)
        if j == 0:
            conv_token[c] = p.ts(M[c], src, w, p.column("conv_b_2", c), ALU.mult, ALU.add, [u_ready, zeros, x_ready[-1]])
        else:
            conv_token[c] = p.stt(M[c], src, w, M[c], ALU.mult, ALU.add, [conv_token[c]])

    def fill(n):
        for _ in range(min(n, len(conv_steps))):
            conv_step(*conv_steps.pop(0))

    last = None
    for c in range(4):
        view, banks, tok = p.product([block_of("w_in_2", k, 512 + c * P) for k in range(8)], hi, lo, THREE, x_ready)
        s = p.activation(grid(sig), view, ACT.Sigmoid, [tok, last, free])
        p.free(banks, s)
        view, banks, tok = p.product([block_of("w_in_2", k, c * P) for k in range(8)], hi, lo, THREE, x_ready)
        last = p.tt(grid(u_pad[:, c, CONV2 - 1:]), view, grid(sig), ALU.mult, [tok, s, switch])
        p.free(banks, last)
        conv_steps += [(c, j, last) for j in range(CONV2)]
        fill(16)
    low_rank = []
    for i in range(5):
        view, banks, tok = p.product([block_of("w_in_2", k, 1024 + i * P) for k in range(8)], hi, lo, THREE, x_ready)
        e = p.copy(grid(T[i]), view, [tok, free])
        p.free(banks, e)
        low_rank.append(e)
        if i < 3:
            fill(10)
    view, banks, tok = p.product([block_of("w_in_2", k, [(64, 1664, 32), (96, 1680, 16), (112, 1664, 16)]) for k in range(8)],
                                 hi, lo, THREE, x_ready)
    k_rot, rot_tmp = T[5], T[8]

    def rotate(out, view, banks, tok, after):
        b = slice(banks[0], banks[0] + 3)
        c1 = p.tt(grid(rot_tmp)[64:96], ps[96:128, b, 0:348], grid(rope_t)[96:128], ALU.mult, [tok, rope, after, p.dve.last()])
        c2 = p.tt(grid(out)[64:96], ps[64:96, b, 0:348], grid(rope_t)[64:96], ALU.mult, [tok, rope, after])
        return c2, p.tt(out[64:96, :], out[64:96, :], rot_tmp[64:96, :], ALU.add, [c1, c2])

    c2, rot_ready = rotate(k_rot, view, banks, tok, [free, switch])
    p.free(banks, rot_ready)
    old = p.pe.last()
    parts = [None] * 5
    for name, first, n in (("q_norm_g_2", 0, 3), ("kv_norm_g_2", 3, 2)):
        rs, _ = p.norm([T[first + i] for i in range(n)], low_rank[first:first + n], THREE, n * P, EPS,
                       (T[9], T[10], T[11]), (T[8], T[7]), banks=(0, 1, 2) if first else (3, 4, 5), after=p.pe.last())
        for i in range(first, first + n):
            c = p.stt(T[i], T[i], p.column(name, i - first), T[9], ALU.mult, ALU.mult, [rs])
            parts[i] = p.split(T[i], i, 0, WIDE, [c, old])

    slots = [T[i] for i in (0, 1, 2, 3, 4, 7, 9, 10, 11)]
    keys, q_t, v_f, v_t = slots[0:2], slots[2], slots[3], slots[4]
    probs, probs_t = slots[5:7], slots[7:9]
    v_meta, pt_meta = small[:, 0, :], small[:, 1, :]
    start = p.everything()
    zm = p.memset(small[:, :, :], 0.0, switch)
    st = dict(keys=start, q=start, v_f=start, v_t=start, probs=[start, start], probs_t=[start, start], meta=zm)
    SCALE = QK ** -0.5
    o_ready = []

    def keys_and_values(j):
        view, banks, tok = p.product([("w_ukv_2", k * P, P, [(0, 2 * j * P, 64), (64, (2 * j + 1) * P, 64)]) for k in range(2)],
                                     lambda k: p.x_hi[:, 3 + k, :], lambda k: p.x_lo[:, 3 + k, :], THREE, parts[3:5])
        out = []
        for i in range(2):
            e = p.copy(grid(keys[i])[0:64], ps[64 * i:64 * i + 64, banks[0]:banks[0] + 3, 0:348], [tok, st["keys"]])
            r = p.dcopy(keys[i][64:96, :], k_rot[64:96, :], [rot_ready, st["keys"]])
            out += [e, r]
        p.free(banks, e)
        view, banks, tok = p.product([("w_ukv_2", k * P, P, [(0, 2 * j * P + 64, 64), (64, (2 * j + 1) * P + 64, 64)]) for k in range(2)],
                                     lambda k: p.x_hi[:, 3 + k, :], lambda k: p.x_lo[:, 3 + k, :], THREE, parts[3:5])
        e = p.copy(grid(v_f), view, [tok, st["v_f"]])
        p.free(banks, e)
        for g in range(2):
            t = p.mm([(ps[:, 6 + g, i * P:(i + 1) * P], v_f[:, META + (4 * g + i) * P:META + (4 * g + i + 1) * P], p.ident[:, :], True, True)
                      for i in range(4)], [e, p.bank_free[6 + g]], transpose=True)
            c = p.copy(v_t[:, g * 512:(g + 1) * 512], ps[:, 6 + g, :], [t, st["v_t"]])
            p.free([6 + g], c)
            out.append(c)
        t = p.mm([(ps[0:META, 6, 0:P], v_f[:, 0:META], p.ident[:, :], True, True)], [e, p.bank_free[6]], transpose=True)
        c = p.copy(v_meta[0:META, :], ps[0:META, 6, 0:P], [t, st["v_t"], zm])
        p.free([6], c)
        st["v_f"] = t
        return out + [c]

    def queries(h):
        c = h * QK
        view, banks, tok = p.product([("w_uq_2", k * P, P, [(0, c, 64), (64, c + 64, 32), (96, c + 80, 16), (112, c + 64, 16)]) for k in range(3)],
                                     hi, lo, THREE, parts[0:3])
        e = p.copy(grid(q_t)[0:64], ps[0:64, banks[0]:banks[0] + 3, 0:348], [tok, st["q"]])
        _, r = rotate(q_t, view, banks, tok, st["q"])
        p.free(banks, [e, r])
        return [e, r]

    tiles = [(0, META, META)] + [(META + i * P, P, META + (i + 1) * P) for i in range(8)]
    step = [0]

    def head(h, key, ready):
        def scores(i):
            q0, _, nk = tiles[i]
            b = 3 * p.slot
            p.slot = (p.slot + 1) % 2
            t = p.mm([(ps[:, b + n // 512, 0:min(512, nk - n)], q_t[0:QK, q0:q0 + P], key[0:QK, n:n + min(512, nk - n)], True, True)
                      for n in range(0, nk, 512)], [ready, p.bank_free[b], p.bank_free[b + 1], p.bank_free[b + 2]])
            st["q"] = t
            return b, t

        nxt = scores(0)
        for i, (q0, used, nk) in enumerate(tiles):
            b, tok = nxt
            r = step[0] % 2
            step[0] += 1
            flat = ps[:, b:b + 3, :].rearrange("p a b -> p (a b)")
            c = tok
            if i:
                c = p.memset(flat[0:64, nk - 64:nk], -1e30, [tok])
            c = p.dve.do(lambda e, r=r, flat=flat, nk=nk: e.tensor_reduce(col[:, r, 0:1], flat[:, 0:nk], AX.X, ALU.max), [c, tok, st["probs"][r]])
            c = p.ts(col[:, r, 1:2], col[:, r, 0:1], -SCALE, None, ALU.mult, None, [c])
            pr = probs[r]
            ex = p.activation(pr[:, 0:nk], flat[:, 0:nk], ACT.Exp, [c, st["probs"][r]], bias=col[:, r, 1:2], scale=SCALE, accum=col[:, r, 2:3])
            if i + 1 < len(tiles):
                nxt = scores(i + 1)
            c = p.dve.do(lambda e, r=r: e.reciprocal(col[:, r, 3:4], col[:, r, 2:3]), [ex])
            c = p.ts(pr[:, 0:nk], pr[:, 0:nk], col[:, r, 3:4], None, ALU.mult, None, [c])
            fill(1)
            pt = probs_t[r]
            t_ready = []
            n_full = (nk - META) // P
            for g in range(0, max(n_full, 1), 4):
                bank = 6 + (g // 4) % 2
                n = min(4, n_full - g)
                if n > 0:
                    t = p.mm([(ps[:, bank, x * P:(x + 1) * P], pr[:, META + (g + x) * P:META + (g + x + 1) * P], p.ident[:, :], True, True)
                              for x in range(n)], [c, p.bank_free[bank]], transpose=True)
                    out = pt[:, g * P:(g + n) * P]
                    e = (p.copy if g == 0 else p.dcopy)(out, ps[:, bank, 0:n * P], [t, st["probs_t"][r]])
                    p.free([bank], e)
                    t_ready.append(e)
            t = p.mm([(ps[0:META, 7, 0:P], pr[:, 0:META], p.ident[:, :], True, True)], [c, p.bank_free[7]], transpose=True)
            e = p.copy(pt_meta[0:META, :], ps[0:META, 7, 0:P], [t, st["meta"], zm])
            p.free([7], e)
            st["probs"][r] = t
            t_ready.append(e)
            t = p.mm([(ps[:, b, 0:P], v_meta, pt_meta, True, n_full == 0)] +
                     [(ps[:, b, 0:P], v_t[:, x * P:(x + 1) * P], pt[:, x * P:(x + 1) * P], False, x == n_full - 1) for x in range(n_full)],
                     [t_ready, ready, ex])
            st["probs_t"][r] = st["meta"] = t
            half = slice(64 * (h % 2), 64 * (h % 2) + 64)
            e = p.copy(mix[half, 4 + h // 2, q0:q0 + used], ps[half, b, 0:used], [t, x_ready[-1]])
            p.free([b, b + 1, b + 2], e)
            o_ready.append(e)
        st["v_t"] = t

    pads = p.memset(mix[:, 4:8, META + S:WIDE], 0.0, [x_ready[-1]])
    for j in range(H2 // 2):
        kv = keys_and_values(j)
        for i in range(2):
            head(2 * j + i, keys[i], [kv, queries(2 * j + i)])
        st["keys"] = st["q"]
    fill(len(conv_steps))

    A = [u_pad[:, c, 0:WIDE] for c in range(4)]
    done = p.everything()
    rs, ready = p.norm(M[0:4], conv_token, THREE, 4 * P, EPS, (T[8], T[9], T[10]), (T[11], A[0]), center=True, after=done)
    for c in range(4):
        x = p.tt(M[c], M[c], T[8], ALU.mult, [rs, ready[c]])
        ready[c] = p.activation(M[c], M[c], ACT.Silu, [x], scale=p.column("conv_ln_g_2", c), bias=p.column("conv_ln_b_2", c))
    m_ready = []
    rsu, _ = p.norm(M[0:4], ready, THREE, 4 * P, EPS, (T[8], T[9], T[10]), (T[11], A[0]))
    rso, _ = p.norm(M[4:8], [[o_ready, pads]] * 4, THREE, 4 * P, EPS, (A[1], A[2], A[3]), (T[11], A[0]), banks=(3, 4, 5), after=done)
    for k in range(8):
        name, r, rt = ("conv_out_g_2", T[8], rsu) if k < 4 else ("attn_out_g_2", A[1], rso)
        c = p.stt(M[k], M[k], p.column(name, k % 4), r, ALU.mult, ALU.mult, [rt, rsu, rso])
        m_ready.append(p.split(M[k], k, 0, WIDE, [c, done]))
    back = Dma(p.sp, p.sem("h0_back"))
    h_back = back.start(p.res[:, :, :], dram["spill_2"], [done, spilled])
    h1 = []
    for m in range(8):
        view, banks, tok = p.product([block_of("w_out_2", k, m * P) for k in range(8)], hi, lo, THREE, m_ready)
        c = p.tt(grid(p.res[:, m, :]), grid(p.res[:, m, :]), view, ALU.add, [tok, h_back])
        p.free(banks, c)
        h1.append(c)
    rs, _ = p.norm([p.res[:, k, :] for k in range(8)], h1, THREE, D, EPS, (T[8], T[9], T[10]), (T[11], A[0]))
    old = p.pe.last()
    n_ready = []
    for k in range(8):
        t = M[k % 2]
        c = p.stt(t, p.res[:, k, :], p.column("ffn_norm_g_2", k), T[8], ALU.mult, ALU.mult, [rs, n_ready[k - 2] if k >= 2 else None])
        n_ready.append(p.split(t, k, 0, WIDE, [c, old]))
    switch = p.everything()
    ctx.close()

    ctx = ExitStack()
    h_hi = p.sbuf("h2_hi", [P, 6, S], F32R, ctx=ctx)
    h_lo = p.sbuf("h2_lo", [P, 6, S], F32R, ctx=ctx)
    up = p.sbuf("up_2", [P, 2, S + 2], ctx=ctx)
    conv = p.sbuf("up_conv_2", [P, 2, S], ctx=ctx)
    h_used, h_ready = [switch] * 6, {}
    up_free, conv_free = [switch] * 2, [switch] * 2
    acc = list(h1)

    def hidden(j):
        got = []
        for i in range(2):
            view, banks, tok = p.product([block_of("w_ffn_up_2", k, i * FF2 * P + j * P) for k in range(8)], hi, lo, FFN2, n_ready)
            e = p.copy(up[:, i, :].rearrange("p (a b) -> p a b", a=3), view, [tok, up_free[i]])
            p.free(banks, e)
            chunk = i * FF2 + j
            w = lambda tap: p.column("ffn_conv_w_2", tap * 44 + chunk)
            c = p.ts(conv[:, i, :], up[:, i, 0:S], w(0), p.column("ffn_conv_b_2", chunk), ALU.mult, ALU.add, [e, conv_free[i]])
            c = p.stt(conv[:, i, :], up[:, i, 1:S + 1], w(1), conv[:, i, :], ALU.mult, ALU.add, [c])
            c = p.stt(conv[:, i, :], up[:, i, 2:S + 2], w(2), conv[:, i, :], ALU.mult, ALU.add, [c])
            up_free[i] = c
            if i == 0:
                c = p.activation(conv[:, 0, :], conv[:, 0, :], ACT.Silu, [c])
            got.append(c)
        c = p.tt(conv[:, 0, :], conv[:, 0, :], conv[:, 1, :], ALU.mult, got)
        conv_free[1] = c
        c = p.split(conv[:, 0, :], j % 6, 0, S, [c, h_used[j % 6]], h_hi, h_lo)
        h_ready[j] = conv_free[0] = c

    def project(ks):
        for m in range(8):
            view, banks, tok = p.product([block_of("w_ffn_down_2", k, m * P) for k in ks],
                                         lambda i: h_hi[:, ks[i] % 6, :], lambda i: h_lo[:, ks[i] % 6, :],
                                         TWO, [h_ready[k] for k in ks])
            c = p.tt(real(m), real(m), view, ALU.add, [tok, acc[m], n_ready[m]])
            p.free(banks, c)
            acc[m] = c
        for k in ks:
            h_used[k % 6] = tok

    done_to = 0
    for g in range(0, FF2, 4):
        ks = list(range(g, min(g + 4, FF2)))
        ahead = min(ks[-1] + 3, FF2)
        for j in range(done_to, ahead):
            hidden(j)
        done_to = ahead
        project(ks)
    switch = p.everything()
    ctx.close()
    return acc, switch


def layer_3(p, acc, switch, out):
    nc, dram, ps = p.nc, p.dram, p.ps
    hi, lo = p.x_parts()
    real = lambda k: p.res[:, k, META:META + S]
    ctx = ExitStack()
    mix = p.sbuf("mix_3", [P, 8, S], ctx=ctx)
    work = p.sbuf("work_3", [P, 7, S], ctx=ctx)
    w_a2 = p.sbuf("w_a2", [16, 4, P], ctx=ctx)
    pair = p.sbuf("pair_scores", [P, 2, P], ctx=ctx)
    ends = p.sbuf("chunk_decay", [P, 16], ctx=ctx)
    M = [mix[:, i, :] for i in range(8)]
    chunks = lambda t: t.rearrange("p (c l) -> p c l", l=CHUNK)
    grid = lambda t: t.rearrange("p (a b) -> p a b", a=2)

    xs = [real(k) for k in range(8)]
    rs, _ = p.norm(xs, acc, TWO, D, EPS, M[0:3], M[3:5], banks=(4, 5), after=switch)
    x_in = [p.stt(real(k), real(k), p.column("final_norm_g_2", k), M[0], ALU.mult, ALU.mult, [rs]) for k in range(8)]
    spill = Dma(p.sp, p.sem("x3_spilled"))
    spilled = spill.start(dram["spill_3"][:, :, 0:S], p.res[:, :, META:META + S], x_in)
    w_a2_dma = Dma(p.sp, p.sem("w_a2_landed"))
    w_a2_ready = w_a2_dma.start(w_a2[:, :, :], dram["w_a2"].rearrange("r (h c) -> r h c", h=4), switch)
    rs, _ = p.norm(xs, x_in, TWO, D, EPS, M[0:3], M[3:5], banks=(4, 5))
    old = p.pe.last()
    x_ready = []
    for k in range(8):
        t = M[5 + k % 2]
        c = p.stt(t, xs[k], p.column("pre_norm_g_3", k), M[0], ALU.mult, ALU.mult, [rs, x_ready[k - 2] if k >= 2 else None])
        x_ready.append(p.split(t, k, 0, S, [c, old]))
    free = [spilled, x_ready[-1], switch]

    T = [p.res[:, i, 0:S] for i in range(8)] + [work[:, i, :] for i in range(7)]

    def w_in(col, n=P):
        return p.product([block_of("w_in_3", k, col if n == P else [(0, col, n)]) for k in range(8)], hi, lo, TWO, x_ready)

    w_s, b_s = T[6].rearrange("p (g t) -> p g t", g=8), T[7]
    s_dma = Dma(p.sp, p.sem("w_s_landed"))
    s_dma.start(w_s, dram["a_w_s"], free)
    landed = s_dma.start(b_s, dram["a_b_s"].broadcast_to([P, 8 * P]), free)
    masked = p.tt(w_s, w_s, p.upper[:, :].unsqueeze(1).broadcast_to([P, 8, P]), ALU.mult, [landed, p.const])
    v_ready = []
    for g in range(8):
        view, banks, tok = w_in(OFF3["v"] + g * P)
        e = p.activation(grid(M[g]), view, ACT.Gelu, [tok, x_ready[-1]])
        p.free(banks, e)
        v_ready.append(e)
    rs, v_ready = p.norm(M, v_ready, TWO, D, EPS, T[0:3], T[3:5], banks=(4, 5), center=True, after=free)
    u_g, s_g, v_t, sp_t = T[8], T[9], T[10:12], T[12]
    vt_used, gates_used, a_ready, spilled_a = [switch] * 2, switch, [], []
    spill_a = [Dma(p.sp, p.sem(f"a_spilled{i}")) for i in range(2)]
    for g in range(8):
        c = p.stt(M[g], M[g], p.column("a_ln_g_3", g), T[0], ALU.mult, ALU.mult, [rs, v_ready[g]])
        v_ready[g] = p.ts(M[g], M[g], p.column("a_ln_b_3", g), None, ALU.add, None, [c])
    for g in range(8):
        view, banks, tok = w_in(OFF3["u"] + g * P)
        u_tok = p.activation(grid(u_g), view, ACT.Gelu, [tok, gates_used])
        p.free(banks, u_tok)
        view, banks, tok = w_in(OFF3["gate"] + g * P)
        s_tok = p.activation(grid(s_g), view, ACT.Silu, [tok, gates_used])
        p.free(banks, s_tok)
        vt = v_t[g % 2]
        t_ready = []
        for half in range(2):
            t = p.mm([(ps[:, 6 + half, i * P:(i + 1) * P], M[g][:, (4 * half + i) * P:(4 * half + i + 1) * P], p.ident[:, :], True, True)
                      for i in range(4)], [v_ready[g], p.bank_free[6 + half]], transpose=True)
            e = p.copy(vt[:, half * 512:(half + 1) * 512], ps[:, 6 + half, :], [t, vt_used[g % 2]])
            p.free([6 + half], e)
            t_ready.append(e)
        t = p.mm([(ps[:, 4 + n // 4, (n % 4) * P:(n % 4 + 1) * P], vt[:, n * P:(n + 1) * P], w_s[:, g, :], True, True) for n in range(8)],
                 [t_ready, masked, p.bank_free[4], p.bank_free[5]])
        vt_used[g % 2] = t
        bias = b_s[:, g * P:(g + 1) * P].unsqueeze(1).broadcast_to([P, 8, P])
        c = p.tt(sp_t.rearrange("p (n t) -> p n t", n=8), ps[:, 4:6, :].rearrange("p a (n t) -> p (a n) t", t=P), bias, ALU.add, [t, landed, gates_used])
        p.free([4, 5], c)
        c = p.tt(u_g, u_g, sp_t, ALU.mult, [c, u_tok])
        c = p.tt(M[g], u_g, s_g, ALU.mult, [c, s_tok, t_ready])
        gates_used = c
        spilled_a.append(spill_a[g % 2].start(dram["spill_a"][:, g, 0:S], M[g], [c, spilled_a[g - 2] if g >= 2 else None]))

    (lr, reset, q_t, k_t, b_t, e_t, qe, ke, kd_tok, v_f, v0, v1, g0, g1, states) = T
    start = p.everything()
    z = [p.memset(pair[:, :, :], 0.0, switch)]
    c = p.memset(reset, 1.0, [start])
    z.append(p.memset(chunks(reset)[:, :, 0:1], 0.0, [c]))
    view, banks, tok = w_in(OFF3["lr"], 16)
    lr_ready = p.copy(lr[0:16, :], ps[0:16, banks[0]:banks[0] + 2, :], [tok, start])
    p.free(banks, lr_ready)
    b_ready = []
    SCALE = P ** -0.5
    TAU = 1.0 / 16.0
    done = start
    for h in range(H3):
        got = []
        for dst, off in ((q_t, "q"), (k_t, "k")):
            view, banks, tok = w_in(OFF3[off] + h * P)
            e = p.copy(dst, view, [tok, done])
            p.free(banks, e)
            got.append(e)
        t = p.mm([(ps[:, 4 + i, :], w_a2[:, h, :], lr[0:16, i * 512:(i + 1) * 512], True, True) for i in range(2)],
                 [lr_ready, w_a2_ready, p.bank_free[4], p.bank_free[5]])
        x = p.ts(qe, ps[:, 4:6, :], p.column("b_a2_3", h), None, ALU.add, None, [t, done])
        p.free([4, 5], x)
        c = p.stt(e_t, qe, -1.0, qe, ALU.mult, ALU.max, [x, done])
        c = p.activation(e_t, e_t, ACT.Exp, [c], scale=-1.0)
        c = p.activation(e_t, e_t, ACT.Ln, [c], bias=p.tiny[:, 2:3])
        c = p.stt(e_t, qe, 0.0, e_t, ALU.min, ALU.subtract, [c])
        b = p.dve.do(lambda e: e.tensor_tensor_scan(b_t, reset, e_t, 0.0, ALU.mult, ALU.add), [c, z, done])
        ref = chunks(b_t)[:, :, CHUNK // 2 - 1:CHUNK // 2].broadcast_to([P, 16, CHUNK])
        end = chunks(b_t)[:, :, CHUNK - 1:CHUNK]
        decay = p.activation(ends[:, :], end.rearrange("p c l -> p (c l)"), ACT.Exp, [b, done], scale=TAU)
        d = p.tt(chunks(v_f), chunks(b_t), ref, ALU.subtract, [b, done])
        c = p.activation(e_t, v_f, ACT.Exp, [d], scale=TAU)
        r1 = p.stt(qe, q_t, SCALE, e_t, ALU.mult, ALU.mult, [c, got[0]])
        c = p.activation(ke, v_f, ACT.Exp, [d, done], scale=-TAU)
        r2 = p.tt(ke, ke, k_t, ALU.mult, [c, got[1]])
        c = p.activation(e_t, b_t, ACT.Exp, [r1], scale=TAU)
        r3 = p.stt(q_t, q_t, SCALE, e_t, ALU.mult, ALU.mult, [c, r1])
        d = p.tt(chunks(v_f), end.broadcast_to([P, 16, CHUNK]), chunks(b_t), ALU.subtract, [r2, c])
        c = p.activation(v_f, v_f, ACT.Exp, [d], scale=TAU)
        r4 = p.tt(k_t, k_t, v_f, ALU.mult, [c, r2])
        v_free = r4
        ready = [r1, r2, r3]
        for i, (dst, off) in enumerate(((v0, "bv"), (v1, "bv"))):
            view, banks, tok = w_in(OFF3[off] + (2 * h + i) * P)
            e = p.copy(v_f, view, [tok, v_free])
            p.free(banks, e)
            for half in range(2):
                t = p.mm([(ps[:, 6 + half, n * P:(n + 1) * P], v_f[:, (4 * half + n) * P:(4 * half + n + 1) * P], p.ident[:, :], True, True)
                          for n in range(4)], [e, p.bank_free[6 + half]], transpose=True)
                c = p.copy(dst[:, half * 512:(half + 1) * 512], ps[:, 6 + half, :], [t, done])
                p.free([6 + half], c)
                ready.append(c)
            v_free = t
        gates = []
        for i, dst in enumerate((g0, g1)):
            view, banks, tok = w_in(OFF3["bgate"] + (2 * h + i) * P)
            e = p.activation(dst, view, ACT.Silu, [tok, done])
            p.free(banks, e)
            gates.append(e)
        for half in range(2):
            t = p.mm([(ps[:, 6 + half, n * P:(n + 1) * P], k_t[:, (4 * half + n) * P:(4 * half + n + 1) * P], p.ident[:, :], True, True)
                      for n in range(4)], [r4, p.bank_free[6 + half]], transpose=True)
            c = p.copy(kd_tok[:, half * 512:(half + 1) * 512], ps[:, 6 + half, :], [t, done])
            p.free([6 + half], c)
            ready.append(c)
        state = lambda c: states[:, (c % 4) * 256:(c % 4) * 256 + 256]
        s_ready, s_used, pair_used, o_last = {}, {}, [done, done], []

        def update(c):
            bank, n, rows = 7, c // 2, slice(64 * (c % 2), 64 * (c % 2) + 64)
            t = p.mm([(ps[:, bank, i * P:(i + 1) * P], kd_tok[rows, n * P:(n + 1) * P], v[rows, n * P:(n + 1) * P], True, True)
                      for i, v in enumerate((v0, v1))], [ready, p.bank_free[bank]])
            if c == 0:
                s = p.dcopy(state(1), ps[:, bank, 0:256], [t, done])
            else:
                s = p.stt(state(c + 1), state(c), ends[:, c:c + 1], ps[:, bank, 0:256], ALU.mult, ALU.add,
                          [t, s_ready[c], decay, s_used.get(c - 3)])
            p.free([bank], s)
            s_ready[c + 1] = s

        update(0)
        for n in range(8):
            bank = 4 + n % 2
            cols = slice(n * P, (n + 1) * P)
            t = p.mm([(ps[:, bank, 0:P], ke[:, cols], qe[:, cols], True, True)], [ready, p.bank_free[bank]])
            tri = pair[:, n % 2, :]
            c1 = p.tt(tri[0:64, 0:64], ps[0:64, bank, 0:64], p.upper[0:64, 0:64], ALU.mult, [t, z, pair_used[n % 2]])
            c2 = p.tt(tri[64:128, 64:128], ps[64:128, bank, 64:128], p.upper[64:128, 64:128], ALU.mult, [t, z])
            p.free([bank], c2)
            if n:
                update(2 * n)
            products = []
            for i, v in enumerate((v0, v1)):
                o = i * P
                products.append((ps[:, 6, o:o + P], v[:, cols], tri, True, False))
                if n:
                    products.append((ps[:, 6, o:o + 64], state(2 * n)[:, o:o + P], q_t[:, n * P:n * P + 64], False, False))
                products.append((ps[:, 6, o + 64:o + P], state(2 * n + 1)[:, o:o + P], q_t[:, n * P + 64:(n + 1) * P], False, True))
            t = p.mm(products, [c1, c2, s_ready.get(2 * n), s_ready[2 * n + 1], p.bank_free[6]])
            pair_used[n % 2] = s_used[2 * n] = s_used[2 * n + 1] = t
            e = p.copy(mix[:, 2 * h:2 * h + 2, cols], ps[:, 6, 0:256].rearrange("p (i t) -> p i t", i=2), [t, spilled_a])
            p.free([6], e)
            o_last.append(e)
            if n < 7:
                update(2 * n + 1)
        pe_done = p.pe.last()
        rs, _ = p.norm([M[2 * h], M[2 * h + 1]], [o_last, o_last], TWO, 256, EPS, (b_t, e_t, qe), (ke, kd_tok), banks=(4, 5), after=pe_done)
        for i, g in enumerate((g0, g1)):
            c = p.stt(M[2 * h + i], M[2 * h + i], p.column("b_norm_g_3", 2 * h + i), b_t, ALU.mult, ALU.mult, [rs])
            c = p.tt(M[2 * h + i], M[2 * h + i], g, ALU.mult, [c, gates[i]])
            b_ready.append(c)
        done = [c, p.pe.last(), p.act.last()]

    done = p.everything()
    a_back = [Dma(p.sp, p.sem(f"a_back{i}")) for i in range(2)]
    a_landed = [a_back[i].start(p.res[:, 4 * i:4 * i + 4, 0:S], dram["spill_a"][:, 4 * i:4 * i + 4, 0:S], [done, spilled_a]) for i in range(2)]
    operand = [p.split(M[k], k, 0, S, [b_ready[k], done]) for k in range(8)]
    switch = p.everything()
    ctx.close()
    ctx = ExitStack()
    a_hi = p.sbuf("a_hi", [P, 8, S], F32R, ctx=ctx)
    a_lo = p.sbuf("a_lo", [P, 8, S], F32R, ctx=ctx)
    operand += [p.split(p.res[:, k, 0:S], k, 0, S, [a_landed[k // 4], switch], a_hi, a_lo) for k in range(8)]
    y = [p.res[:, k, 0:S] for k in range(8)]
    ready = []
    for m in range(8):
        view, banks, tok = p.product([block_of("w_out_3", (8 + k) % 16, m * P) for k in range(16)],
                                     lambda k: (p.x_hi if k < 8 else a_hi)[:, k % 8, :], lambda k: (p.x_lo if k < 8 else a_lo)[:, k % 8, :],
                                     TWO, operand)
        e = p.copy(y[m], view, [tok, operand[8 + m]])
        p.free(banks, e)
        ready.append(e)
    switch = p.everything()
    ctx.close()
    ctx = ExitStack()
    x3 = p.sbuf("x3_again", [P, 8, S], ctx=ctx)
    scratch = p.sbuf("last_scratch", [P, 5, S], ctx=ctx)
    back = [Dma(p.sp, p.sem(f"x3_back{i}")) for i in range(2)]
    landed = [back[i].start(x3[:, 4 * i:4 * i + 4, :], dram["spill_3"][:, 4 * i:4 * i + 4, 0:S], [switch, spilled]) for i in range(2)]
    sc = [scratch[:, i, :] for i in range(5)]
    rs, _ = p.norm(y, ready, TWO, D, EPS, sc[0:3], sc[3:5], banks=(4, 5), after=switch)
    stores = [Dma(p.sp, p.sem(f"stored{k}")) for k in range(4)]
    tokens = []
    for k in range(8):
        c = p.stt(y[k], y[k], p.column("post_norm_g_3", k), sc[0], ALU.mult, ALU.mult, [rs])
        c = p.tt(y[k], y[k], x3[:, k, :], ALU.add, [c, landed[k // 4]])
        tokens.append(stores[k % 4].start(out[k], y[k], [c, tokens[k - 4] if k >= 4 else None]))
    p.sp.wait(tokens)
    ctx.close()


def run_layers(p, out):
    acc, switch = layer_1(p)
    acc, switch = layer_2(p, acc, switch)
    layer_3(p, acc, switch, out)
    assert len(p.blocks) == N_BLOCKS, (len(p.blocks), N_BLOCKS)


def build(nc, dram, out):
    ctx = ExitStack()
    with ctx:
        p = Program(nc, ctx, dram)
        run_layers(p, out)
        with nc.Block() as block:
            @block.sync
            def _(e):
                p.sp.emit(e)

            @block.tensor
            def _(e):
                p.pe.emit(e)

            @block.vector
            def _(e):
                p.dve.emit(e)

            @block.scalar
            def _(e):
                p.act.emit(e)

            @block.gpsimd
            def _(e):
                p.pool.emit(e)
    return p.blocks


def weight_array(blocks, inputs):
    w = np.zeros((N_TILES, P, BLOCKS, P), np.float32)
    for i, (name, row, rows, cols) in enumerate(blocks):
        src = inputs[name][0]
        for to, start, n in cols:
            w[i // BLOCKS, 0:rows, i % BLOCKS, to:to + n] = src[row:row + rows, start:start + n]
    return w


def constant_arrays():
    head_row = np.zeros((H1, H1, P), np.float32)
    head_row[np.arange(H1), np.arange(H1)] = 1.0
    fix = np.ones((P, 4, 16), np.float32)
    for g in range(4):
        fix[:, g] = (2 << g) / np.minimum(np.arange(1, 17), 2 << g)
    freq = (np.float32(1.0) / np.float32(10000.0) ** (np.arange(0, ROPE, 2, dtype=np.float32) / np.float32(ROPE))).astype(np.float32)
    angle = (np.arange(WIDE, dtype=np.float32)[None, :] * freq[:, None]).astype(np.float32)
    rope = np.zeros((P, WIDE), np.float32)
    rope[64:80] = rope[80:96] = np.cos(angle)
    rope[96:112], rope[112:128] = -np.sin(angle), np.sin(angle)
    return {"identity": np.eye(P, dtype=np.float32), "upper": np.triu(np.ones((P, P), np.float32)),
            "head_row": head_row, "pool_fix": fix, "rope": rope}


def kernel(**inputs):
    import concourse.bacc as bacc
    from concourse.bass_utils import run_bass_kernel_spmd

    inputs = {k: np.asarray(v) for k, v in inputs.items()}
    nc = bacc.Bacc("TRN2", target_bir_lowering=False, num_devices=1)
    vectors = np.concatenate([inputs[name].reshape(-1, P) for name, _ in VECTORS]).T
    gate_bias = np.zeros((P, 1), np.float32)
    gate_bias[0:4, 0], gate_bias[32:36, 0] = inputs["b_gate"][0, :4], inputs["b_gate"][0, 4:]
    arrays = {
        "x": inputs["x"][0].T.reshape(DC, P, S),
        "vectors": vectors,
        "gate_bias": gate_bias,
        "w_pool": inputs["w_pool"][0].transpose(1, 0, 2),
        "meta": inputs["meta_tokens_2"].T.reshape(DC, P, META).transpose(1, 0, 2),
        "w_a2": inputs["w_a2_3"][0],
        "a_w_s": inputs["a_w_s_3"][0].transpose(2, 0, 1),
        "a_b_s": inputs["a_b_s_3"][0].reshape(1, 8 * P),
        **constant_arrays(),
    }
    arrays = {k: np.ascontiguousarray(v) for k, v in arrays.items()}
    dram = {k: nc.dram_tensor(f"{k}_dram", v.shape, mybir.dt.from_np(v.dtype), kind="ExternalInput").ap()
            for k, v in arrays.items()}
    dram["w"] = nc.dram_tensor("w_dram", (N_TILES, P, BLOCKS, P), F32, kind="ExternalInput").ap()
    for name in ("spill_2", "spill_3", "spill_a"):
        dram[name] = nc.dram_tensor(name, (P, DC, WIDE), F32).ap()
    out = nc.dram_tensor("out_dram", (DC, P, S), F32, kind="ExternalOutput").ap()
    blocks = build(nc, dram, out)
    arrays["w"] = weight_array(blocks, inputs)
    r = run_bass_kernel_spmd(nc, [{f"{k}_dram": v for k, v in arrays.items()}], core_ids=[0])
    return np.ascontiguousarray(r.results[0]["out_dram"].reshape(D, S).T)[None]
```

```python
from contextlib import ExitStack

import numpy as np

import concourse.bass as bass
from concourse import mybir

P = 128
S = 1024
D = 1024
DC = D // P
META = 16
WIDE = 1044
F32, F32R = mybir.dt.float32, mybir.dt.float32r
ACT, ALU, AX = mybir.ActivationFunctionType, mybir.AluOpType, mybir.AxisListType
ALPHA = 2.0 ** 0.25
LN_EPS, EPS = 1e-5, 1e-6
BLOCKS = 8

TWO = [(0, 512), (512, 512)]
THREE = [(0, 348), (348, 348), (696, 348)]
FFN2 = [(14, 342), (356, 342), (698, 342)]

H1, FF1 = 4, 32
OFF_G, OFF_O, OFF_P = 1536, 1544, 2056
CONV1 = 4
H2, QK, NOPE, ROPE = 8, 96, 64, 32
CONV2, FF2, CONV3 = 31, 22, 3
H3, CHUNK = 4, 64
OFF3 = dict(u=0, v=1024, gate=2048, q=3072, k=3584, bv=4096, bgate=5120, lr=6144)

N_BLOCKS = (
    8 * (1 + 4 * 4 + 4) + 8 * 8 + 2 * 8 * 32
    + 8 * 14 + 4 * 2 * 2 + 8 * 3 + 8 * 8 + 3 * 8 * 22
    + 8 * (8 * 3 + 1 + 4 * 6) + 16 * 8
)
N_TILES = -(-N_BLOCKS // BLOCKS)

VECTORS = [
    ("w_conv", CONV1 * 8), ("hn_g", 4), ("pool_scale", 4), ("ln1_g", 8), ("ln1_b", 8), ("ln2_g", 8), ("ln2_b", 8),
    ("mix_norm_g_2", 8), ("q_norm_g_2", 3), ("kv_norm_g_2", 2), ("conv_w_2", CONV2 * 4), ("conv_b_2", 4),
    ("conv_ln_g_2", 4), ("conv_ln_b_2", 4), ("conv_out_g_2", 4), ("attn_out_g_2", 4), ("ffn_norm_g_2", 8),
    ("ffn_conv_w_2", CONV3 * 44), ("ffn_conv_b_2", 44), ("final_norm_g_2", 8), ("pre_norm_g_3", 8), ("b_a2_3", 4),
    ("a_ln_g_3", 8), ("a_ln_b_3", 8), ("b_norm_g_3", 8), ("post_norm_g_3", 8),
]
VCOL = {}
for _name, _n in VECTORS:
    VCOL[_name] = sum(n for _, n in VECTORS[:len(VCOL)])
N_VEC = sum(n for _, n in VECTORS)


class Engine:

    def __init__(self, sem):
        self.sem, self.count, self.steps, self.waited = sem, 0, [], {}

    def wait(self, after):
        for token in after:
            if token is None:
                continue
            if isinstance(token, list):
                self.wait(token)
                continue
            sem, value = token
            if self.waited.get(sem.name, 0) < value:
                self.waited[sem.name] = value
                self.steps.append(lambda e, sem=sem, value=value: e.wait_ge(sem, value))

    def run(self, step, after=()):
        self.wait(after)
        self.steps.append(step)

    def do(self, step, after=()):
        self.wait(after)
        self.count += 1
        self.steps.append(lambda e: step(e).then_inc(self.sem, 1))
        return (self.sem, self.count)

    def last(self):
        return (self.sem, self.count) if self.count else None

    def emit(self, e):
        for step in self.steps:
            step(e)


class Dma:

    def __init__(self, engine, sem):
        self.engine, self.sem, self.count = engine, sem, 0

    def start(self, out, in_, after=()):
        self.count += 16
        self.engine.run(lambda e: e.dma_start(out() if callable(out) else out,
                                              in_() if callable(in_) else in_).then_inc(self.sem, 16), after)
        return (self.sem, self.count)


class Program:
    def __init__(self, nc, ctx, dram):
        self.nc, self.ctx, self.dram = nc, ctx, dram
        self.n_sem = 0
        self.pe, self.dve, self.act, self.pool, self.sp = (
            Engine(self.sem(n)) for n in ("pe_done", "dve_done", "act_done", "pool_done", "sp_done"))
        sb = self.sbuf
        self.w_raw = [sb(f"w_raw{i}", [P, BLOCKS, P]) for i in range(3)]
        self.w_hi = [sb(f"w_hi{i}", [P, BLOCKS, P], F32R) for i in range(3)]
        self.w_lo = [sb(f"w_lo{i}", [P, BLOCKS, P], F32R) for i in range(3)]
        self.w_dma = [Dma(self.sp, self.sem(f"w_landed{i}")) for i in range(3)]
        self.w_landed, self.w_ready, self.w_used = [], [], []
        self.blocks = []
        self.x_hi = sb("x_hi", [P, DC, WIDE], F32R)
        self.x_lo = sb("x_lo", [P, DC, WIDE], F32R)
        self.res = sb("res", [P, DC, WIDE])
        self.vec = sb("vectors", [P, N_VEC])
        self.ident = sb("identity", [P, P])
        self.upper = sb("upper", [P, P])
        self.ones = sb("ones", [P, P])
        self.head_row = sb("head_row", [H1, H1, P])
        self.tiny = sb("tiny", [P, 4])
        self.ps = ctx.enter_context(nc.psum_tensor("psum", [P, 8, 512], F32))
        self.bank_free = [None] * 8
        self.slot = 0
        self.jobs = []

        once = Dma(self.sp, self.sem("constants_landed"))
        once.start(self.vec[:, :], dram["vectors"])
        once.start(self.ident[:, :], dram["identity"])
        once.start(self.upper[:, :], dram["upper"])
        self.const = [once.start(self.head_row[:, :, :], dram["head_row"])]
        self.const.append(self.dve.do(lambda e: e.memset(self.ones[:, :], 1.0)))
        for i, value in enumerate((LN_EPS, EPS, 1.0)):
            self.const.append(self.dve.do(lambda e, i=i, value=value: e.memset(self.tiny[:, i:i + 1], value)))

    def sem(self, name):
        return self.ctx.enter_context(self.nc.semaphore(name))

    def sbuf(self, name, shape, dt=F32, ctx=None):
        return (ctx or self.ctx).enter_context(self.nc.sbuf_tensor(name, shape, dt))

    def everything(self):
        return [e.last() for e in (self.pe, self.dve, self.act, self.pool)]

    def column(self, name, i):
        c = VCOL[name] + i
        return self.vec[:, c:c + 1]

    def activation(self, out, in_, func, after, bias=0.0, scale=1.0, accum=None):
        if accum is None:
            return self.act.do(lambda e: e.activation(out, in_, func, bias=bias, scale=scale), after)
        return self.act.do(lambda e: e.activation(out, in_, func, bias=bias, scale=scale, accum_out=accum), after)

    def copy(self, out, in_, after):
        return self.act.do(lambda e: e.copy(out, in_), after)

    def tt(self, out, a, b, op, after, eng=None):
        return (eng or self.dve).do(lambda e: e.tensor_tensor(out, a, b, op), after)

    def ts(self, out, a, s1, s2, op0, op1, after):
        if s2 is None:
            return self.dve.do(lambda e: e.tensor_scalar(out, a, s1, None, op0), after)
        return self.dve.do(lambda e: e.tensor_scalar(out, a, s1, s2, op0, op1), after)

    def stt(self, out, a, s, b, op0, op1, after):
        return self.dve.do(lambda e: e.scalar_tensor_tensor(out, a, s, b, op0, op1), after)

    def dcopy(self, out, in_, after):
        return self.dve.do(lambda e: e.tensor_copy(out, in_), after)

    def memset(self, out, value, after=()):
        return self.dve.do(lambda e: e.memset(out, value), after)

    def mm(self, products, after, transpose=False):
        def step(e):
            for out, lhsT, rhs, start, stop in products:
                if transpose:
                    ins = e.transpose(out, lhsT, rhs)
                else:
                    ins = e.matmul(out, lhsT, rhs, start=start, stop=stop, skip_group_check=True)
            return ins
        return self.pe.do(step, after)

    def prefetch(self, tile):
        while len(self.w_ready) < min(tile + 3, N_TILES):
            n = len(self.w_ready)
            if n >= 3 and n - 3 >= len(self.w_used):
                break
            self.load_tile(n)
            raw, hi, lo = self.w_raw[n % 3], self.w_hi[n % 3], self.w_lo[n % 3]
            used = self.w_used[n - 3] if n >= 3 else None
            high = self.copy(hi[:, :, :], raw[:, :, :], [self.w_landed[n], used])
            low = self.tt(lo[:, :, :], raw[:, :, :], hi[:, :, :].bitcast(F32), ALU.subtract,
                          [high, self.w_landed[n], used], self.pool)
            self.w_ready.append(low)
        for n in range(len(self.w_landed), min(len(self.w_ready) + 3, N_TILES)):
            self.load_tile(n)

    def load_tile(self, n):
        if n < len(self.w_landed):
            return
        freed = self.w_ready[n - 3] if n >= 3 else None
        self.w_landed.append(self.w_dma[n % 3].start(self.w_raw[n % 3][:, :, :], self.dram["w"][n], [freed]))

    def product_steps(self, chunks, hi, lo, pieces, x_ready, take):
        width = len(pieces)
        first = self.slot * (2 if width == 2 else 3)
        banks = range(first, first + width)
        self.slot = (self.slot + 1) % 2
        wait_banks = [self.bank_free[b] for b in banks]
        start = len(self.blocks)
        self.blocks += chunks
        token = None
        for i, (t0, m) in enumerate(pieces):
            for k in range(len(chunks)):
                tile, at = divmod(start + k, BLOCKS)
                if i == 0 and (at == 0 or k == 0):
                    self.prefetch(tile)
                last_k = k == len(chunks) - 1

                def step(e, whi=self.w_hi[tile % 3][:, at, :], wlo=self.w_lo[tile % 3][:, at, :],
                         out=self.ps[:, first + i, 0:m], xhi=hi(k)[:, t0:t0 + m], xlo=lo(k)[:, t0:t0 + m],
                         first_k=k == 0, last_k=last_k):
                    e.matmul(out, whi, xhi, start=first_k, stop=False, skip_group_check=True)
                    e.matmul(out, whi, xlo, start=False, stop=False, skip_group_check=True)
                    return e.matmul(out, wlo, xhi, start=False, stop=last_k, skip_group_check=True)
                ready = x_ready[k]
                if isinstance(ready, PerPiece):
                    ready = ready[i]
                after = [self.w_ready[tile], ready] + (wait_banks if k == 0 and i == 0 else [])
                used = i == width - 1 and (at == BLOCKS - 1 or start + k == N_BLOCKS - 1)
                if used or (last_k and i == width - 1):
                    token = self.pe.do(step, after)
                    if used:
                        self.w_used.append(token)
                else:
                    self.pe.run(step, after)
                if i < width - 1 or not last_k:
                    yield
        done = take(self.ps[:, first:first + width, 0:pieces[0][1]], list(banks), token)
        self.free(banks, done)
        yield

    def product(self, *args):
        self.jobs.append(self.product_steps(*args))

    def pump(self, n):
        while n > 0 and self.jobs:
            try:
                next(self.jobs[0])
                n -= 1
            except StopIteration:
                self.jobs.pop(0)

    def drain(self, keep=0):
        while len(self.jobs) > keep:
            for _ in self.jobs.pop(0):
                pass

    def take_slot(self):
        first = 3 * self.slot
        self.slot = (self.slot + 1) % 2
        return [first, first + 1, first + 2]

    def free(self, banks, token):
        for b in banks:
            self.bank_free[b] = token

    def x_parts(self):
        return (lambda k: self.x_hi[:, k, :]), (lambda k: self.x_lo[:, k, :])

    def split(self, src, k, t0, t1, after, hi=None, lo=None, eng=None):
        hi, lo = self.x_hi if hi is None else hi, self.x_lo if lo is None else lo
        high = self.copy(hi[:, k, t0:t1], src, after)
        return self.tt(lo[:, k, t0:t1], src, hi[:, k, t0:t1].bitcast(F32), ALU.subtract, [high, after], eng)

    def split_scaled(self, src, column, k, t0, t1, after, grid=lambda t: t):
        hi, lo = grid(self.x_hi[:, k, t0:t1]), grid(self.x_lo[:, k, t0:t1])
        high = self.activation(hi, src, ACT.Copy, after, scale=column)
        return self.stt(lo, src, column, hi.bitcast(F32), ALU.mult, ALU.subtract, [high, after])

    def ones_product(self, view, pieces, banks, after):
        return self.mm([(self.ps[:, b, 0:m], self.ones[:, :], view[:, t0:t0 + m], True, True)
                        for b, (t0, m) in zip(banks, pieces)], [after, self.const, [self.bank_free[b] for b in banks]])

    def inverse_root(self, out, scratch, sums, n, eps, after, factor=None):
        eps_col = self.tiny[:, 0:1] if eps == LN_EPS else self.tiny[:, 1:2]
        a = self.activation(out, sums, ACT.Ln, [after, self.const], bias=eps_col, scale=1.0 / n)
        b = self.activation(out, out, ACT.Exp, [a], scale=-0.5)
        c = self.tt(scratch, out, out, ALU.mult, [b])
        d = self.stt(scratch, sums, n * eps, scratch, ALU.add, ALU.mult, [c])
        e = self.ts(scratch, scratch, -0.5 / n, 1.5, ALU.mult, ALU.add, [d])
        return self.tt(out, out, scratch, ALU.mult, [e])

    def norm(self, xs, ready, pieces, n, eps, scratch, squares, banks=(0, 1, 2), center=False, after=None, fill=0):
        view = lambda t: t[:, pieces[0][0]:pieces[-1][0] + pieces[-1][1]]
        grid = lambda t: view(t).rearrange("p (a b) -> p a b", a=len(pieces))
        banks = list(banks)[:len(pieces)]
        sums = self.ps[:, banks[0]:banks[0] + len(pieces), 0:pieces[0][1]]
        rstd, mean, tmp = scratch
        if center:
            x, r = xs[0], ready[0]
            if len(xs) > 1:
                x = tmp
                r = self.tt(view(tmp), view(xs[0]), view(xs[1]), ALU.add, [ready[0], ready[1], after])
                for y, s in zip(xs[2:], ready[2:]):
                    r = self.tt(view(tmp), view(tmp), view(y), ALU.add, [r, s])
            s = self.ones_product(x, pieces, banks, r)
            self.pump(fill)
            m = self.activation(grid(mean), sums, ACT.Copy, [s, self.dve.last(), after], scale=1.0 / n)
            self.free(banks, m)
            ready = [self.tt(view(x), view(x), view(mean), ALU.subtract, [m, r, s]) for x, r in zip(xs, ready)]
        sums_of = Moments(self, squares[0], squares[1:] + (tmp,) if isinstance(squares, tuple) else list(squares[1:]) + [tmp],
                          len(xs), view, [after, self.dve.last()])
        for x, r in zip(xs, ready):
            sums_of.square(view(x), r)
        s = self.ones_product(squares[0], pieces, banks, sums_of.token)
        self.pump(fill)
        rs = self.inverse_root(grid(rstd), grid(tmp), sums, n, eps, [s, self.dve.last(), after])
        self.free(banks, rs)
        return rs, ready


def layer_norm(p, xs, ready, sums_token, mean, rstd, tmp, squares, n, eps, apply, after, fill=0):
    used = [after] * len(squares)
    centred, roots, turn = {}, [], 0
    for i in range(2):
        cols = slice(512 * i, 512 * i + 512)
        m = p.activation(mean[:, cols], p.ps[:, 4 + i, :], ACT.Copy, [sums_token, after], scale=1.0 / n)
        p.free([4 + i], m)
        for k, x in enumerate(xs):
            centred[k, i] = p.tt(x[:, cols], x[:, cols], mean[:, cols], ALU.subtract, [m, ready[k]])
            r = turn % len(squares)
            turn += 1
            sq = squares[r][:, 0:512]
            q = p.activation(sq, x[:, cols], ACT.Square, [centred[k, i], used[r]])
            used[r] = p.mm([(p.ps[:, 6 + i, :], p.ones[:, :], sq, k == 0, k == len(xs) - 1)],
                           [q, p.const, p.bank_free[6 + i] if k == 0 else None])
            p.pump(fill)
        roots.append(used[r])
    for i in range(2):
        cols = slice(512 * i, 512 * i + 512)
        root = p.inverse_root(rstd[:, cols], tmp[:, cols], p.ps[:, 6 + i, :], n, eps, [roots[i], after])
        p.free([6 + i], root)
        for k, x in enumerate(xs):
            apply(k, i, cols, x[:, cols], rstd[:, cols], [root, centred[k, i]])


class PerPiece(list):
    pass


class Moments:

    def __init__(self, p, total, squares, n, view=lambda t: t, after=None):
        self.p, self.total, self.squares, self.view, self.token, self.i = p, total, squares, view, None, 0
        self.used, self.after = [after] * len(squares), after

    def square(self, x, ready, scale=1.0):
        p, i = self.p, self.i
        self.i += 1
        if i == 0:
            self.token = p.activation(self.view(self.total), x, ACT.Square, [ready, self.after], scale=scale)
            return
        r = i % len(self.squares)
        sq = self.view(self.squares[r])
        c = p.activation(sq, x, ACT.Square, [ready, self.used[r]], scale=scale)
        self.token = self.used[r] = p.tt(self.view(self.total), self.view(self.total), sq, ALU.add, [c, self.token])


def block_of(name, k, cols):
    return (name, k * P, P, [(0, cols, P)] if isinstance(cols, int) else cols)


FILL = (20, 2, 8)


def layer_1(p):
    nc, dram, ps = p.nc, p.dram, p.ps
    hi, lo = p.x_parts()
    ctx = ExitStack()
    mix = p.sbuf("mix_1", [P, 8, WIDE], ctx=ctx)
    work = p.sbuf("work_1", [P, 7, WIDE], ctx=ctx)
    w_pool = p.sbuf("w_pool", [P, 4, P], ctx=ctx)
    gate_bias = p.sbuf("gate_bias", [P, 1], ctx=ctx)
    pool_fix = p.sbuf("pool_fix", [P, 4, 16], ctx=ctx)
    b_cols = p.sbuf("b_cols", [P, 8, H1], ctx=ctx)

    xin = [Dma(p.sp, p.sem(f"x_landed{k % 4}")) if k < 4 else None for k in range(8)]
    x_ready = []
    for k in range(8):
        landed = xin[k % 4].start(p.res[:, k, 0:S], dram["x"][k], [x_ready[k - 4] if k >= 4 else None])
        if k == 0:
            p.prefetch(0)
        x_ready.append(p.split(p.res[:, k, 0:S], k, 0, S, [landed]))
    small = Dma(p.sp, p.sem("small_1_landed"))
    small.start(gate_bias[:, :], dram["gate_bias"])
    small.start(pool_fix[:, :, :], dram["pool_fix"])
    const = p.const + [small.start(w_pool[:, :, :], dram["w_pool"])]

    T = [p.res[:, i, :] for i in range(8)] + [work[:, i, :] for i in range(7)]
    row_b, row_m, row_am, row_t, row_u = T[0], T[1], T[2], T[3], T[4]
    q_in, k_in, q_t, k_t = T[3], T[4], T[5], T[6]
    v_f, v_t, m_bc, floor, prob = T[7], T[8], T[9], T[10], T[11]
    o_sig = [T[12], T[13]]
    hbuf = T[14]
    tmp = v_f
    res_free = x_ready[-1]

    gts = work[:, 5, 0:S]

    def take_gates(view, banks, tok):
        return p.ts(gts[0:36, :], ps[0:36, banks[0]:banks[0] + 2, :], gate_bias[0:36, :], None, ALU.add, None, [tok, const])

    p.product([block_of("w_in", k, [(0, OFF_G, 4), (32, OFF_G + 4, 4)]) for k in range(8)], hi, lo, TWO, x_ready, take_gates)
    p.drain()
    a = p.dve.last()
    i_row, f_row, l_row, e_row = work[0:4, 5, 0:S], work[0:4, 6, 0:S], work[0:4, 0, 0:S], work[0:4, 1, 0:S]
    one_row = work[0:4, 2, 0:S]
    b = p.dcopy(f_row, gts[32:36, :], [a])
    c = p.stt(e_row, f_row, -1.0, f_row, ALU.mult, ALU.max, [b])
    c = p.activation(e_row, e_row, ACT.Exp, [c], scale=-1.0)
    c = p.activation(e_row, e_row, ACT.Ln, [c, const], bias=p.tiny[0:4, 2:3])
    c = p.stt(l_row, f_row, 0.0, e_row, ALU.min, ALU.subtract, [c])
    one = p.memset(one_row, 1.0)
    A, B, M, AM = work[0:4, 3, 0:S], row_b[0:4, 0:S], row_m[0:4, 0:S], row_am[0:4, 0:S]
    c = p.dve.do(lambda e: e.tensor_tensor_scan(A, one_row, l_row, 0.0, ALU.mult, ALU.add), [c, one])
    bt = p.tt(B, i_row, A, ALU.subtract, [c, res_free])
    mt = p.dve.do(lambda e: e.tensor_tensor_scan(M, one_row, B, 0.0, ALU.mult, ALU.max), [bt])
    amt = p.tt(AM, A, M, ALU.add, [mt])
    t = p.mm([(ps[:, 4, 4 * j:4 * j + 4], row_b[0:4, j * P:(j + 1) * P], p.ident[0:4, 0:4], True, True) for j in range(8)],
             [bt, const], transpose=True)
    cols = p.dcopy(b_cols[:, :, :], ps[:, 4, 0:32], [t])
    p.free([4], cols)
    pads = [p.memset(x[:, 0:3], 0.0, [res_free]) for x in (q_in, k_in)]

    state = dict(q_in=None, v_f=None, q=None, v=None, o=[None, None], m_bc=None, prob=[None, None], h=None)

    def products_of_head(h):
        out = {}
        for n, off in (("q", 0), ("k", 512), ("v", 1024), ("o", OFF_O)):
            def take(view, banks, tok, n=n):
                if n == "o":
                    e = p.activation(o_sig[h % 2][:, 0:S], view, ACT.Sigmoid, [tok, state["o"][h % 2]])
                elif n == "v":
                    e = p.copy(v_f[:, 0:S], view, [tok, state["v_f"], res_free])
                else:
                    e = p.copy((q_in if n == "q" else k_in)[:, 3:3 + S], view, [tok, state["q_in"], res_free])
                out[n] = e
                return e
            p.product([block_of("w_in", k, off + h * P) for k in range(8)], hi, lo, TWO, x_ready, take)
        return out

    def prepare(h, got):
        ready = []
        for n, src, dst in (("q", q_in, q_t), ("k", k_in, k_t)):
            chunk = h + (4 if n == "k" else 0)
            acc = dst[:, 0:S]
            w = lambda j: p.column("w_conv", j * 8 + chunk)
            c = p.ts(acc, src[:, 0:S], w(0), None, ALU.mult, None, [got[n], pads, state["q"], const, res_free])
            for j in range(1, CONV1):
                c = p.stt(acc, src[:, j:j + S], w(j), acc, ALU.mult, ALU.add, [c])
            state["q_in"] = c
            c = p.activation(acc, acc, ACT.Silu, [c])
            if n == "k":
                c = p.ts(acc, acc, P ** -0.5, None, ALU.mult, None, [c])
            ready.append(c)
        for g in range(2):
            t = p.mm([(ps[:, 4 + g, j * P:(j + 1) * P], v_f[:, (4 * g + j) * P:(4 * g + j + 1) * P], p.ident[:, :], True, True)
                      for j in range(4)], [got["v"], const, p.bank_free[4 + g]], transpose=True)
            state["v_f"] = t
            e = p.copy(v_t[:, g * 512:(g + 1) * 512], ps[:, 4 + g, :], [t, state["v"]])
            p.free([4 + g], e)
            ready.append(e)
        return ready

    def attend(h, ready, got):
        p.pump(FILL[0])
        for row, dst, tok in ((M, m_bc, mt), (AM, floor, amt)):
            for g in range(2):
                t = p.mm([(ps[:, 4 + g, :], p.head_row[:, h, :], row[:, g * 512:(g + 1) * 512], True, True)],
                         [tok, const, p.bank_free[4 + g]])
                half = dst[:, g * 512:(g + 1) * 512]
                if row is M:
                    e = p.copy(half, ps[:, 4 + g, :], [t, state["m_bc"]])
                    m_tok = e
                else:
                    e = p.activation(half, ps[:, 4 + g, :], ACT.Exp, [t, state["m_bc"]], scale=-1.0)
                    floor_tok = e
                p.free([4 + g], e)
        n = 0
        for half in range(2):
            blocks = []
            for j in range(4 * half + 4):
                t0 = max(half * 512, j * P)
                blocks.append((j, t0, (half + 1) * 512 - t0))

            def scores(i):
                j, t0, w = blocks[i]
                bank = 4 + i % 2
                return p.mm([(ps[:, bank, 0:w], k_t[:, j * P:(j + 1) * P], q_t[:, t0:t0 + w], True, True)],
                            [ready, p.bank_free[bank]])

            def weights(i, n):
                j, t0, w = blocks[i]
                pr = prob[:, (n % 2) * 512:(n % 2) * 512 + w]
                c = p.ts(pr, m_bc[:, t0:t0 + w], b_cols[:, j, h:h + 1], 0.0, ALU.subtract, ALU.max, [m_tok, cols, state["prob"][n % 2]])
                return pr, p.activation(pr, pr, ACT.Exp, [c], scale=-1.0)

            s_tok = {0: scores(0)}
            following = weights(0, n)
            for i, (j, t0, w) in enumerate(blocks):
                pr, c = following
                if i + 1 < len(blocks):
                    s_tok[i + 1] = scores(i + 1)
                    following = weights(i + 1, n + 1)
                p.pump(FILL[1])
                bank = 4 + i % 2
                if t0 == j * P:
                    c = p.tt(pr[:, 0:P], pr[:, 0:P], p.upper[:, :], ALU.mult, [c, const])
                c = p.tt(pr, pr, ps[:, bank, 0:w], ALU.mult, [c, s_tok[i]])
                p.free([bank], c)
                o0 = t0 - half * 512
                last = i == len(blocks) - 1
                t = p.mm([(ps[:, 6, o0:o0 + w], v_t[:, j * P:(j + 1) * P], pr, i == 0, last),
                          (ps[:, 7, o0:o0 + w], p.ones[:, :], pr, i == 0, last)],
                         [c, ready] + ([p.bank_free[6], p.bank_free[7]] if i == 0 else []))
                state["prob"][n % 2] = t
                n += 1
            sl = slice(half * 512, (half + 1) * 512)
            c = p.activation(hbuf[:, sl], ps[:, 7, :], ACT.Abs, [t, state["h"]])
            c = p.tt(floor[:, sl], hbuf[:, sl], floor[:, sl], ALU.max, [c, floor_tok])
            c = p.dve.do(lambda e, sl=sl: e.reciprocal(floor[:, sl], floor[:, sl]), [c])
            c = p.tt(hbuf[:, sl], ps[:, 6, :], floor[:, sl], ALU.mult, [c, state["h"]])
            p.free([6, 7], c)
        state["q"] = state["v"] = t
        rs, (r,) = p.norm([hbuf], [c], TWO, P, LN_EPS, (m_bc, floor, prob), (k_t, q_t), banks=(6, 7), center=True, after=p.pe.last(), fill=FILL[2])
        state["q"] = [state["q"], p.pe.last()]
        c = p.stt(hbuf[:, 0:S], hbuf[:, 0:S], p.column("hn_g", h), m_bc[:, 0:S], ALU.mult, ALU.mult, [rs, const])
        c = p.tt(mix[:, h, 0:S], hbuf[:, 0:S], o_sig[h % 2][:, 0:S], ALU.mult, [c, got["o"]])
        state["o"][h % 2] = state["m_bc"] = state["h"] = c
        state["prob"] = [c, c]
        return c

    def pool_product(g):
        def take(view, banks, tok):
            p_in = mix[:, 4 + g, :]
            e = p.copy(p_in[:, 0:S], view, [tok])
            src, dst, c = p_in, q_in, e
            for step in range(g + 1):
                shift = 1 << step
                c1 = p.tt(dst[:, shift:S], src[:, shift:S], src[:, 0:S - shift], ALU.add, [c])
                c = [c1, p.dcopy(dst[:, 0:shift], src[:, 0:shift], [c])]
                src, dst = dst, (k_in if dst is q_in else q_in)
            win = 2 << g
            c = p.tt(src[:, 0:16], src[:, 0:16], pool_fix[:, g, :], ALU.mult, [c, const])
            pooled[g] = p.stt(p_in[:, 0:S], src[:, 0:S], 1.0 / win, p_in[:, 0:S], ALU.mult, ALU.subtract, [c])
            return e
        p.product([block_of("w_in", k, OFF_P + g * P) for k in range(8)], hi, lo, TWO, x_ready, take)

    mix_ready, pooled = [None] * 8, {}
    got = products_of_head(0)
    p.drain()
    ready = prepare(0, got)
    for h in range(H1):
        if h + 1 < H1:
            got_next = products_of_head(h + 1)
        else:
            for g in range(4):
                pool_product(g)
        mix_ready[h] = attend(h, ready, got)
        p.drain()
        if h + 1 < H1:
            got = got_next
            ready = prepare(h + 1, got)

    old = p.pe.last()
    m_ready = {k: p.split(mix[:, k, 0:S], k, 0, S, [mix_ready[k], old]) for k in range(3)}
    for g in range(4):
        banks = [4 + 2 * (g % 2), 5 + 2 * (g % 2)]
        t = p.mm([(ps[:, banks[i], :], w_pool[:, g, :], mix[:, 4 + g, i * 512:(i + 1) * 512], True, True) for i in range(2)],
                 [pooled[g], const, p.bank_free[banks[0]], p.bank_free[banks[1]]])
        view, scale = ps[:, banks[0]:banks[0] + 2, :], p.column("pool_scale", g)
        grid = lambda t: t.rearrange("p (a b) -> p a b", a=2)
        m_ready[4 + g] = p.split_scaled(view, scale, 4 + g, 0, S, [t, old], grid)
        p.free(banks, m_ready[4 + g])
    m_ready[3] = p.split(mix[:, 3, 0:S], 3, 0, S, [mix_ready[3], old])

    back = [Dma(p.sp, p.sem(f"x_again_landed{i}")) for i in range(4)]
    free = p.everything()
    x_back = [back[i].start(p.res[:, 2 * i:2 * i + 2, META:META + S], dram["x"][2 * i:2 * i + 2].rearrange("k p t -> p k t"), free)
              for i in range(4)]
    real = lambda k: p.res[:, k, META:META + S]
    order = [0, 1, 2, 4, 5, 6, 7, 3]
    total, mean, rstd, tmp = (T[i][:, 0:S] for i in (8, 9, 10, 11))
    squares = [T[12], T[13], T[14]]
    r_ready = []
    for m in range(8):
        def take(view, banks, tok, m=m):
            c = p.stt(real(m), real(m), ALPHA, view, ALU.mult, ALU.add, [tok, x_back[m // 2]])
            r_ready.append(c)
            if m == 1:
                p.tt(total, real(0), real(1), ALU.add, [r_ready, free])
            elif m > 1:
                p.tt(total, total, real(m), ALU.add, [c, (p.dve.sem, p.dve.count - 1)])
            return c
        p.product([block_of("w_out", k, m * P) for k in order], lambda i: p.x_hi[:, order[i], :], lambda i: p.x_lo[:, order[i], :],
                  TWO, [m_ready[k] for k in order], take)
    p.drain()
    summed = p.ones_product(total, TWO, [4, 5], p.dve.last())
    old = p.pe.last()
    x1 = [PerPiece([None, None]) for _ in range(8)]

    def apply(k, i, cols, x, r, after):
        c = p.stt(x, x, p.column("ln1_g", k), r, ALU.mult, ALU.mult, after)
        c = p.activation(x, x, ACT.Identity, [c], bias=p.column("ln1_b", k))
        x1[k][i] = p.split(x, k, cols.start, cols.stop, [c, old])

    layer_norm(p, [real(k) for k in range(8)], r_ready, summed, mean, rstd, tmp, squares, D, LN_EPS, apply, free)
    switch = p.everything()
    ctx.close()

    ctx = ExitStack()
    h_hi = p.sbuf("h1_hi", [P, 6, S], F32R, ctx=ctx)
    h_lo = p.sbuf("h1_lo", [P, 6, S], F32R, ctx=ctx)
    tmp = p.sbuf("h1_tmp", [P, 2, S], ctx=ctx)
    total = p.sbuf("h1_total", [P, S], ctx=ctx)
    h_used = [switch] * 6
    t_used = [switch] * 2
    h_ready = {}
    acc = [None] * 8

    def hidden(j):
        def take(view, banks, tok):
            r = tmp[:, j % 2, :]
            e = p.activation(r, view, ACT.Relu, [tok, t_used[j % 2]])
            c = p.tt(r, r, r, ALU.mult, [e])
            c = p.split(r, j % 6, 0, S, [c, h_used[j % 6]], h_hi, h_lo)
            h_ready[j] = t_used[j % 2] = c
            return e
        p.product([block_of("w_ff1", k, j * P) for k in range(8)], hi, lo, TWO, x1, take)
        p.drain()

    def project(g):
        ks = range(4 * g, 4 * g + 4)
        for m in range(8):
            def take(view, banks, tok, m=m):
                out = real(m)
                c = p.stt(out, out, ALPHA if g == 0 else 1.0, view, ALU.mult, ALU.add, [tok, acc[m], x1[m]])
                acc[m] = c
                if g == FF1 // 4 - 1 and m:
                    p.tt(total[:, :], real(0) if m == 1 else total[:, :], real(m), ALU.add, [c, acc[0], (p.dve.sem, p.dve.count - 1), switch])
                return c
            p.product([block_of("w_ff2", k, m * P) for k in ks],
                      lambda i: h_hi[:, (4 * g + i) % 6, :], lambda i: h_lo[:, (4 * g + i) % 6, :],
                      TWO, [h_ready[k] for k in ks], take)
            p.drain()
        for k in ks:
            h_used[k % 6] = p.pe.last()

    for g in range(FF1 // 4):
        for j in range(4):
            if g == 0 or j >= 2:
                hidden(4 * g + j)
        if g + 1 < FF1 // 4:
            hidden(4 * g + 4)
            hidden(4 * g + 5)
        project(g)
    summed = p.ones_product(total[:, :], TWO, [4, 5], p.dve.last())
    switch = p.everything()
    ctx.close()
    return acc, summed, switch


def layer_2(p, acc, summed, switch):
    nc, dram, ps = p.nc, p.dram, p.ps
    hi, lo = p.x_parts()
    real = lambda k: p.res[:, k, META:META + S]
    grid = lambda t: t.rearrange("p (a b) -> p a b", a=3)
    ctx = ExitStack()
    mix = p.sbuf("mix_2", [P, 8, WIDE], ctx=ctx)
    u_pad = p.sbuf("u_padded", [P, 4, CONV2 - 1 + WIDE], ctx=ctx)
    work = p.sbuf("work_2", [P, 4, WIDE], ctx=ctx)
    small = p.sbuf("v_and_probs_of_meta", [P, 3, P], ctx=ctx)
    col = p.sbuf("softmax_columns", [P, 4, 4], ctx=ctx)
    pair_out = p.sbuf("pair_out", [P, 2, P], ctx=ctx)
    M = [mix[:, i, :] for i in range(8)]

    meta_dma = Dma(p.sp, p.sem("meta_landed"))
    meta = meta_dma.start(p.res[:, :, 0:META], dram["meta"], switch)
    pad = [p.memset(p.res[:, :, META + S:WIDE], 0.0, switch)]
    pad += [p.memset(x[:, :, META + S:WIDE].bitcast(F32), 0.0, switch) for x in (p.x_hi, p.x_lo)]
    edges = [p.split_scaled(p.res[:, k, 0:META], p.column("mix_norm_g_2", k), k, 0, META, [meta, switch]) for k in range(8)]
    mean, rstd, tmp, total, part = M[0], M[1], M[2], M[3], M[4]
    meta_sq = part[:, 0:8 * META].rearrange("p (k t) -> p k t", k=8)
    c = p.activation(meta_sq, p.res[:, :, 0:META], ACT.Square, [meta, switch])
    e = p.dve.do(lambda e: e.tensor_reduce(total[:, 0:META], part[:, 0:8 * META].rearrange("p (k t) -> p t k", k=8), AX.X, ALU.add), [c])
    total_ends = [e, p.memset(total[:, META + S:WIDE], 0.0, switch)]

    h_ready, x_ready = [PerPiece([None] * 2) for _ in range(8)], [PerPiece([None] * 3) for _ in range(8)]
    squares = [M[5], M[6], M[7]]
    rms_used = [switch, switch]
    totals = [None, None]

    def apply(k, i, cols, x, r, after):
        c = p.stt(x, x, p.column("ln2_g", k), r, ALU.mult, ALU.mult, after)
        c = h_ready[k][i] = p.activation(x, x, ACT.Identity, [c], bias=p.column("ln2_b", k))
        s = p.split_scaled(x, p.column("mix_norm_g_2", k), k, META + cols.start, META + cols.stop, [c, switch])
        if i == 0:
            x_ready[k][0] = [s, edges[k]]
        x_ready[k][1] = x_ready[k][2] = [s, pad]
        t = total[:, META + cols.start:META + cols.stop]
        if k == 0:
            totals[i] = p.activation(t, x, ACT.Square, [c, total_ends])
        else:
            sq = part[:, (k % 2) * 512:(k % 2) * 512 + 512]
            q = p.activation(sq, x, ACT.Square, [c, rms_used[k % 2], total_ends])
            totals[i] = rms_used[k % 2] = p.tt(t, t, sq, ALU.add, [q, totals[i]])

    layer_norm(p, [real(k) for k in range(8)], acc, summed, mean, rstd, tmp, squares, D, LN_EPS, apply, switch)
    spill = Dma(p.sp, p.sem("h0_spilled"))
    spilled = spill.start(dram["spill_2"], p.res[:, :, :], [h_ready, meta, pad])
    free = [spilled, x_ready]

    T = [p.res[:, i, :] for i in range(8)] + [work[:, i, :] for i in range(4)]
    rope_t, sig, rms = T[6], T[7], T[8]
    rope_dma = Dma(p.sp, p.sem("rope_landed"))
    rope = rope_dma.start(rope_t, dram["rope"], free)
    zeros = p.memset(u_pad[:, :, 0:CONV2 - 1], 0.0, switch)

    def rms_of(total, ready, n, out, scratch, after):
        banks = p.take_slot()
        t = p.ones_product(total, THREE, banks, ready)
        r = p.inverse_root(grid(out), grid(scratch), ps[:, banks[0]:banks[0] + 3, 0:348], n, EPS, [t, after])
        p.free(banks, r)
        return r

    mix_rms = []

    def leave(out, rows=slice(0, P)):
        def take(view, banks, tok):
            if not mix_rms:
                mix_rms.append(rms_of(total, totals, D, rms, tmp, [x_ready, p.dve.last()]))
            return p.tt(grid(out)[rows], ps[rows, banks[0]:banks[0] + 3, 0:348], grid(rms)[rows], ALU.mult, [tok, mix_rms, free])
        return take

    def w_in(cols, take):
        p.product([block_of("w_in_2", k, cols) for k in range(8)], hi, lo, THREE, x_ready, take)
        p.drain()
        return p.dve.last()

    def compressed(first, n, name):
        m = Moments(p, T[9], [T[10]], n, after=p.dve.last())
        for i in range(first, first + n):
            m.square(T[i], w_in(1024 + i * P, leave(T[i])))
        return m

    def normed(m, first, n, name):
        r = rms_of(T[9], m.token, n * P, T[11], T[10], p.dve.last())
        return [p.stt(T[i], T[i], p.column(name, i - first), T[11], ALU.mult, ALU.mult, [r]) for i in range(first, first + n)]

    kv_m = compressed(3, 2, "kv_norm_g_2")
    k_rot = T[5]

    def rotate(out, banks, tok, after):
        x = lambda a, b: ps[a:b, banks[0]:banks[0] + 3, 0:348]
        c = p.tt(grid(out)[64:96], x(96, 128), grid(rope_t)[96:128], ALU.mult, [tok, rope, after])
        d = p.tt(x(64, 96), x(64, 96), grid(rope_t)[64:96], ALU.mult, [tok, rope])
        return p.tt(grid(out)[64:96], grid(out)[64:96], x(64, 96), ALU.add, [c, d])

    def take_rotary(view, banks, tok):
        c = rotate(k_rot, banks, tok, free)
        return p.tt(k_rot[64:96, :], k_rot[64:96, :], rms[64:96, :], ALU.mult, [c, mix_rms])

    rot_ready = w_in([(64, 1664, 32), (96, 1680, 16), (112, 1664, 16)], take_rotary)
    parts_in = [None] * 5
    parts_in[3:5] = normed(kv_m, 3, 2, "kv_norm_g_2")
    q_m = compressed(0, 3, "q_norm_g_2")

    steps = []
    conv_token = [None] * 4

    def conv_step(c, j, u_ready):
        src = u_pad[:, c, j:j + WIDE]
        w = p.column("conv_w_2", j * 4 + c)
        if j == 0:
            conv_token[c] = p.ts(M[c], src, w, p.column("conv_b_2", c), ALU.mult, ALU.add, [u_ready, zeros, mix_rms, x_ready])
        else:
            conv_token[c] = p.stt(M[c], src, w, M[c], ALU.mult, ALU.add, [conv_token[c]])

    def fill(n):
        for _ in range(min(n, len(steps))):
            steps.pop(0)()

    last = [None]
    for c in range(4):
        def take_gate(view, banks, tok):
            e = p.tt(grid(sig), view, grid(rms), ALU.mult, [tok, mix_rms, free, last])
            s = p.activation(sig, sig, ACT.Sigmoid, [e])
            last[0] = p.tt(sig, sig, rms, ALU.mult, [s])
            return e

        def take_a(view, banks, tok, c=c):
            last[0] = p.tt(grid(u_pad[:, c, CONV2 - 1:]), view, grid(sig), ALU.mult, [tok, last, switch])
            return last[0]

        w_in(512 + c * P, take_gate)
        if c == 0:
            parts_in[0:3] = normed(q_m, 0, 3, "q_norm_g_2")
        w_in(c * P, take_a)
        steps += [lambda c=c, j=j, r=last[0]: conv_step(c, j, r) for j in range(CONV2)]
        fill(12)

    old = p.pe.last()
    parts = [None] * 5
    for i in (3, 4, 0, 1, 2):
        parts[i] = p.split(T[i], i, 0, WIDE, [parts_in[i], old])

    slots = [T[i] for i in (0, 1, 2, 3, 4, 7, 8, 9, 10, 11)]
    keys, q_t, v_f, v_t = slots[0:2], slots[2:4], slots[4], slots[5]
    probs, probs_t = slots[6:8], slots[8:10]
    v_meta, pt_meta = small[:, 0, :], [small[:, 1, :], small[:, 2, :]]
    start = p.everything()
    zm = p.memset(small[:, :, :], 0.0, switch)
    st = dict(scored=start, v_f=start, v_t=start, probs=[start, start], probs_t=[start, start], out=[start, start])
    SCALE = QK ** -0.5
    kv_part = lambda part: lambda k: part[:, 3 + k, :]

    def pair_keys(j):
        out = []

        def take(view, banks, tok):
            for i in range(2):
                out.append(p.copy(grid(keys[i])[0:64], ps[64 * i:64 * i + 64, banks[0]:banks[0] + 3, 0:348], [tok, st["scored"]]))
                out.append(p.dcopy(keys[i][64:96, :], k_rot[64:96, :], [rot_ready, st["scored"]]))
            return out[2]
        p.product([("w_ukv_2", k * P, P, [(0, 2 * j * P, 64), (64, (2 * j + 1) * P, 64)]) for k in range(2)],
                  kv_part(p.x_hi), kv_part(p.x_lo), THREE, parts[3:5], take)
        p.drain()
        return out

    def pair_values(j):
        out = []

        def take(view, banks, tok):
            out.append(p.copy(grid(v_f), view, [tok, st["v_f"]]))
            return out[0]
        p.product([("w_ukv_2", k * P, P, [(0, 2 * j * P + 64, 64), (64, (2 * j + 1) * P + 64, 64)]) for k in range(2)],
                  kv_part(p.x_hi), kv_part(p.x_lo), THREE, parts[3:5], take)
        p.drain()
        return out

    def turn_values(e):
        out = []
        for g in range(2):
            t = p.mm([(ps[:, 6 + g, i * P:(i + 1) * P], v_f[:, META + (4 * g + i) * P:META + (4 * g + i + 1) * P], p.ident[:, :], True, True)
                      for i in range(4)], [e, p.bank_free[6 + g]], transpose=True)
            c = p.copy(v_t[:, g * 512:(g + 1) * 512], ps[:, 6 + g, :], [t, st["v_t"]])
            p.free([6 + g], c)
            out.append(c)
        t = p.mm([(ps[0:META, 6, 0:P], v_f[:, 0:META], p.ident[:, :], True, True)], [e, p.bank_free[6]], transpose=True)
        c = p.copy(v_meta[0:META, :], ps[0:META, 6, 0:P], [t, st["v_t"], zm])
        p.free([6], c)
        st["v_f"] = t
        return out + [c]

    def queries(h, i):
        c = h * QK
        out = []

        def take(view, banks, tok):
            e = p.copy(grid(q_t[i])[0:64], ps[0:64, banks[0]:banks[0] + 3, 0:348], [tok, st["scored"]])
            out.extend([e, rotate(q_t[i], banks, tok, st["scored"])])
            return out
        p.product([("w_uq_2", k * P, P, [(0, c, 64), (64, c + 64, 32), (96, c + 80, 16), (112, c + 64, 16)]) for k in range(3)],
                  hi, lo, THREE, parts[0:3], take)
        p.drain()
        return out

    tiles = [(0, META, META)] + [(META + i * P, P, META + (i + 1) * P) for i in range(8)]
    count = [0]

    def score(i, hh, ready):
        q0, used, nk = tiles[i]
        banks = [0, 1, 2] if nk > 1024 or (2 * i + hh) % 2 == 0 else [3, 4]
        b = banks[0]
        t = p.mm([(ps[:, b + n // 512, 0:min(512, nk - n)], q_t[hh][0:QK, q0:q0 + P], keys[hh][0:QK, n:n + min(512, nk - n)], True, True)
                  for n in range(0, nk, 512)], [ready, [p.bank_free[x] for x in banks]])
        st["scored"] = t
        r = count[0] % 2
        cc = col[:, count[0] % 4, :]
        count[0] += 1
        flat = ps[:, b:b + len(banks), :].rearrange("p a b -> p (a b)")
        c = t
        if i:
            c = p.memset(flat[0:64, nk - 64:nk], -1e30, [t])
        c = p.dve.do(lambda e: e.tensor_reduce(cc[:, 0:1], flat[:, 0:nk], AX.X, ALU.max), [c, t])
        c = p.ts(cc[:, 1:2], cc[:, 0:1], -SCALE, None, ALU.mult, None, [c])
        ex = p.activation(probs[r][:, 0:nk], flat[:, 0:nk], ACT.Exp, [c, st["probs"][r]], bias=cc[:, 1:2], scale=SCALE, accum=cc[:, 2:3])
        p.free(banks, ex)
        inv = p.dve.do(lambda e: e.reciprocal(cc[:, 3:4], cc[:, 2:3]), [ex])
        return dict(i=i, hh=hh, r=r, cc=cc, ex=ex, inv=inv)

    def turn(s):
        pr, pt, r = probs[s["r"]], probs_t[s["r"]], s["r"]
        n_full = (tiles[s["i"]][2] - META) // P
        out = []
        for g in range(0, n_full, 4):
            bank = 6 + (g // 4) % 2
            n = min(4, n_full - g)
            t = p.mm([(ps[:, bank, x * P:(x + 1) * P], pr[:, META + (g + x) * P:META + (g + x + 1) * P], p.ident[:, :], True, True)
                      for x in range(n)], [s["ex"], p.bank_free[bank]], transpose=True)
            e = (p.copy if g == 0 else p.dcopy)(pt[:, g * P:(g + n) * P], ps[:, bank, 0:n * P], [t, st["probs_t"][r]])
            p.free([bank], e)
            out.append(e)
        t = p.mm([(ps[0:META, 7, 0:P], pr[:, 0:META], p.ident[:, :], True, True)], [s["ex"], p.bank_free[7]], transpose=True)
        e = p.dcopy(pt_meta[r][0:META, :], ps[0:META, 7, 0:P], [t, st["probs_t"][r], zm])
        p.free([7], e)
        st["probs"][r] = t
        s["turned"] = out + [e]

    def weigh(j, s, ready):
        i, hh, r = s["i"], s["hh"], s["r"]
        q0, used, nk = tiles[i]
        pt, n_full = probs_t[r], (nk - META) // P
        v = slice(64 * hh, 64 * hh + 64)
        o = ps[:, 5, 0:64]
        t = p.mm([(o, pt_meta[r], v_meta[:, v], True, n_full == 0)] +
                 [(o, pt[:, x * P:(x + 1) * P], v_t[:, x * P + v.start:x * P + v.stop], False, x == n_full - 1) for x in range(n_full)],
                 [s["turned"], ready, p.bank_free[5]])
        st["probs_t"][r] = st["v_t"] = t
        c = p.ts(pair_out[:, i % 2, v], o, s["cc"][:, 3:4], None, ALU.mult, None, [t, s["inv"], st["out"][i % 2]])
        p.free([5], c)
        halves.append(c)

    def turn_back(j, s):
        q0, used, nk = tiles[s["i"]]
        back = ps[:, 5, P:2 * P]
        t = p.mm([(back, pair_out[:, s["i"] % 2, :], p.ident[:, :], True, True)], [halves[-2:], p.bank_free[5]], transpose=True)
        st["out"][s["i"] % 2] = t
        e = p.copy(mix[:, 4 + j, q0:q0 + used], back[:, 0:used], [t, x_ready, mix_rms])
        p.free([5], e)
        o_ready[j].append(e)

    A = [u_pad[:, c, 0:WIDE] for c in range(4)]
    u = dict()

    def ones_of(total, ready):
        banks = p.take_slot()
        return banks, p.ones_product(total, THREE, banks, ready)

    def after_conv():
        c = p.tt(A[0], M[0], M[1], ALU.add, conv_token)
        c = p.tt(A[0], A[0], M[2], ALU.add, [c])
        u["c"] = p.tt(A[0], A[0], M[3], ALU.add, [c])

    def u_mean():
        banks, t = ones_of(A[0], u["c"])
        m = p.activation(grid(A[1]), ps[:, banks[0]:banks[0] + 3, 0:348], ACT.Copy, [t, u["c"]], scale=1.0 / (4 * P))
        p.free(banks, m)
        u["m"] = [m, t]
        u["moments"] = Moments(p, A[0], [A[2]], 4, after=[t, m, u["c"]])

    def u_centre(c):
        t = p.tt(M[c], M[c], A[1], ALU.subtract, [u["m"], conv_token])
        u["moments"].square(M[c], t)

    def u_root():
        u["r"] = rms_of(A[0], u["moments"].token, 4 * P, A[1], A[2], p.dve.last())
        u["moments"] = Moments(p, A[0], [A[2]], 4, after=[u["r"]])

    def u_silu(c):
        t = p.tt(M[c], M[c], A[1], ALU.mult, [u["r"]])
        t = p.activation(M[c], M[c], ACT.Silu, [t], scale=p.column("conv_ln_g_2", c), bias=p.column("conv_ln_b_2", c))
        u["moments"].square(M[c], t)

    def u_rms():
        u["r"] = rms_of(A[0], u["moments"].token, 4 * P, A[1], A[2], p.dve.last())
        u["c"] = [p.stt(M[c], M[c], p.column("conv_out_g_2", c), A[1], ALU.mult, ALU.mult, [u["r"]]) for c in range(4)]

    steps += [after_conv, u_mean] + [lambda c=c: u_centre(c) for c in range(4)] + [u_root] + [lambda c=c: u_silu(c) for c in range(4)] + [u_rms]

    halves, o_ready = [], [[] for _ in range(4)]
    pads = p.memset(mix[:, 4:8, META + S:WIDE], 0.0, [x_ready, mix_rms])
    o_moments = None
    ready = [pair_keys(0), queries(0, 0), queries(1, 1)]
    values = turn_values(pair_values(0))
    for j in range(H2 // 2):
        items = [(i, hh) for i in range(9) for hh in range(2)]
        previous, current = None, score(0, 0, ready)
        for n, (i, hh) in enumerate(items):
            following = score(*items[n + 1], ready) if n + 1 < len(items) else None
            if following is None and j < 3:
                ready = [pair_keys(j + 1), queries(2 * j + 2, 0), queries(2 * j + 3, 1)]
                values_in = pair_values(j + 1)
            if previous:
                weigh(j, previous, values)
            turn(current)
            if previous and previous["hh"]:
                turn_back(j, previous)
            fill(1 if i < 3 else 2)
            previous, current = current, following
        weigh(j, previous, values)
        turn_back(j, previous)
        if j < 3:
            values = turn_values(values_in)
        if j == 2:
            fill(len(steps))
            old = p.pe.last()
            m_ready = [p.split(M[k], k, 0, WIDE, [u["c"], old]) for k in range(4)]
            o_moments = Moments(p, A[3], [A[2]], 4, after=p.dve.last())
            for k in range(3):
                o_moments.square(M[4 + k], [o_ready[k], pads])
                m_ready.append(p.split_scaled(M[4 + k], p.column("attn_out_g_2", k), 4 + k, 0, WIDE, [o_ready[k], pads, old]))
    m_ready.append(p.split_scaled(M[7], p.column("attn_out_g_2", 3), 7, 0, WIDE, [o_ready[3], pads, old]))
    o_moments.square(M[7], [o_ready[3], pads])

    done = p.everything()
    back = [Dma(p.sp, p.sem(f"h0_back{i}")) for i in range(4)]
    h_back = [back[i].start(p.res[:, 2 * i:2 * i + 2, :], dram["spill_2"][:, 2 * i:2 * i + 2, :], [done, spilled]) for i in range(4)]
    o_rms = []
    h1, turn_tmp = [], A[2]
    h_moments = Moments(p, T[8], [T[9]], 8, after=done)
    for m in range(8):
        def take_u(view, banks, tok, m=m):
            h1.append(p.tt(grid(p.res[:, m, :]), grid(p.res[:, m, :]), view, ALU.add, [tok, h_back[m // 2]]))
            return h1[m]

        def take_o(view, banks, tok, m=m):
            if m == 0:
                o_rms.append(rms_of(A[3], o_moments.token, 4 * P, A[0], A[1], done))
            e = p.tt(grid(turn_tmp), view, grid(A[0]), ALU.mult, [tok, o_rms, h1[m], p.dve.last()])
            h1[m] = p.tt(p.res[:, m, :], p.res[:, m, :], turn_tmp, ALU.add, [e])
            h_moments.square(p.res[:, m, :], h1[m])
            return e
        for first, take in ((0, take_u), (4, take_o)):
            p.product([block_of("w_out_2", first + k, m * P) for k in range(4)],
                      lambda k, first=first: p.x_hi[:, first + k, :], lambda k, first=first: p.x_lo[:, first + k, :],
                      THREE, m_ready[first:first + 4], take)
            p.drain()
    old = p.pe.last()
    n_ready = [p.split_scaled(p.res[:, k, :], p.column("ffn_norm_g_2", k), k, 0, WIDE, [h1[k], old]) for k in range(8)]
    banks = p.take_slot()
    moments_ready = h_moments.token
    t = p.ones_product(T[8], THREE, banks, moments_ready)
    sums = ps[:, banks[0]:banks[0] + 3, 0:348]
    switch = p.everything()
    ctx.close()

    ctx = ExitStack()
    RING = 5
    h_hi = p.sbuf("h2_hi", [P, RING, S], F32R, ctx=ctx)
    h_lo = p.sbuf("h2_lo", [P, RING, S], F32R, ctx=ctx)
    up = p.sbuf("up_2", [P, 2, S + 2], ctx=ctx)
    conv = p.sbuf("up_conv_2", [P, 2, S], ctx=ctx)
    ffn_rms = p.sbuf("ffn_rms", [P, WIDE], ctx=ctx)
    scratch = up[:, :, :].rearrange("p a b -> p (a b)")[:, 0:WIDE]
    ffn_rms_ready = p.inverse_root(grid(ffn_rms[:, :]), grid(scratch), sums, D, EPS, [t, switch])
    p.free(banks, ffn_rms_ready)
    gains = p.sbuf("gains_3", [P, 8], ctx=ctx)
    h_used, h_ready = [switch] * RING, {}
    up_free, conv_free = [switch] * 2, [switch] * 2
    acc = list(h1)
    tri = lambda t: t.rearrange("p (a b) -> p a b", a=3)
    gain_ready = p.tt(gains[:, :], p.vec[:, VCOL["final_norm_g_2"]:VCOL["final_norm_g_2"] + 8],
                      p.vec[:, VCOL["pre_norm_g_3"]:VCOL["pre_norm_g_3"] + 8], ALU.mult, switch)

    def hidden(j):
        got = []
        for i in range(2):
            def take(view, banks, tok, i=i):
                e = p.tt(tri(up[:, i, :]), view, tri(ffn_rms[:, META - 2:META + S]), ALU.mult, [tok, up_free[i], ffn_rms_ready])
                chunk = i * FF2 + j
                w = lambda tap: p.column("ffn_conv_w_2", tap * 44 + chunk)
                c = p.ts(conv[:, i, :], up[:, i, 0:S], w(0), p.column("ffn_conv_b_2", chunk), ALU.mult, ALU.add, [e, conv_free[i]])
                c = p.stt(conv[:, i, :], up[:, i, 1:S + 1], w(1), conv[:, i, :], ALU.mult, ALU.add, [c])
                c = p.stt(conv[:, i, :], up[:, i, 2:S + 2], w(2), conv[:, i, :], ALU.mult, ALU.add, [c])
                up_free[i] = c
                if i == 0:
                    c = p.activation(conv[:, 0, :], conv[:, 0, :], ACT.Silu, [c])
                got.append(c)
                return e
            p.product([block_of("w_ffn_up_2", k, i * FF2 * P + j * P) for k in range(8)], hi, lo, FFN2, n_ready, take)
            p.drain()
        c = p.tt(conv[:, 0, :], conv[:, 0, :], conv[:, 1, :], ALU.mult, got)
        conv_free[1] = c
        c = p.split(conv[:, 0, :], j % RING, 0, S, [c, h_used[j % RING]], h_hi, h_lo)
        h_ready[j] = conv_free[0] = c

    m1, m2 = None, None
    x_ready = [None] * 8

    def project(ks, last):
        for m in range(8):
            def take(view, banks, tok, m=m):
                c = acc[m] = p.tt(real(m), real(m), view, ALU.add, [tok, acc[m], n_ready[m]])
                if last:
                    m1.square(real(m), c)
                    m2.square(real(m), c, scale=p.column("final_norm_g_2", m))
                    x_ready[m] = p.split_scaled(real(m), gains[:, m:m + 1], m, 0, S, [c, old, gain_ready])
                return c
            p.product([block_of("w_ffn_down_2", k, m * P) for k in ks],
                      lambda i: h_hi[:, ks[i] % RING, :], lambda i: h_lo[:, ks[i] % RING, :],
                      TWO, [h_ready[k] for k in ks], take)
            p.drain()
        for k in ks:
            h_used[k % RING] = p.pe.last()

    groups = [list(range(0, 2))] + [list(range(g, g + 4)) for g in range(2, FF2, 4)]
    done_to = 0
    for ks in groups:
        ahead = min(ks[-1] + 2, FF2)
        for j in range(done_to, ahead):
            hidden(j)
        done_to = ahead
        last = ks is groups[-1]
        if last:
            old = p.pe.last()
            idle = p.dve.last()
            m1 = Moments(p, conv[:, 0, :], [up[:, 0, 0:S]], 8, after=idle)
            m2 = Moments(p, conv[:, 1, :], [up[:, 1, 0:S]], 8, after=idle)
        project(ks, last)
    moments = [p.ones_product(conv[:, 0, :], TWO, [4, 5], m1.token), p.ones_product(conv[:, 1, :], TWO, [6, 7], m2.token)]
    switch = p.everything()
    ctx.close()
    return acc, x_ready, moments, switch


def layer_3(p, acc, x_ready, moments, switch, out):
    nc, dram, ps = p.nc, p.dram, p.ps
    hi, lo = p.x_parts()
    real = lambda k: p.res[:, k, META:META + S]
    grid = lambda t: t.rearrange("p (a b) -> p a b", a=2)
    chunks = lambda t: t.rearrange("p (c l) -> p c l", l=CHUNK)
    ctx = ExitStack()
    mix = p.sbuf("mix_3", [P, 8, S], ctx=ctx)
    work = p.sbuf("work_3", [P, 7, S], ctx=ctx)
    w_a2 = p.sbuf("w_a2", [16, 4, P], ctx=ctx)
    pair = p.sbuf("pair_scores", [P, 2, P], ctx=ctx)
    ends = p.sbuf("chunk_decay", [P, 16], ctx=ctx)
    M = [mix[:, i, :] for i in range(8)]
    W = [work[:, i, :] for i in range(7)]

    rms, tmp, rms2 = W[0], W[1], W[2]
    first = p.inverse_root(grid(rms), grid(tmp), ps[:, 4:6, :], D, EPS, [moments, switch])
    p.free([4, 5], first)
    c = p.tt(tmp, rms, rms, ALU.mult, [first])
    c = p.tt(grid(tmp), ps[:, 6:8, :], grid(tmp), ALU.mult, [c, moments])
    p.free([6, 7], c)
    c = p.inverse_root(rms2, W[3], tmp, D, EPS, [c, switch])
    scale_ready = p.tt(rms2, rms2, rms, ALU.mult, [c])
    x_in = [p.stt(real(k), real(k), p.column("final_norm_g_2", k), rms, ALU.mult, ALU.mult, [first, x_ready[k]]) for k in range(8)]
    spill = Dma(p.sp, p.sem("x3_spilled"))
    spilled = spill.start(dram["spill_3"][:, :, 0:S], p.res[:, :, META:META + S], x_in)
    w_a2_dma = Dma(p.sp, p.sem("w_a2_landed"))
    w_a2_ready = w_a2_dma.start(w_a2[:, :, :], dram["w_a2"].rearrange("r (h c) -> r h c", h=4), switch)
    free = [spilled, x_in, switch]
    T = [p.res[:, i, 0:S] for i in range(8)]

    def w_in(col, take, n=P):
        p.product([block_of("w_in_3", k, col if n == P else [(0, col, n)]) for k in range(8)], hi, lo, TWO, x_ready, take)

    def scaled(out, func, after, told):
        def take(view, banks, tok):
            e = p.tt(grid(out), view, grid(rms2), ALU.mult, [tok, scale_ready, after])
            told(p.activation(out, out, func, [e]) if func else e)
            return e
        return take

    w_s, b_s = T[6].rearrange("p (g t) -> p g t", g=8), T[7]
    s_dma = Dma(p.sp, p.sem("w_s_landed"))
    s_dma.start(w_s, dram["a_w_s"], free)
    landed = s_dma.start(b_s, dram["a_b_s"].broadcast_to([P, 8 * P]), free)
    total, mean, root = W[3], W[4], T[0]
    v_ready, summed = {}, [None]

    def told_v(g):
        def told(tok):
            v_ready[g] = tok
            if g:
                summed[0] = p.tt(total, M[0] if g == 1 else total, M[g], ALU.add, [v_ready[0], tok, summed[0], scale_ready])
        return told

    for g in range(8):
        w_in(OFF3["v"] + g * P, scaled(M[g], ACT.Gelu, switch, told_v(g)))
    p.drain()
    masked = p.tt(w_s, w_s, p.upper[:, :].unsqueeze(1).broadcast_to([P, 8, P]), ALU.mult, [landed, p.const])
    u_g, s_g, u_tok, s_tok, lr_tok = [W[5], W[6]], [T[1], T[2]], {}, {}, []
    gates_used = [free, free]

    def gate_products(g):
        r = g % 2
        w_in(OFF3["u"] + g * P, scaled(u_g[r], ACT.Gelu, gates_used[r], lambda t: u_tok.update({g: t})))
        w_in(OFF3["gate"] + g * P, scaled(s_g[r], ACT.Silu, gates_used[r], lambda t: s_tok.update({g: t})))

    lr = T[5]
    w_in(OFF3["lr"], lambda view, banks, tok: lr_tok.append(p.tt(
        lr[0:16, :].rearrange("p (a b) -> p a b", a=2), ps[0:16, banks[0]:banks[0] + 2, :], grid(rms2[:, :])[0:16], ALU.mult, [tok, scale_ready, free])) or lr_tok[0], 16)
    gate_products(0)
    gate_products(1)
    s = p.ones_product(total, TWO, [4, 5], summed[0])
    p.pump(4)
    v_done = [PerPiece([None] * 2) for _ in range(8)]

    def apply(g, i, cols, x, r, after):
        c = p.stt(x, x, p.column("a_ln_g_3", g), r, ALU.mult, ALU.mult, after)
        v_done[g][i] = p.activation(x, x, ACT.Identity, [c], bias=p.column("a_ln_b_3", g))

    layer_norm(p, M, v_ready, s, mean, root, W[1], [T[3], T[4]], D, EPS, apply, [free, p.dve.last()], fill=2)
    p.drain()
    v_t, sp_t = [W[3], W[4]], T[3]
    vt_used, spilled_a = [p.everything()] * 2, []
    spill_a = [Dma(p.sp, p.sem(f"a_spilled{i}")) for i in range(2)]
    for g in range(8):
        r = g % 2
        vt = v_t[r]
        t_ready = []
        for half in range(2):
            t = p.mm([(ps[:, 6 + half, i * P:(i + 1) * P], M[g][:, (4 * half + i) * P:(4 * half + i + 1) * P], p.ident[:, :], True, True)
                      for i in range(4)], [v_done[g][half], p.bank_free[6 + half]], transpose=True)
            e = p.copy(vt[:, half * 512:(half + 1) * 512], ps[:, 6 + half, :], [t, vt_used[r]])
            p.free([6 + half], e)
            t_ready.append(e)
        p.pump(4)
        t = p.mm([(ps[:, 4 + n // 4, (n % 4) * P:(n % 4 + 1) * P], vt[:, n * P:(n + 1) * P], w_s[:, g, :], True, True) for n in range(8)],
                 [t_ready, masked, p.bank_free[4], p.bank_free[5]])
        vt_used[r] = t
        bias = b_s[:, g * P:(g + 1) * P].unsqueeze(1).broadcast_to([P, 8, P])
        c = p.tt(sp_t.rearrange("p (n t) -> p n t", n=8), ps[:, 4:6, :].rearrange("p a (n t) -> p (a n) t", t=P), bias, ALU.add, [t, landed, p.dve.last(), vt_used])
        p.free([4, 5], c)
        c = p.tt(u_g[r], u_g[r], sp_t, ALU.mult, [c, u_tok[g]])
        c = p.tt(M[g], u_g[r], s_g[r], ALU.mult, [c, s_tok[g], t_ready])
        gates_used[r] = c
        spilled_a.append(spill_a[r].start(dram["spill_a"][:, g, 0:S], M[g], [c, spilled_a[g - 2] if g >= 2 else None]))
        p.drain()
        if g + 2 < 8:
            gate_products(g + 2)

    q_in, k_in = M[6], M[7]
    qb, kd, reset, qe, ke, kd_tok = T[0], T[1], T[2], T[3], T[4], T[6]
    v_f, v0, v1, b_t, e_t, g0, g1, states = T[7], W[0], W[1], W[3], W[4], W[5], W[6], None
    states = p.sbuf("states", [P, 4, 256], ctx=ctx)
    start = p.everything()
    z = [p.memset(pair[:, :, :], 0.0, switch)]
    c = p.memset(reset, 1.0, [start])
    z.append(p.memset(chunks(reset)[:, :, 0:1], 0.0, [c]))
    SCALE = P ** -0.5
    TAU = 1.0 / 16.0
    b_ready = []
    st = dict(q=[start, spilled_a], v_f=start, v0=start, v1=start, done=start, gates=start)
    got = {}

    def tell(name):
        return lambda tok: got.update({name: tok})

    def q_and_k(h):
        w_in(OFF3["q"] + h * P, scaled(q_in, None, st["q"], tell(("q", h))))
        w_in(OFF3["k"] + h * P, scaled(k_in, None, st["q"], tell(("k", h))))

    def v_product(h, i):
        w_in(OFF3["bv"] + (2 * h + i) * P, scaled(v_f, None, st["v_f"], tell(("v", h, i))))

    def gate_product(h, i, dst):
        w_in(OFF3["bgate"] + (2 * h + i) * P, scaled(dst, ACT.Silu, st["gates"], tell(("g", h, i))))

    def turn_v(h, i, dst):
        out = []
        for half in range(2):
            t = p.mm([(ps[:, 6 + half, n * P:(n + 1) * P], v_f[:, (4 * half + n) * P:(4 * half + n + 1) * P], p.ident[:, :], True, True)
                      for n in range(4)], [got["v", h, i], p.bank_free[6 + half]], transpose=True)
            c = p.copy(dst[:, half * 512:(half + 1) * 512], ps[:, 6 + half, :], [t, st["done"]])
            p.free([6 + half], c)
            out.append(c)
        st["v_f"] = t
        return out

    q_and_k(0)
    v_product(0, 0)
    p.drain()
    for h in range(H3):
        done = st["done"]
        ready = turn_v(h, 0, v0)
        v_product(h, 1)
        gate_product(h, 0, g0)
        gate_product(h, 1, g1)
        t = p.mm([(ps[:, 4 + i, :], w_a2[:, h, :], lr[0:16, i * 512:(i + 1) * 512], True, True) for i in range(2)],
                 [lr_tok, w_a2_ready, p.bank_free[4], p.bank_free[5]])
        x = p.ts(qe, ps[:, 4:6, :], p.column("b_a2_3", h), None, ALU.add, None, [t, done])
        p.free([4, 5], x)
        c = p.stt(e_t, qe, -1.0, qe, ALU.mult, ALU.max, [x, done])
        c = p.activation(e_t, e_t, ACT.Exp, [c], scale=-1.0)
        c = p.activation(e_t, e_t, ACT.Ln, [c], bias=p.tiny[:, 2:3])
        c = p.stt(e_t, qe, 0.0, e_t, ALU.min, ALU.subtract, [c])
        b = p.dve.do(lambda e: e.tensor_tensor_scan(b_t, reset, e_t, 0.0, ALU.mult, ALU.add), [c, z, done])
        ref = chunks(b_t)[:, :, CHUNK // 2 - 1:CHUNK // 2].broadcast_to([P, 16, CHUNK])
        end = chunks(b_t)[:, :, CHUNK - 1:CHUNK]
        decay = p.activation(ends[:, :], end.rearrange("p c l -> p (c l)"), ACT.Exp, [b, done], scale=TAU)
        d = p.tt(chunks(kd), chunks(b_t), ref, ALU.subtract, [b, done])
        c1 = p.activation(e_t, kd, ACT.Exp, [d], scale=TAU)
        c2 = p.activation(ke, kd, ACT.Exp, [d, done], scale=-TAU)
        c3 = p.activation(qb, b_t, ACT.Exp, [b, done], scale=TAU)
        d = p.tt(chunks(kd), end.broadcast_to([P, 16, CHUNK]), chunks(b_t), ALU.subtract, [c1, c2])
        c4 = p.activation(kd, kd, ACT.Exp, [d], scale=TAU)
        r1 = p.stt(qe, q_in, SCALE, e_t, ALU.mult, ALU.mult, [c1, got["q", h]])
        r2 = p.tt(ke, ke, k_in, ALU.mult, [c2, got["k", h]])
        r3 = p.stt(qb, q_in, SCALE, qb, ALU.mult, ALU.mult, [c3])
        r4 = p.tt(kd, kd, k_in, ALU.mult, [c4])
        st["q"] = r4
        p.drain()
        ready += [r1, r2, r3] + turn_v(h, 1, v1)
        for half in range(2):
            t = p.mm([(ps[:, 6 + half, n * P:(n + 1) * P], kd[:, (4 * half + n) * P:(4 * half + n + 1) * P], p.ident[:, :], True, True)
                      for n in range(4)], [r4, p.bank_free[6 + half]], transpose=True)
            c = p.copy(kd_tok[:, half * 512:(half + 1) * 512], ps[:, 6 + half, :], [t, done])
            p.free([6 + half], c)
            ready.append(c)
        if h + 1 < H3:
            q_and_k(h + 1)
            v_product(h + 1, 0)
        else:
            old = p.pe.last()
            operand = [p.split(M[k], k, 0, S, [b_ready[k], old]) for k in range(6)]
        state = lambda c: states[:, c % 4, :]
        s_ready, s_used, pair_used, o_last = {}, {}, [done, done], []

        def update(c):
            n, rows = c // 2, slice(64 * (c % 2), 64 * (c % 2) + 64)
            t = p.mm([(ps[:, 7, i * P:(i + 1) * P], kd_tok[rows, n * P:(n + 1) * P], v[rows, n * P:(n + 1) * P], True, True)
                      for i, v in enumerate((v0, v1))], [ready, p.bank_free[7]])
            if c == 0:
                s = p.dcopy(state(1), ps[:, 7, 0:256], [t, done])
            else:
                s = p.stt(state(c + 1), state(c), ends[:, c:c + 1], ps[:, 7, 0:256], ALU.mult, ALU.add,
                          [t, s_ready[c], decay, s_used.get(c - 3)])
            p.free([7], s)
            s_ready[c + 1] = s

        def masked_scores(n):
            bank = 4 + n % 2
            cols = slice(n * P, (n + 1) * P)
            t = p.mm([(ps[:, bank, 0:P], ke[:, cols], qe[:, cols], True, True)], [ready, p.bank_free[bank]])
            tri = pair[:, n % 2, :]
            c1 = p.tt(tri[0:64, 0:64], ps[0:64, bank, 0:64], p.upper[0:64, 0:64], ALU.mult, [t, z, pair_used[n % 2]])
            c2 = p.tt(tri[64:128, 64:128], ps[64:128, bank, 64:128], p.upper[64:128, 64:128], ALU.mult, [t, z])
            p.free([bank], c2)
            return [c1, c2]

        update(0)
        following = masked_scores(0)
        p.pump(3)
        for n in range(8):
            cols = slice(n * P, (n + 1) * P)
            tri = pair[:, n % 2, :]
            now = following
            if n < 7:
                update(2 * n + 1)
                following = masked_scores(n + 1)
            products = []
            for i, v in enumerate((v0, v1)):
                o = i * P
                products.append((ps[:, 6, o:o + P], v[:, cols], tri, True, False))
                if n:
                    products.append((ps[:, 6, o:o + 64], state(2 * n)[:, o:o + P], qb[:, n * P:n * P + 64], False, False))
                products.append((ps[:, 6, o + 64:o + P], state(2 * n + 1)[:, o:o + P], qb[:, n * P + 64:(n + 1) * P], False, True))
            t = p.mm(products, [now, s_ready.get(2 * n), s_ready[2 * n + 1], p.bank_free[6]])
            pair_used[n % 2] = s_used[2 * n] = s_used[2 * n + 1] = t
            e = p.copy(mix[:, 2 * h:2 * h + 2, cols], ps[:, 6, 0:256].rearrange("p (i t) -> p i t", i=2), [t, spilled_a, st["q"]])
            p.free([6], e)
            o_last.append(e)
            if n < 7:
                update(2 * n + 2)
            p.pump(3)
        pe_done = p.pe.last()
        rs, _ = p.norm([M[2 * h], M[2 * h + 1]], [o_last, o_last], TWO, 256, EPS, (b_t, e_t, qe), (ke, kd_tok), banks=(4, 5), after=pe_done, fill=10)
        for i, g in enumerate((g0, g1)):
            c = p.stt(M[2 * h + i], M[2 * h + i], p.column("b_norm_g_3", 2 * h + i), b_t, ALU.mult, ALU.mult, [rs])
            c = p.tt(M[2 * h + i], M[2 * h + i], g, ALU.mult, [c, got["g", h, i]])
            b_ready.append(c)
        p.drain()
        st["gates"] = c
        st["done"] = [c, p.pe.last(), p.act.last()]

    operand += [p.split(M[k], k, 0, S, [b_ready[k], old]) for k in (6, 7)]
    done = p.everything()
    a_back = [Dma(p.sp, p.sem(f"a_back{i}")) for i in range(4)]
    a_landed = [a_back[i].start(p.res[:, 2 * i:2 * i + 2, 0:S], dram["spill_a"][:, 2 * i:2 * i + 2, 0:S], [done, spilled_a]) for i in range(4)]
    switch = p.everything()
    ctx.close()
    ctx = ExitStack()
    a_hi = p.sbuf("a_hi", [P, 8, S], F32R, ctx=ctx)
    a_lo = p.sbuf("a_lo", [P, 8, S], F32R, ctx=ctx)
    operand += [p.split(p.res[:, k, 0:S], k, 0, S, [a_landed[k // 2], switch], a_hi, a_lo) for k in range(8)]
    y = [p.res[:, k, 0:S] for k in range(8)]
    ready = []
    for m in range(8):
        def take(view, banks, tok, m=m):
            ready.append(p.copy(grid(y[m]), view, [tok, operand[8 + m]]))
            return ready[m]
        p.product([block_of("w_out_3", (8 + k) % 16, m * P) for k in range(16)],
                  lambda k: (p.x_hi if k < 8 else a_hi)[:, k % 8, :], lambda k: (p.x_lo if k < 8 else a_lo)[:, k % 8, :],
                  TWO, operand, take)
        p.drain()
    switch = p.everything()
    ctx.close()
    ctx = ExitStack()
    x3 = p.sbuf("x3_again", [P, 8, S], ctx=ctx)
    scratch = p.sbuf("last_scratch", [P, 5, S], ctx=ctx)
    back = [Dma(p.sp, p.sem(f"x3_back{i}")) for i in range(4)]
    landed = [back[i].start(x3[:, 2 * i:2 * i + 2, :], dram["spill_3"][:, 2 * i:2 * i + 2, 0:S], [switch, spilled]) for i in range(4)]
    sc = [scratch[:, i, :] for i in range(5)]
    rs, _ = p.norm(y, ready, TWO, D, EPS, sc[0:3], sc[3:5], banks=(4, 5), after=switch)
    stores = [Dma(p.sp, p.sem(f"stored{k}")) for k in range(4)]
    tokens = []
    for k in range(8):
        c = p.stt(y[k], y[k], p.column("post_norm_g_3", k), sc[0], ALU.mult, ALU.mult, [rs])
        c = p.tt(y[k], y[k], x3[:, k, :], ALU.add, [c, landed[k // 2]])
        tokens.append(stores[k % 4].start(out[k], y[k], [c, tokens[k - 4] if k >= 4 else None]))
    p.sp.wait(tokens)
    ctx.close()


def run_layers(p, out):
    result = layer_1(p)
    result = layer_2(p, *result)
    layer_3(p, *result, out)
    assert len(p.blocks) == N_BLOCKS and not p.jobs, (len(p.blocks), N_BLOCKS)


def build(nc, dram, out):
    ctx = ExitStack()
    with ctx:
        p = Program(nc, ctx, dram)
        run_layers(p, out)
        with nc.Block() as block:
            @block.sync
            def _(e):
                p.sp.emit(e)

            @block.tensor
            def _(e):
                p.pe.emit(e)

            @block.vector
            def _(e):
                p.dve.emit(e)

            @block.scalar
            def _(e):
                p.act.emit(e)

            @block.gpsimd
            def _(e):
                p.pool.emit(e)
    return p.blocks


def weight_array(blocks, inputs):
    w = np.zeros((N_TILES, P, BLOCKS, P), np.float32)
    for i, (name, row, rows, cols) in enumerate(blocks):
        src = inputs[name][0]
        for to, start, n in cols:
            w[i // BLOCKS, 0:rows, i % BLOCKS, to:to + n] = src[row:row + rows, start:start + n]
    return w


def constant_arrays():
    head_row = np.zeros((H1, H1, P), np.float32)
    head_row[np.arange(H1), np.arange(H1)] = 1.0
    fix = np.ones((P, 4, 16), np.float32)
    for g in range(4):
        fix[:, g] = (2 << g) / np.minimum(np.arange(1, 17), 2 << g)
    freq = (np.float32(1.0) / np.float32(10000.0) ** (np.arange(0, ROPE, 2, dtype=np.float32) / np.float32(ROPE))).astype(np.float32)
    angle = (np.arange(WIDE, dtype=np.float32)[None, :] * freq[:, None]).astype(np.float32)
    rope = np.zeros((P, WIDE), np.float32)
    rope[64:80] = rope[80:96] = np.cos(angle)
    rope[96:112], rope[112:128] = -np.sin(angle), np.sin(angle)
    return {"identity": np.eye(P, dtype=np.float32), "upper": np.triu(np.ones((P, P), np.float32)),
            "head_row": head_row, "pool_fix": fix, "rope": rope}


def kernel(**inputs):
    import concourse.bacc as bacc
    from concourse.bass_utils import run_bass_kernel_spmd

    inputs = {k: np.asarray(v) for k, v in inputs.items()}
    nc = bacc.Bacc("TRN2", target_bir_lowering=False, num_devices=1)
    vectors = np.concatenate([inputs[name].reshape(-1, P) for name, _ in VECTORS]).T
    gate_bias = np.zeros((P, 1), np.float32)
    gate_bias[0:4, 0], gate_bias[32:36, 0] = inputs["b_gate"][0, :4], inputs["b_gate"][0, 4:]
    arrays = {
        "x": inputs["x"][0].T.reshape(DC, P, S),
        "vectors": vectors,
        "gate_bias": gate_bias,
        "w_pool": inputs["w_pool"][0].transpose(1, 0, 2),
        "meta": inputs["meta_tokens_2"].T.reshape(DC, P, META).transpose(1, 0, 2),
        "w_a2": inputs["w_a2_3"][0],
        "a_w_s": inputs["a_w_s_3"][0].transpose(2, 0, 1),
        "a_b_s": inputs["a_b_s_3"][0].reshape(1, 8 * P),
        **constant_arrays(),
    }
    arrays = {k: np.ascontiguousarray(v) for k, v in arrays.items()}
    dram = {k: nc.dram_tensor(f"{k}_dram", v.shape, mybir.dt.from_np(v.dtype), kind="ExternalInput").ap()
            for k, v in arrays.items()}
    dram["w"] = nc.dram_tensor("w_dram", (N_TILES, P, BLOCKS, P), F32, kind="ExternalInput").ap()
    for name in ("spill_2", "spill_3", "spill_a"):
        dram[name] = nc.dram_tensor(name, (P, DC, WIDE), F32).ap()
    out = nc.dram_tensor("out_dram", (DC, P, S), F32, kind="ExternalOutput").ap()
    blocks = build(nc, dram, out)
    arrays["w"] = weight_array(blocks, inputs)
    r = run_bass_kernel_spmd(nc, [{f"{k}_dram": v for k, v in arrays.items()}], core_ids=[0])
    return np.ascontiguousarray(r.results[0]["out_dram"].reshape(D, S).T)[None]
```

```python
from contextlib import ExitStack

import numpy as np

import concourse.bass as bass
from concourse import mybir

P = 128
S = 1024
D = 1024
DC = D // P
META = 16
WIDE = 1044
F32, F32R = mybir.dt.float32, mybir.dt.float32r
ACT, ALU, AX = mybir.ActivationFunctionType, mybir.AluOpType, mybir.AxisListType
ALPHA = 2.0 ** 0.25
LN_EPS, EPS = 1e-5, 1e-6
BLOCKS = 8

TWO = [(0, 512), (512, 512)]
THREE = [(0, 348), (348, 348), (696, 348)]
FFN2 = [(14, 342), (356, 342), (698, 342)]

H1, FF1 = 4, 32
OFF_G, OFF_O, OFF_P = 1536, 1544, 2056
CONV1 = 4
H2, QK, NOPE, ROPE = 8, 96, 64, 32
CONV2, FF2, CONV3 = 31, 22, 3
H3, CHUNK = 4, 64
OFF3 = dict(u=0, v=1024, gate=2048, q=3072, k=3584, bv=4096, bgate=5120, lr=6144)

N_BLOCKS = (
    8 * (1 + 4 * 4 + 4) + 2 * 8 * 8 + 2 * 8 * 32 + 2 * 8 * 4
    + 8 * 14 + 4 * 2 * 2 + 8 * 3 + 8 * 8 + 3 * 8 * 22
    + 8 * (8 * 3 + 1 + 4 * 6) + 2 * 16 * 8
)
N_TILES = -(-N_BLOCKS // BLOCKS)

VECTORS = [
    ("w_conv", CONV1 * 8), ("hn_g", 4), ("pool_scale", 4), ("ln1_g", 8), ("ln1_b", 8), ("ln2_g", 8), ("ln2_b", 8),
    ("mix_norm_g_2", 8), ("q_norm_g_2", 3), ("kv_norm_g_2", 2), ("conv_w_2", CONV2 * 4), ("conv_b_2", 4),
    ("conv_ln_g_2", 4), ("conv_ln_b_2", 4), ("conv_out_g_2", 4), ("attn_out_g_2", 4), ("ffn_norm_g_2", 8),
    ("ffn_conv_w_2", CONV3 * 44), ("ffn_conv_b_2", 44), ("final_norm_g_2", 8), ("pre_norm_g_3", 8), ("b_a2_3", 4),
    ("a_ln_g_3", 8), ("a_ln_b_3", 8), ("b_norm_g_3", 8), ("post_norm_g_3", 8),
]
VCOL = {}
for _name, _n in VECTORS:
    VCOL[_name] = sum(n for _, n in VECTORS[:len(VCOL)])
N_VEC = sum(n for _, n in VECTORS)


class Engine:

    def __init__(self, sem):
        self.sem, self.count, self.steps, self.waited = sem, 0, [], {}

    def wait(self, after):
        for token in after:
            if token is None:
                continue
            if isinstance(token, list):
                self.wait(token)
                continue
            sem, value = token
            if self.waited.get(sem.name, 0) < value:
                self.waited[sem.name] = value
                self.steps.append(lambda e, sem=sem, value=value: e.wait_ge(sem, value))

    def run(self, step, after=()):
        self.wait(after)
        self.steps.append(step)

    def do(self, step, after=()):
        self.wait(after)
        self.count += 1
        self.steps.append(lambda e: step(e).then_inc(self.sem, 1))
        return (self.sem, self.count)

    def last(self):
        return (self.sem, self.count) if self.count else None

    def emit(self, e):
        for step in self.steps:
            step(e)


class Dma:

    def __init__(self, engine, sem):
        self.engine, self.sem, self.count = engine, sem, 0

    def start(self, out, in_, after=()):
        self.count += 16
        self.engine.run(lambda e: e.dma_start(out() if callable(out) else out,
                                              in_() if callable(in_) else in_).then_inc(self.sem, 16), after)
        return (self.sem, self.count)


class Program:
    def __init__(self, nc, ctx, dram):
        self.nc, self.ctx, self.dram = nc, ctx, dram
        self.pe, self.dve, self.act, self.pool, self.sp = (
            Engine(self.sem(n)) for n in ("pe_done", "dve_done", "act_done", "pool_done", "sp_done"))
        sb = self.sbuf
        self.w_raw = [sb(f"w_raw{i}", [P, BLOCKS, P]) for i in range(3)]
        self.w_hi = [sb(f"w_hi{i}", [P, BLOCKS, P], F32R) for i in range(3)]
        self.w_lo = [sb(f"w_lo{i}", [P, BLOCKS, P], F32R) for i in range(3)]
        self.w_dma = [Dma(self.sp, self.sem(f"w_landed{i}")) for i in range(3)]
        self.w_landed, self.w_ready, self.w_used = [], [], []
        self.blocks = []
        self.x_plain = self.same_place("x_plain", [P, 2, DC, WIDE])
        self.x_hi = sb("x_hi", [P, DC, WIDE], F32R)
        self.x_lo = sb("x_lo", [P, DC, WIDE], F32R)
        self.res = sb("res", [P, DC, WIDE])
        self.vec = sb("vectors", [P, N_VEC])
        self.ident = sb("identity", [P, P])
        self.upper = sb("upper", [P, P])
        self.ones = sb("ones", [P, P])
        self.head_row = sb("head_row", [H1, H1, P])
        self.tiny = sb("tiny", [P, 4])
        self.ps = ctx.enter_context(nc.psum_tensor("psum", [P, 8, 512], F32))
        self.bank_free = [None] * 8
        self.slot, self.single = 0, 3
        self.jobs = []

        once = Dma(self.sp, self.sem("constants_landed"))
        once.start(self.vec[:, :], dram["vectors"])
        once.start(self.ident[:, :], dram["identity"])
        once.start(self.upper[:, :], dram["upper"])
        self.const = [once.start(self.head_row[:, :, :], dram["head_row"])]
        self.const.append(self.dve.do(lambda e: e.memset(self.ones[:, :], 1.0)))
        for i, value in enumerate((LN_EPS, EPS, 1.0)):
            self.const.append(self.dve.do(lambda e, i=i, value=value: e.memset(self.tiny[:, i:i + 1], value)))

    def sem(self, name):
        return self.ctx.enter_context(self.nc.semaphore(name))

    def sbuf(self, name, shape, dt=F32, ctx=None):
        return (ctx or self.ctx).enter_context(self.nc.sbuf_tensor(name, shape, dt))

    def same_place(self, name, shape):
        with ExitStack() as closed:
            return self.sbuf(name, shape, ctx=closed)

    def everything(self):
        return [e.last() for e in (self.pe, self.dve, self.act, self.pool)]

    def column(self, name, i):
        c = VCOL[name] + i
        return self.vec[:, c:c + 1]

    def activation(self, out, in_, func, after, bias=0.0, scale=1.0, accum=None):
        if accum is None:
            return self.act.do(lambda e: e.activation(out, in_, func, bias=bias, scale=scale), after)
        return self.act.do(lambda e: e.activation(out, in_, func, bias=bias, scale=scale, accum_out=accum), after)

    def copy(self, out, in_, after):
        return self.act.do(lambda e: e.copy(out, in_), after)

    def tt(self, out, a, b, op, after, eng=None):
        return (eng or self.dve).do(lambda e: e.tensor_tensor(out, a, b, op), after)

    def ts(self, out, a, s1, s2, op0, op1, after):
        if s2 is None:
            return self.dve.do(lambda e: e.tensor_scalar(out, a, s1, None, op0), after)
        return self.dve.do(lambda e: e.tensor_scalar(out, a, s1, s2, op0, op1), after)

    def stt(self, out, a, s, b, op0, op1, after):
        return self.dve.do(lambda e: e.scalar_tensor_tensor(out, a, s, b, op0, op1), after)

    def dcopy(self, out, in_, after):
        return self.dve.do(lambda e: e.tensor_copy(out, in_), after)

    def memset(self, out, value, after=()):
        return self.dve.do(lambda e: e.memset(out, value), after)

    def mm(self, products, after, transpose=False):
        def step(e):
            for out, lhsT, rhs, start, stop in products:
                if transpose:
                    ins = e.transpose(out, lhsT, rhs)
                else:
                    ins = e.matmul(out, lhsT, rhs, start=start, stop=stop, skip_group_check=True)
            return ins
        return self.pe.do(step, after)

    def prefetch(self, tile):
        while len(self.w_ready) < min(tile + 3, N_TILES):
            n = len(self.w_ready)
            if n >= 3 and n - 3 >= len(self.w_used):
                break
            self.load_tile(n)
            raw, hi, lo = self.w_raw[n % 3], self.w_hi[n % 3], self.w_lo[n % 3]
            used = self.w_used[n - 3] if n >= 3 else None
            high = self.copy(hi[:, :, :], raw[:, :, :], [self.w_landed[n], used])
            low = self.tt(lo[:, :, :], raw[:, :, :], hi[:, :, :].bitcast(F32), ALU.subtract,
                          [high, self.w_landed[n], used], self.pool)
            self.w_ready.append(low)
        for n in range(len(self.w_landed), min(len(self.w_ready) + 3, N_TILES)):
            self.load_tile(n)

    def load_tile(self, n):
        if n < len(self.w_landed):
            return
        freed = self.w_ready[n - 3] if n >= 3 else None
        self.w_landed.append(self.w_dma[n % 3].start(self.w_raw[n % 3][:, :, :], self.dram["w"][n], [freed]))

    def product_steps(self, chunks, hi, lo, pieces, x_ready, take):
        width = len(pieces)
        first = self.slot * (2 if width == 2 else 3)
        if width == 1:
            first = self.single = (self.single + 1) % 4
        else:
            self.slot = (self.slot + 1) % 2
        banks = range(first, first + width)
        wait_banks = [self.bank_free[b] for b in banks]
        start = len(self.blocks)
        self.blocks += chunks
        token = None
        for i, (t0, m) in enumerate(pieces):
            for k in range(len(chunks)):
                tile, at = divmod(start + k, BLOCKS)
                if i == 0 and (at == 0 or k == 0):
                    self.prefetch(tile)
                last_k = k == len(chunks) - 1

                def step(e, whi=self.w_hi[tile % 3][:, at, :], wlo=self.w_lo[tile % 3][:, at, :],
                         out=self.ps[:, first + i, 0:m], xhi=hi(k)[:, t0:t0 + m], xlo=lo(k)[:, t0:t0 + m],
                         first_k=k == 0, last_k=last_k):
                    e.matmul(out, whi, xhi, start=first_k, stop=False, skip_group_check=True)
                    e.matmul(out, whi, xlo, start=False, stop=False, skip_group_check=True)
                    return e.matmul(out, wlo, xhi, start=False, stop=last_k, skip_group_check=True)
                ready = x_ready[k]
                if isinstance(ready, PerPiece):
                    ready = ready[i]
                after = [self.w_ready[tile], ready] + (wait_banks if k == 0 and i == 0 else [])
                used = i == width - 1 and (at == BLOCKS - 1 or start + k == N_BLOCKS - 1)
                if used or (last_k and i == width - 1):
                    token = self.pe.do(step, after)
                    if used:
                        self.w_used.append(token)
                else:
                    self.pe.run(step, after)
                if i < width - 1 or not last_k:
                    yield
        done = take(self.ps[:, first:first + width, 0:pieces[0][1]], list(banks), token)
        self.free(banks, done)
        yield

    def product(self, *args):
        self.jobs.append(self.product_steps(*args))

    def pump(self, n):
        while n > 0 and self.jobs:
            try:
                next(self.jobs[0])
                n -= 1
            except StopIteration:
                self.jobs.pop(0)

    def drain(self):
        while self.jobs:
            for _ in self.jobs.pop(0):
                pass

    def take_slot(self):
        first = 3 * self.slot
        self.slot = (self.slot + 1) % 2
        return [first, first + 1, first + 2]

    def free(self, banks, token):
        for b in banks:
            self.bank_free[b] = token

    def x_parts(self):
        return (lambda k: self.x_hi[:, k, :]), (lambda k: self.x_lo[:, k, :])

    def split(self, src, k, t0, t1, after, hi=None, lo=None, eng=None):
        hi, lo = self.x_hi if hi is None else hi, self.x_lo if lo is None else lo
        high = self.copy(hi[:, k, t0:t1], src, after)
        return self.tt(lo[:, k, t0:t1], src, hi[:, k, t0:t1].bitcast(F32), ALU.subtract, [high, after], eng)

    def split_scaled(self, src, column, k, t0, t1, after, grid=lambda t: t):
        hi, lo = grid(self.x_hi[:, k, t0:t1]), grid(self.x_lo[:, k, t0:t1])
        high = self.activation(hi, src, ACT.Copy, after, scale=column)
        return self.stt(lo, src, column, hi.bitcast(F32), ALU.mult, ALU.subtract, [high, after])

    def ones_product(self, view, pieces, banks, after):
        return self.mm([(self.ps[:, b, 0:m], self.ones[:, :], view[:, t0:t0 + m], True, True)
                        for b, (t0, m) in zip(banks, pieces)], [after, self.const, [self.bank_free[b] for b in banks]])

    def inverse_root(self, out, scratch, sums, n, eps, after):
        guess = self.root_guess(out, sums, n, eps, after)
        return self.root_newton(out, scratch, sums, n, eps, [guess])

    def root_guess(self, out, sums, n, eps, after):
        eps_col = self.tiny[:, 0:1] if eps == LN_EPS else self.tiny[:, 1:2]
        a = self.activation(out, sums, ACT.Ln, [after, self.const], bias=eps_col, scale=1.0 / n)
        return self.activation(out, out, ACT.Exp, [a], scale=-0.5)

    def root_newton(self, out, scratch, sums, n, eps, after):
        c = self.tt(scratch, out, out, ALU.mult, after)
        d = self.stt(scratch, sums, n * eps, scratch, ALU.add, ALU.mult, [c])
        e = self.ts(scratch, scratch, -0.5 / n, 1.5, ALU.mult, ALU.add, [d])
        return self.tt(out, out, scratch, ALU.mult, [e])

    def norm(self, xs, ready, pieces, n, eps, scratch, squares, banks=(0, 1, 2), center=False, after=None, fill=0):
        view = lambda t: t[:, pieces[0][0]:pieces[-1][0] + pieces[-1][1]]
        grid = lambda t: view(t).rearrange("p (a b) -> p a b", a=len(pieces))
        banks = list(banks)[:len(pieces)]
        sums = self.ps[:, banks[0]:banks[0] + len(pieces), 0:pieces[0][1]]
        rstd, mean, tmp = scratch
        if center:
            x, r = xs[0], ready[0]
            if len(xs) > 1:
                x = tmp
                r = self.tt(view(tmp), view(xs[0]), view(xs[1]), ALU.add, [ready[0], ready[1], after])
                for y, s in zip(xs[2:], ready[2:]):
                    r = self.tt(view(tmp), view(tmp), view(y), ALU.add, [r, s])
            s = self.ones_product(x, pieces, banks, r)
            self.pump(fill)
            m = self.activation(grid(mean), sums, ACT.Copy, [s, self.dve.last(), after], scale=1.0 / n)
            self.free(banks, m)
            ready = [self.tt(view(x), view(x), view(mean), ALU.subtract, [m, r, s]) for x, r in zip(xs, ready)]
        sums_of = Moments(self, squares[0], [squares[1], tmp], view, [after, self.dve.last()])
        for x, r in zip(xs, ready):
            sums_of.square(view(x), r)
        s = self.ones_product(squares[0], pieces, banks, sums_of.token)
        self.pump(fill)
        rs = self.inverse_root(grid(rstd), grid(tmp), sums, n, eps, [s, self.dve.last(), after])
        self.free(banks, rs)
        return rs, ready


def half_stats(p, i, xs, ready, sums_token, mean, squares, n, after, fill=0):
    cols = slice(512 * i, 512 * i + 512)
    used = [after] * len(squares)
    m = p.activation(mean[:, 0:512], p.ps[:, 4 + i, :], ACT.Copy, [sums_token, after], scale=1.0 / n)
    p.free([4 + i], m)
    p.pump(fill)
    centred = []
    for k, x in enumerate(xs):
        centred.append(p.tt(x[:, cols], x[:, cols], mean[:, 0:512], ALU.subtract, [m, ready[k]]))
        r = k % len(squares)
        q = p.activation(squares[r][:, 0:512], x[:, cols], ACT.Square, [centred[k], used[r]])
        p.pump(fill)
        used[r] = p.mm([(p.ps[:, 6 + i, :], p.ones[:, :], squares[r][:, 0:512], k == 0, k == len(xs) - 1)],
                       [q, p.const, p.bank_free[6 + i] if k == 0 else None])
    return centred, used[r]


def half_apply(p, i, xs, stats, rstd, tmp, n, eps, gain, apply, after, fill=0):
    cols = slice(512 * i, 512 * i + 512)
    centred, summed = stats
    root = p.inverse_root(rstd[:, 0:512], tmp[:, 0:512], p.ps[:, 6 + i, :], n, eps, [summed, after])
    p.free([6 + i], root)
    scaled = lambda k: p.stt(xs[k][:, cols], xs[k][:, cols], p.column(gain, k), rstd[:, 0:512], ALU.mult, ALU.mult, [root, centred[k]])
    following = scaled(0)
    for k, x in enumerate(xs):
        now, following = following, scaled(k + 1) if k + 1 < len(xs) else None
        apply(k, i, cols, x[:, cols], now)
        p.pump(fill)


def layer_norm(p, xs, ready, sums_token, mean, rstd, tmp, squares, n, eps, gain, apply, after, fill=0):
    half = lambda t, i: t[:, 512 * i:512 * i + 512]
    stats = []
    for i in range(2):
        stats.append(half_stats(p, i, xs, ready, sums_token, half(mean, i), squares, n, [after, stats[0][1] if i else None], fill))
    for i in range(2):
        half_apply(p, i, xs, stats[i], half(rstd, i), half(tmp, i), n, eps, gain, apply, after)


class PerPiece(list):
    pass


class Moments:

    def __init__(self, p, total, squares, view=lambda t: t, after=None):
        self.p, self.total, self.squares, self.view, self.token, self.i = p, total, squares, view, None, 0
        self.used, self.after = [after] * len(squares), after

    def square(self, x, ready, scale=1.0):
        p, i = self.p, self.i
        self.i += 1
        if i == 0:
            self.token = p.activation(self.view(self.total), x, ACT.Square, [ready, self.after], scale=scale)
            return
        r = i % len(self.squares)
        sq = self.view(self.squares[r])
        c = p.activation(sq, x, ACT.Square, [ready, self.used[r]], scale=scale)
        self.token = self.used[r] = p.tt(self.view(self.total), self.view(self.total), sq, ALU.add, [c, self.token])


def block_of(name, k, cols):
    return (name, k * P, P, [(0, cols, P)] if isinstance(cols, int) else cols)


FILL = (24, 2, 6)
NORM1 = ((3, 2, 3), (3, 2, 1))


def layer_1(p):
    dram, ps = p.dram, p.ps
    hi, lo = p.x_parts()
    ctx = ExitStack()
    mix = p.sbuf("mix_1", [P, 8, WIDE], ctx=ctx)
    work = p.sbuf("work_1", [P, 7, WIDE], ctx=ctx)
    w_pool = p.sbuf("w_pool", [P, 4, P], ctx=ctx)
    gate_bias = p.sbuf("gate_bias", [P, 1], ctx=ctx)
    pool_fix = p.sbuf("pool_fix", [P, 4, 16], ctx=ctx)
    b_cols = p.sbuf("b_cols", [P, 8, H1], ctx=ctx)

    xin = [Dma(p.sp, p.sem(f"x_landed{k % 4}")) if k < 4 else None for k in range(8)]
    x_ready = []
    for k in range(8):
        landed = xin[k % 4].start(p.res[:, k, 0:S], dram["x"][k], [x_ready[k - 4] if k >= 4 else None])
        if k == 0:
            p.prefetch(0)
        x_ready.append(p.split(p.res[:, k, 0:S], k, 0, S, [landed]))
    small = Dma(p.sp, p.sem("small_1_landed"))
    small.start(gate_bias[:, :], dram["gate_bias"])
    small.start(pool_fix[:, :, :], dram["pool_fix"])
    const = p.const + [small.start(w_pool[:, :, :], dram["w_pool"])]

    T = [p.res[:, i, :] for i in range(8)] + [work[:, i, :] for i in range(7)]
    row_b, row_m, row_am = T[0], T[1], T[2]
    q_in, k_in, q_t, k_t = T[3], T[4], T[5], T[6]
    v_f, v_t, m_bc, floor, prob = T[7], T[8], T[9], T[10], T[11]
    o_sig = [T[12], T[13]]
    hbuf = T[14]
    res_free = x_ready[-1]

    gts = work[:, 5, 0:S]

    def take_gates(view, banks, tok):
        return p.ts(gts[0:36, :], ps[0:36, banks[0]:banks[0] + 2, :], gate_bias[0:36, :], None, ALU.add, None, [tok, const])

    p.product([block_of("w_in", k, [(0, OFF_G, 4), (32, OFF_G + 4, 4)]) for k in range(8)], hi, lo, TWO, x_ready, take_gates)
    p.drain()
    a = p.dve.last()
    i_row, f_row, l_row, e_row = work[0:4, 5, 0:S], work[0:4, 6, 0:S], work[0:4, 0, 0:S], work[0:4, 1, 0:S]
    one_row = work[0:4, 2, 0:S]
    b = p.dcopy(f_row, gts[32:36, :], [a])
    c = p.stt(e_row, f_row, -1.0, f_row, ALU.mult, ALU.max, [b])
    c = p.activation(e_row, e_row, ACT.Exp, [c], scale=-1.0)
    c = p.activation(e_row, e_row, ACT.Ln, [c, const], bias=p.tiny[0:4, 2:3])
    c = p.stt(l_row, f_row, 0.0, e_row, ALU.min, ALU.subtract, [c])
    one = p.memset(one_row, 1.0)
    A, B, M, AM = work[0:4, 3, 0:S], row_b[0:4, 0:S], row_m[0:4, 0:S], row_am[0:4, 0:S]
    c = p.dve.do(lambda e: e.tensor_tensor_scan(A, one_row, l_row, 0.0, ALU.mult, ALU.add), [c, one])
    bt = p.tt(B, i_row, A, ALU.subtract, [c, res_free])
    mt = p.dve.do(lambda e: e.tensor_tensor_scan(M, one_row, B, 0.0, ALU.mult, ALU.max), [bt])
    amt = p.tt(AM, A, M, ALU.add, [mt])
    pads = [p.memset(x[:, 0:3], 0.0, [res_free]) for x in (q_in, k_in)]

    state = dict(q_in=None, v_f=None, q=None, v=None, o=[None, None], m_bc=None, prob=[None, None], h=None)

    def products_of_head(h):
        out = {}
        for n, off in (("q", 0), ("k", 512), ("v", 1024), ("o", OFF_O)):
            def take(view, banks, tok, n=n):
                if n == "o":
                    e = p.activation(o_sig[h % 2][:, 0:S], view, ACT.Sigmoid, [tok, state["o"][h % 2]])
                elif n == "v":
                    e = p.copy(v_f[:, 0:S], view, [tok, state["v_f"], res_free])
                else:
                    e = p.copy((q_in if n == "q" else k_in)[:, 3:3 + S], view, [tok, state["q_in"], res_free])
                out[n] = e
                return e
            p.product([block_of("w_in", k, off + h * P) for k in range(8)], hi, lo, TWO, x_ready, take)
        return out

    def prepare(h, got):
        ready = []
        for n, src, dst in (("q", q_in, q_t), ("k", k_in, k_t)):
            chunk = h + (4 if n == "k" else 0)
            acc = dst[:, 0:S]
            w = lambda j: p.column("w_conv", j * 8 + chunk)
            c = p.ts(acc, src[:, 0:S], w(0), None, ALU.mult, None, [got[n], pads, state["q"], const, res_free])
            for j in range(1, CONV1):
                c = p.stt(acc, src[:, j:j + S], w(j), acc, ALU.mult, ALU.add, [c])
            state["q_in"] = c
            c = p.activation(acc, acc, ACT.Silu, [c])
            if n == "k":
                c = p.ts(acc, acc, P ** -0.5, None, ALU.mult, None, [c])
            ready.append(c)
        for g in range(2):
            t = p.mm([(ps[:, 4 + g, j * P:(j + 1) * P], v_f[:, (4 * g + j) * P:(4 * g + j + 1) * P], p.ident[:, :], True, True)
                      for j in range(4)], [got["v"], const, p.bank_free[4 + g]], transpose=True)
            state["v_f"] = t
            e = p.copy(v_t[:, g * 512:(g + 1) * 512], ps[:, 4 + g, :], [t, state["v"]])
            p.free([4 + g], e)
            ready.append(e)
        return ready

    def attend(h, ready, got):
        p.pump(FILL[0])
        for row, dst, tok in ((M, m_bc, mt), (AM, floor, amt)):
            for g in range(2):
                t = p.mm([(ps[:, 4 + g, :], p.head_row[:, h, :], row[:, g * 512:(g + 1) * 512], True, True)],
                         [tok, const, p.bank_free[4 + g]])
                half = dst[:, g * 512:(g + 1) * 512]
                if row is M:
                    e = p.copy(half, ps[:, 4 + g, :], [t, state["m_bc"]])
                    m_tok = e
                else:
                    e = p.activation(half, ps[:, 4 + g, :], ACT.Exp, [t, state["m_bc"]], scale=-1.0)
                    floor_tok = e
                p.free([4 + g], e)
        n = 0
        for half in range(2):
            blocks = []
            for j in range(4 * half + 4):
                t0 = max(half * 512, j * P)
                blocks.append((j, t0, (half + 1) * 512 - t0))

            def scores(i):
                j, t0, w = blocks[i]
                bank = 4 + i % 2
                return p.mm([(ps[:, bank, 0:w], k_t[:, j * P:(j + 1) * P], q_t[:, t0:t0 + w], True, True)],
                            [ready, p.bank_free[bank]])

            def weights(i, n):
                j, t0, w = blocks[i]
                pr = prob[:, (n % 2) * 512:(n % 2) * 512 + w]
                c = p.ts(pr, m_bc[:, t0:t0 + w], b_cols[:, j, h:h + 1], 0.0, ALU.subtract, ALU.max, [m_tok, cols, state["prob"][n % 2]])
                return pr, p.activation(pr, pr, ACT.Exp, [c], scale=-1.0)

            s_tok = {0: scores(0)}
            following = weights(0, n)
            for i, (j, t0, w) in enumerate(blocks):
                pr, c = following
                if i + 1 < len(blocks):
                    s_tok[i + 1] = scores(i + 1)
                    following = weights(i + 1, n + 1)
                p.pump(FILL[1])
                bank = 4 + i % 2
                if t0 == j * P:
                    c = p.tt(pr[:, 0:P], pr[:, 0:P], p.upper[:, :], ALU.mult, [c, const])
                c = p.tt(pr, pr, ps[:, bank, 0:w], ALU.mult, [c, s_tok[i]])
                p.free([bank], c)
                o0 = t0 - half * 512
                last = i == len(blocks) - 1
                t = p.mm([(ps[:, 6, o0:o0 + w], v_t[:, j * P:(j + 1) * P], pr, i == 0, last),
                          (ps[:, 7, o0:o0 + w], p.ones[:, :], pr, i == 0, last)],
                         [c, ready] + ([p.bank_free[6], p.bank_free[7]] if i == 0 else []))
                state["prob"][n % 2] = t
                n += 1
            sl = slice(half * 512, (half + 1) * 512)
            c = p.activation(hbuf[:, sl], ps[:, 7, :], ACT.Abs, [t, state["h"]])
            c = p.tt(floor[:, sl], hbuf[:, sl], floor[:, sl], ALU.max, [c, floor_tok])
            c = p.dve.do(lambda e, sl=sl: e.reciprocal(floor[:, sl], floor[:, sl]), [c])
            c = p.tt(hbuf[:, sl], ps[:, 6, :], floor[:, sl], ALU.mult, [c, state["h"]])
            p.free([6, 7], c)
        state["q"] = state["v"] = t
        rs, _ = p.norm([hbuf], [c], TWO, P, LN_EPS, (m_bc, floor, prob), (k_t, q_t), banks=(6, 7), center=True, after=p.pe.last(), fill=FILL[2])
        state["q"] = [state["q"], p.pe.last()]
        c = p.stt(hbuf[:, 0:S], hbuf[:, 0:S], p.column("hn_g", h), m_bc[:, 0:S], ALU.mult, ALU.mult, [rs, const])
        c = p.tt(mix[:, h, 0:S], hbuf[:, 0:S], o_sig[h % 2][:, 0:S], ALU.mult, [c, got["o"]])
        state["o"][h % 2] = state["m_bc"] = state["h"] = c
        state["prob"] = [c, c]
        return c

    def pool_product(g):
        def take(view, banks, tok):
            p_in = mix[:, 4 + g, :]
            e = p.copy(p_in[:, 0:S], view, [tok])
            src, dst, c = p_in, q_in, e
            for step in range(g + 1):
                shift = 1 << step
                c1 = p.tt(dst[:, shift:S], src[:, shift:S], src[:, 0:S - shift], ALU.add, [c])
                c = [c1, p.dcopy(dst[:, 0:shift], src[:, 0:shift], [c])]
                src, dst = dst, (k_in if dst is q_in else q_in)
            win = 2 << g
            c = p.tt(src[:, 0:16], src[:, 0:16], pool_fix[:, g, :], ALU.mult, [c, const])
            pooled[g] = p.stt(p_in[:, 0:S], src[:, 0:S], 1.0 / win, p_in[:, 0:S], ALU.mult, ALU.subtract, [c])
            return e
        p.product([block_of("w_in", k, OFF_P + g * P) for k in range(8)], hi, lo, TWO, x_ready, take)

    mix_ready, pooled = [None] * 8, {}
    got = products_of_head(0)
    p.drain()
    t = p.mm([(ps[:, 4, 4 * j:4 * j + 4], row_b[0:4, j * P:(j + 1) * P], p.ident[0:4, 0:4], True, True) for j in range(8)],
             [bt, const], transpose=True)
    cols = p.dcopy(b_cols[:, :, :], ps[:, 4, 0:32], [t])
    p.free([4], cols)
    ready = prepare(0, got)
    for h in range(H1):
        if h + 1 < H1:
            got_next = products_of_head(h + 1)
        else:
            for g in range(4):
                pool_product(g)
        mix_ready[h] = attend(h, ready, got)
        p.drain()
        if h + 1 < H1:
            got = got_next
            ready = prepare(h + 1, got)

    old = p.pe.last()
    m_ready = {k: p.split(mix[:, k, 0:S], k, 0, S, [mix_ready[k], old]) for k in range(3)}
    for g in range(4):
        banks = [4 + 2 * (g % 2), 5 + 2 * (g % 2)]
        t = p.mm([(ps[:, banks[i], :], w_pool[:, g, :], mix[:, 4 + g, i * 512:(i + 1) * 512], True, True) for i in range(2)],
                 [pooled[g], const, p.bank_free[banks[0]], p.bank_free[banks[1]]])
        view, scale = ps[:, banks[0]:banks[0] + 2, :], p.column("pool_scale", g)
        grid = lambda t: t.rearrange("p (a b) -> p a b", a=2)
        m_ready[4 + g] = p.split_scaled(view, scale, 4 + g, 0, S, [t, old], grid)
        p.free(banks, m_ready[4 + g])
    m_ready[3] = p.split(mix[:, 3, 0:S], 3, 0, S, [mix_ready[3], old])

    back = [Dma(p.sp, p.sem(f"x_again_landed{i}")) for i in range(4)]
    switch = p.everything()
    x_back = [back[i].start(p.res[:, 2 * i:2 * i + 2, META:META + S], dram["x"][2 * i:2 * i + 2].rearrange("k p t -> p k t"), switch)
              for i in range(4)]
    ctx.close()
    ctx = ExitStack()
    keep = ExitStack()
    kept = p.sbuf("squares_2", [P, WIDE], ctx=keep)
    plain = p.same_place("h1_plain", [P, 2, 6, S])
    h_hi = p.sbuf("h1_hi", [P, 6, S], F32R, ctx=ctx)
    h_lo = p.sbuf("h1_lo", [P, 6, S], F32R, ctx=ctx)
    tmp = p.sbuf("h1_tmp", [P, 2, S], ctx=ctx)
    total = p.sbuf("total_1", [P, S], ctx=ctx)
    halves_of = lambda part, slot: [plain[:, part, slot, 512 * i:512 * i + 512] for i in range(2)]
    mean, rstd, root_tmp, *squares = halves_of(1, 4) + halves_of(1, 5) + halves_of(0, 4)
    real = lambda k: p.res[:, k, META:META + S]
    xs = [real(k) for k in range(8)]

    def summing(i, ready, residual):
        cols = slice(512 * i, 512 * i + 512)

        def of(m):
            def take(view, banks, tok):
                x = real(m)[:, cols]
                c = p.stt(x, x, ALPHA if residual else 1.0, view[:, 0, :], ALU.mult, ALU.add, [tok, ready[m]])
                done.append(c)
                if m:
                    sums[0] = p.tt(total[:, cols], real(0)[:, cols] if m == 1 else total[:, cols], x, ALU.add, [c, done[0], sums[0], switch])
                return c
            return take
        done, sums = [], [None]
        return of, done, sums

    def sum_product(i, sums):
        return p.mm([(ps[:, 4 + i, :], p.ones[:, :], total[:, 512 * i:512 * i + 512], True, True)], [sums[0], p.const, p.bank_free[4 + i]])

    order = [0, 1, 2, 4, 5, 6, 7, 3]
    x1 = [PerPiece([None, None]) for _ in range(8)]
    x_old = [None, None]

    def apply(k, i, cols, x, c):
        c = p.activation(x, x, ACT.Identity, [c], bias=p.column("ln1_b", k))
        x1[k][i] = p.split(x, k, cols.start, cols.stop, [c, x_old[i]])

    def w_out(i, of):
        for m in range(8):
            p.product([block_of("w_out", k, m * P) for k in order], lambda c: p.x_hi[:, order[c], :], lambda c: p.x_lo[:, order[c], :],
                      TWO[i:i + 1], [m_ready[k] for k in order], of(m))

    def normalise(i, done, sums, apply, fills, after):
        s = sum_product(i, sums)
        p.pump(fills[0])
        stats = half_stats(p, i, xs, done, s, mean, squares, D, after, fills[1])
        half_apply(p, i, xs, stats, rstd, root_tmp, D, LN_EPS, "ln1_g", apply, after, fills[2])

    x_in = [x_back[m // 2] for m in range(8)]
    parts = [summing(i, x_in, True) for i in range(2)]
    w_out(0, parts[0][0])
    p.drain()
    x_old[0] = p.pe.last()
    w_out(1, parts[1][0])
    normalise(0, parts[0][1], parts[0][2], apply, NORM1[0], switch)
    p.drain()
    x_old[1] = p.pe.last()

    h_used = [switch] * 6
    t_used = [switch] * 2
    h_ready = {}
    acc = [None] * 8

    def hidden(j, pieces=TWO):
        c0, c1 = pieces[0][0], pieces[-1][0] + 512

        def take(view, banks, tok):
            r = tmp[:, j % 2, c0:c1]
            e = p.activation(r.rearrange("p (a b) -> p a b", b=512), view, ACT.Relu, [tok, t_used[j % 2]])
            c = p.tt(r, r, r, ALU.mult, [e])
            c = p.split(r, j % 6, c0, c1, [c, h_used[j % 6]], h_hi, h_lo)
            t_used[j % 2] = c
            h_ready[j] = [c, h_ready.get(j)]
            return e
        p.product([block_of("w_ff1", k, j * P) for k in range(8)], hi, lo, pieces,
                  [t[1] for t in x1] if c0 else x1, take)

    for j in range(4):
        hidden(j, TWO[0:1])
    normalise(1, parts[1][1], parts[1][2], apply, NORM1[1], [switch, p.dve.last(), p.act.last()])
    for j in range(4):
        hidden(j, TWO[1:2])
    h_used[4] = h_used[5] = [p.dve.last(), p.act.last()]
    p.drain()

    def project(g):
        ks = range(4 * g, 4 * g + 4)
        for m in range(8):
            def take(view, banks, tok, m=m):
                out = real(m)
                c = p.stt(out, out, ALPHA if g == 0 else 1.0, view, ALU.mult, ALU.add, [tok, acc[m], x1[m]])
                acc[m] = c
                return c
            p.product([block_of("w_ff2", k, m * P) for k in ks],
                      lambda i: h_hi[:, (4 * g + i) % 6, :], lambda i: h_lo[:, (4 * g + i) % 6, :],
                      TWO, [h_ready[k] for k in ks], take)
            p.drain()
        for k in ks:
            h_used[k % 6] = p.pe.last()

    for g in range(FF1 // 4 - 1):
        for j in range(4 * g + (4 if g == 0 else 2), 4 * g + 6):
            hidden(j)
            p.drain()
        project(g)
    for j in range(FF1 - 2, FF1):
        hidden(j)
        p.drain()

    def last_group(i):
        ks = range(FF1 - 4, FF1)
        of, done, sums = summing(i, acc, False)
        for m in range(8):
            p.product([block_of("w_ff2", k, m * P) for k in ks], lambda c: h_hi[:, ks[c] % 6, :], lambda c: h_lo[:, ks[c] % 6, :],
                      TWO[i:i + 1], [h_ready[k] for k in ks], of(m))
        return done, sums
    done_0, sums_0 = last_group(0)
    p.drain()
    done, sums = last_group(1)
    free_halves = [h for part in range(2) for slot in (2, 3) for h in halves_of(part, slot)]
    return [keep, ctx], [done_0, done], [lambda: sum_product(0, sums_0), lambda: sum_product(1, sums)], kept, free_halves, [h_used[2], h_used[3]]


NORM2 = (2, 1, 1)
FILL2 = dict(conv=(12, 12, 8, 0), comp=7, att=(1, 1, 1, 1, 1, 1, 1, 1, 1))
LAG = 1
LATE = 2


def layer_2(p, contexts, done, sum_of, total, halves, switch):
    dram, ps = p.dram, p.ps
    hi, lo = p.x_parts()
    real = lambda k: p.res[:, k, META:META + S]
    grid = lambda t: t.rearrange("p (a b) -> p a b", a=3)
    mean, rstd, tmp, part = halves[0], halves[1], halves[2], halves[6:8]
    squares = halves[3:6]
    old = p.pe.last()

    meta_dma = Dma(p.sp, p.sem("meta_landed"))
    meta = meta_dma.start(p.res[:, :, 0:META], dram["meta"], [old])
    pad = [p.memset(p.res[:, :, META + S:WIDE], 0.0, [old])]
    pad += [p.memset(x[:, :, META + S:WIDE].bitcast(F32), 0.0, [old]) for x in (p.x_hi, p.x_lo)]
    edges = [p.split_scaled(p.res[:, k, 0:META], p.column("mix_norm_g_2", k), k, 0, META, [meta, old]) for k in range(8)]
    c = p.activation(part[0][:, 0:8 * META].rearrange("p (k t) -> p k t", k=8), p.res[:, :, 0:META], ACT.Square, [meta, switch])
    e = p.dve.do(lambda e: e.tensor_reduce(total[:, 0:META], part[0][:, 0:8 * META].rearrange("p (k t) -> p t k", k=8), AX.X, ALU.add), [c])
    total_ends = [e, p.memset(total[:, META + S:WIDE], 0.0, switch)]

    h_ready, x_ready = [PerPiece([None] * 2) for _ in range(8)], [PerPiece([None] * 3) for _ in range(8)]
    rms_used = [switch, switch]
    totals = [None, None]

    def apply(k, i, cols, x, c):
        c = h_ready[k][i] = p.activation(x, x, ACT.Identity, [c], bias=p.column("ln2_b", k))
        s = p.split_scaled(x, p.column("mix_norm_g_2", k), k, META + cols.start, META + cols.stop, [c, old])
        if i == 0:
            x_ready[k][0] = [s, edges[k]]
        x_ready[k][1] = x_ready[k][2] = [s, pad]
        t = total[:, META + cols.start:META + cols.stop]
        if k == 0:
            totals[i] = p.activation(t, x, ACT.Square, [c, total_ends])
        else:
            q = p.activation(part[k % 2], x, ACT.Square, [c, rms_used[k % 2], total_ends])
            totals[i] = rms_used[k % 2] = p.tt(t, t, part[k % 2], ALU.add, [q, totals[i]])

    spill, spilled = Dma(p.sp, p.sem("h0_spilled")), []
    for i in range(2):
        s = sum_of[i]()
        p.pump(NORM2[0])
        after = [switch, p.dve.last(), p.act.last()]
        stats = half_stats(p, i, [real(k) for k in range(8)], done[i], s, mean, squares, D, after, NORM2[1])
        half_apply(p, i, [real(k) for k in range(8)], stats, rstd, tmp, D, LN_EPS, "ln2_g", apply, after, NORM2[2])
        p.drain()
        c0, c1 = (0, META + 512) if i == 0 else (META + 512, WIDE)
        spilled.append(spill.start(dram["spill_2"][:, :, c0:c1], p.res[:, :, c0:c1], [[t[i] for t in h_ready], meta, pad]))
    free = [spilled, x_ready]

    switch = p.everything()
    keep, ctx = contexts
    ctx.close()
    ctx = ExitStack()
    mix = p.sbuf("mix_2", [P, 8, WIDE], ctx=ctx)
    u_pad = p.sbuf("u_padded", [P, 4, CONV2 - 1 + WIDE], ctx=ctx)
    work = p.sbuf("work_2", [P, 3, WIDE], ctx=ctx)
    small = p.sbuf("v_and_probs_of_meta", [P, 3, P], ctx=ctx)
    col = p.sbuf("softmax_columns", [P, 4, 4], ctx=ctx)
    pair_out = p.sbuf("pair_out", [P, 2, P], ctx=ctx)
    M = [mix[:, i, :] for i in range(8)]
    tmp = M[2]

    T = [p.res[:, i, :] for i in range(8)] + [work[:, i, :] for i in range(3)] + [total[:, :]]
    rope_t, sig, rms = T[6], T[10], T[8]
    rope_dma = Dma(p.sp, p.sem("rope_landed"))
    rope = rope_dma.start(rope_t, dram["rope"], free)
    zeros = p.memset(u_pad[:, :, 0:CONV2 - 1], 0.0, switch)

    def rms_of(total, ready, n, out, scratch, after):
        banks = p.take_slot()
        t = p.ones_product(total, THREE, banks, ready)
        r = p.inverse_root(grid(out), grid(scratch), ps[:, banks[0]:banks[0] + 3, 0:348], n, EPS, [t, after])
        p.free(banks, r)
        return r

    mix_rms = []

    def need_rms():
        if not mix_rms:
            mix_rms.append(rms_of(total, totals, D, rms, tmp, [x_ready, switch, p.dve.last()]))

    def leave(out, rows=slice(0, P)):
        def take(view, banks, tok):
            need_rms()
            return p.tt(grid(out)[rows], ps[rows, banks[0]:banks[0] + 3, 0:348], grid(rms)[rows], ALU.mult, [tok, mix_rms, free])
        return take

    def w_in(cols, take):
        p.product([block_of("w_in_2", k, cols) for k in range(8)], hi, lo, THREE, x_ready, take)
        p.drain()
        return p.dve.last()

    def compressed(first, n, total):
        m = Moments(p, total, [T[10]], after=p.dve.last())
        for i in range(first, first + n):
            m.square(T[i], w_in(1024 + i * P, leave(T[i])))
            fill(FILL2["comp"])
        return m

    def normed(m, first, n, name):
        r = rms_of(T[9], m.token, n * P, T[11], T[10], p.dve.last())
        return [p.stt(T[i], T[i], p.column(name, i - first), T[11], ALU.mult, ALU.mult, [r]) for i in range(first, first + n)]

    steps = []
    conv_token = [None] * 4

    def conv_step(c, j, u_ready):
        src = u_pad[:, c, j:j + WIDE]
        w = p.column("conv_w_2", j * 4 + c)
        if j == 0:
            conv_token[c] = p.ts(M[c], src, w, p.column("conv_b_2", c), ALU.mult, ALU.add, [u_ready, zeros, mix_rms, x_ready])
        else:
            conv_token[c] = p.stt(M[c], src, w, M[c], ALU.mult, ALU.add, [conv_token[c]])

    def fill(n):
        for _ in range(min(n, len(steps))):
            steps.pop(0)()

    last = [None]

    def convolved(c):
        def take_gate(view, banks, tok):
            need_rms()
            e = p.tt(grid(sig), view, grid(rms), ALU.mult, [tok, mix_rms, last, p.dve.last()])
            s = p.activation(sig, sig, ACT.Sigmoid, [e])
            last[0] = p.tt(sig, sig, rms, ALU.mult, [s])
            return e

        def take_a(view, banks, tok):
            last[0] = p.tt(grid(u_pad[:, c, CONV2 - 1:]), view, grid(sig), ALU.mult, [tok, last, switch])
            return last[0]

        w_in(512 + c * P, take_gate)
        w_in(c * P, take_a)
        steps.extend([lambda j=j, r=last[0]: conv_step(c, j, r) for j in range(CONV2)])
        fill(FILL2["conv"][c])

    convolved(0)
    convolved(1)

    kv_m = compressed(3, 2, T[9])
    k_rot = T[5]

    def rotate(out, banks, tok, after):
        x = lambda a, b: ps[a:b, banks[0]:banks[0] + 3, 0:348]
        c = p.tt(grid(out)[64:96], x(96, 128), grid(rope_t)[96:128], ALU.mult, [tok, rope, after])
        d = p.tt(x(64, 96), x(64, 96), grid(rope_t)[64:96], ALU.mult, [tok, rope])
        return p.tt(grid(out)[64:96], grid(out)[64:96], x(64, 96), ALU.add, [c, d])

    def take_rotary(view, banks, tok):
        c = rotate(k_rot, banks, tok, free)
        return p.tt(k_rot[64:96, :], k_rot[64:96, :], rms[64:96, :], ALU.mult, [c, mix_rms])

    rot_ready = w_in([(64, 1664, 32), (96, 1680, 16), (112, 1664, 16)], take_rotary)
    parts_in = [None] * 5
    parts_in[3:5] = normed(kv_m, 3, 2, "kv_norm_g_2")
    q_m = compressed(0, 3, T[9])

    parts_in[0:3] = normed(q_m, 0, 3, "q_norm_g_2")

    convolved(2)
    convolved(3)

    old = p.pe.last()
    parts = [None] * 5
    for i in (3, 4, 0, 1, 2):
        parts[i] = p.split(T[i], i, 0, WIDE, [parts_in[i], old])

    slots = [T[i] for i in (0, 1, 2, 3, 4, 7, 8, 9, 10, 11)]
    keys, q_t, v_f, v_t = slots[0:2], slots[2:4], slots[4], slots[5]
    probs, probs_t = slots[6:8], slots[8:10]
    v_meta, pt_meta = small[:, 0, :], [small[:, 1, :], small[:, 2, :]]
    start = p.everything()
    zm = p.memset(small[:, :, :], 0.0, switch)
    st = dict(scored=start, v_f=start, v_t=start, probs=[start, start], probs_t=[start, start], out=[start, start])
    SCALE = QK ** -0.5
    kv_part = lambda part: lambda k: part[:, 3 + k, :]

    def pair_keys(j):
        out = []

        def take(view, banks, tok):
            for i in range(2):
                out.append(p.copy(grid(keys[i])[0:64], ps[64 * i:64 * i + 64, banks[0]:banks[0] + 3, 0:348], [tok, st["scored"]]))
                out.append(p.dcopy(keys[i][64:96, :], k_rot[64:96, :], [rot_ready, st["scored"]]))
            return out[2]
        p.product([("w_ukv_2", k * P, P, [(0, 2 * j * P, 64), (64, (2 * j + 1) * P, 64)]) for k in range(2)],
                  kv_part(p.x_hi), kv_part(p.x_lo), THREE, parts[3:5], take)
        p.drain()
        return out

    def pair_values(j):
        out = []

        def take(view, banks, tok):
            out.append(p.copy(grid(v_f), view, [tok, st["v_f"]]))
            return out[0]
        p.product([("w_ukv_2", k * P, P, [(0, 2 * j * P + 64, 64), (64, (2 * j + 1) * P + 64, 64)]) for k in range(2)],
                  kv_part(p.x_hi), kv_part(p.x_lo), THREE, parts[3:5], take)
        p.drain()
        return out

    def turn_values(e):
        out = []
        for g in range(2):
            t = p.mm([(ps[:, 6 + g, i * P:(i + 1) * P], v_f[:, META + (4 * g + i) * P:META + (4 * g + i + 1) * P], p.ident[:, :], True, True)
                      for i in range(4)], [e, p.bank_free[6 + g]], transpose=True)
            c = p.copy(v_t[:, g * 512:(g + 1) * 512], ps[:, 6 + g, :], [t, st["v_t"]])
            p.free([6 + g], c)
            out.append(c)
        t = p.mm([(ps[0:META, 6, 0:P], v_f[:, 0:META], p.ident[:, :], True, True)], [e, p.bank_free[6]], transpose=True)
        c = p.copy(v_meta[0:META, :], ps[0:META, 6, 0:P], [t, st["v_t"], zm])
        p.free([6], c)
        st["v_f"] = t
        return out + [c]

    def queries(h, i):
        c = h * QK
        out = []

        def take(view, banks, tok):
            e = p.copy(grid(q_t[i])[0:64], ps[0:64, banks[0]:banks[0] + 3, 0:348], [tok, st["scored"]])
            out.extend([e, rotate(q_t[i], banks, tok, st["scored"])])
            return out
        p.product([("w_uq_2", k * P, P, [(0, c, 64), (64, c + 64, 32), (96, c + 80, 16), (112, c + 64, 16)]) for k in range(3)],
                  hi, lo, THREE, parts[0:3], take)
        p.drain()
        return out

    tiles = [(0, META, META)] + [(META + i * P, P, META + (i + 1) * P) for i in range(8)]
    count = [0]

    def score(j, i, hh, ready):
        q0, _, nk = tiles[i]
        banks = [0, 1, 2] if nk > 1024 or (2 * i + hh) % 2 == 0 else [3, 4]
        b = banks[0]
        t = p.mm([(ps[:, b + n // 512, 0:min(512, nk - n)], q_t[hh][0:QK, q0:q0 + P], keys[hh][0:QK, n:n + min(512, nk - n)], True, True)
                  for n in range(0, nk, 512)], [ready, [p.bank_free[x] for x in banks]])
        st["scored"] = t
        r = count[0] % 2
        cc = col[:, count[0] % 4, :]
        count[0] += 1
        flat = ps[:, b:b + len(banks), :].rearrange("p a b -> p (a b)")
        c = t
        if i:
            c = p.memset(flat[0:64, nk - 64:nk], -1e30, [t])
        c = p.dve.do(lambda e: e.tensor_reduce(cc[:, 0:1], flat[:, 0:nk], AX.X, ALU.max), [c, t])
        c = p.ts(cc[:, 1:2], cc[:, 0:1], -SCALE, None, ALU.mult, None, [c])
        ex = p.activation(probs[r][:, 0:nk], flat[:, 0:nk], ACT.Exp, [c, st["probs"][r]], bias=cc[:, 1:2], scale=SCALE, accum=cc[:, 2:3])
        p.free(banks, ex)
        return dict(j=j, i=i, hh=hh, r=r, cc=cc, ex=ex)

    def turn(s):
        pr, pt, r = probs[s["r"]], probs_t[s["r"]], s["r"]
        n_full = (tiles[s["i"]][2] - META) // P
        out = []
        for g in range(0, n_full, 4):
            bank = 6 + (g // 4) % 2
            n = min(4, n_full - g)
            t = p.mm([(ps[:, bank, x * P:(x + 1) * P], pr[:, META + (g + x) * P:META + (g + x + 1) * P], p.ident[:, :], True, True)
                      for x in range(n)], [s["ex"], p.bank_free[bank]], transpose=True)
            e = (p.copy if g == 0 else p.dcopy)(pt[:, g * P:(g + n) * P], ps[:, bank, 0:n * P], [t, st["probs_t"][r]])
            p.free([bank], e)
            out.append(e)
        t = p.mm([(ps[0:META, 7, 0:P], pr[:, 0:META], p.ident[:, :], True, True)], [s["ex"], p.bank_free[7]], transpose=True)
        e = p.dcopy(pt_meta[r][0:META, :], ps[0:META, 7, 0:P], [t, st["probs_t"][r], zm])
        p.free([7], e)
        st["probs"][r] = t
        s["turned"] = out + [e]

    def weigh(s, ready):
        i, hh, r = s["i"], s["hh"], s["r"]
        nk = tiles[i][2]
        pt, n_full = probs_t[r], (nk - META) // P
        v = slice(64 * hh, 64 * hh + 64)
        o = ps[:, 5, 0:64]
        t = p.mm([(o, pt_meta[r], v_meta[:, v], True, n_full == 0)] +
                 [(o, pt[:, x * P:(x + 1) * P], v_t[:, x * P + v.start:x * P + v.stop], False, x == n_full - 1) for x in range(n_full)],
                 [s["turned"], ready, p.bank_free[5]])
        st["probs_t"][r] = st["v_t"] = t
        cc = s["cc"]
        inv = p.dve.do(lambda e: e.reciprocal(cc[:, 3:4], cc[:, 2:3]), [s["ex"]])
        c = p.ts(pair_out[:, i % 2, v], o, s["cc"][:, 3:4], None, ALU.mult, None, [t, inv, st["out"][i % 2]])
        p.free([5], c)
        halves.append(c)

    def turn_back(j, s):
        q0, used, _ = tiles[s["i"]]
        back = ps[:, 5, P:2 * P]
        t = p.mm([(back, pair_out[:, s["i"] % 2, :], p.ident[:, :], True, True)], [halves[-2:], p.bank_free[5]], transpose=True)
        st["out"][s["i"] % 2] = t
        e = p.copy(mix[:, 4 + j, q0:q0 + used], back[:, 0:used], [t, x_ready, mix_rms])
        p.free([5], e)
        o_ready[j].append(e)

    A = [u_pad[:, c, 0:WIDE] for c in range(4)]
    u = dict(out=[])

    def ones_of(total, ready):
        banks = p.take_slot()
        return banks, p.ones_product(total, THREE, banks, ready)

    def after_conv():
        c = p.tt(A[0], M[0], M[1], ALU.add, conv_token)
        c = p.tt(A[0], A[0], M[2], ALU.add, [c])
        u["c"] = u["c0"] = p.tt(A[0], A[0], M[3], ALU.add, [c])

    def u_mean():
        banks, t = ones_of(A[0], u["c"])
        m = p.activation(grid(A[1]), ps[:, banks[0]:banks[0] + 3, 0:348], ACT.Copy, [t, u["c"]], scale=1.0 / (4 * P))
        p.free(banks, m)
        u["m"] = [m, t]
        u["moments"] = Moments(p, A[0], [A[2]], after=[t, m, u["c"]])

    def u_centre(c):
        t = p.tt(M[c], M[c], A[1], ALU.subtract, [u["m"], conv_token])
        u["moments"].square(M[c], t)

    def u_sums():
        banks, t = ones_of(A[0], u["moments"].token)
        u["sums"] = p.copy(grid(A[3]), ps[:, banks[0]:banks[0] + 3, 0:348], [t, u["c0"]])
        p.free(banks, u["sums"])

    def u_guess():
        u["guess"] = p.root_guess(A[1], A[3], 4 * P, EPS, [u["sums"], p.dve.last()])

    def u_newton():
        u["r"] = u["c0"] = p.root_newton(A[1], A[2], A[3], 4 * P, EPS, [u["guess"], u["sums"]])
        u["moments"] = Moments(p, A[0], [A[2]], after=[u["r"]])

    def u_scale(c):
        u["scaled"] = p.tt(M[c], M[c], A[1], ALU.mult, [u["r"]])

    def u_silus(cs):
        for c in cs:
            u["silu", c] = p.activation(M[c], M[c], ACT.Silu, [u["scaled"]], scale=p.column("conv_ln_g_2", c), bias=p.column("conv_ln_b_2", c))

    def u_square(c):
        u["moments"].square(M[c], u["silu", c])

    def u_gain(c):
        u["out"].append(p.stt(M[c], M[c], p.column("conv_out_g_2", c), A[1], ALU.mult, ALU.mult, [u["r"]]))

    pause = lambda: None
    root = [pause, u_sums, u_guess, u_newton]
    each = lambda f: [lambda c=c: f(c) for c in range(4)]
    steps += [after_conv, pause, u_mean] + each(u_centre) + root + each(u_scale) + [lambda: u_silus(range(4))]
    steps += each(u_square) + root + each(u_gain)

    m_ready, halves, o_ready = [], [], [[] for _ in range(4)]
    pads = p.memset(mix[:, 4:8, META + S:WIDE], 0.0, [x_ready, mix_rms])
    o_moments = None
    ready = [pair_keys(0), queries(0, 0), queries(1, 1)]
    values = turn_values(pair_values(0))
    values_in = None
    items = [(j, i, hh) for j in range(H2 // 2) for i in range(9) for hh in range(2)]
    turned = []

    def finish(s):
        nonlocal values
        j = s["j"]
        weigh(s, values)
        if s["hh"]:
            turn_back(j, s)
            if s["i"] == 8 and j < 3:
                values = turn_values(values_in)

    current = score(*items[0], ready)
    for n, (j, i, hh) in enumerate(items):
        following = None
        if n + 1 < len(items):
            if items[n + 1][0] > j:
                ready = [pair_keys(j + 1), queries(2 * j + 2, 0), queries(2 * j + 3, 1)]
                values_in = pair_values(j + 1)
            following = score(*items[n + 1], ready)
        if len(turned) == LAG:
            finish(turned.pop(0))
        turn(current)
        turned.append(current)
        fill(FILL2["att"][i] if j < 3 else LATE)
        current = following
        if (j, i, hh) == (3, 0, 0):
            old = p.pe.last()

            def o_start():
                nonlocal o_moments
                o_moments = Moments(p, A[3], [A[2]], after=p.dve.last())
            steps += [lambda k=k: m_ready.append(p.split(M[k], k, 0, WIDE, [u["out"], old])) for k in range(4)]
            steps.append(o_start)
            for k in range(3):
                steps += [lambda k=k: o_moments.square(M[4 + k], [o_ready[k], pads]),
                          lambda k=k: m_ready.append(p.split_scaled(M[4 + k], p.column("attn_out_g_2", k), 4 + k, 0, WIDE, [o_ready[k], pads, old]))]
    for s in turned:
        finish(s)
    fill(len(steps))
    m_ready.append(p.split_scaled(M[7], p.column("attn_out_g_2", 3), 7, 0, WIDE, [o_ready[3], pads, old]))
    o_moments.square(M[7], [o_ready[3], pads])

    done = p.everything()
    back = [Dma(p.sp, p.sem(f"h0_back{i}")) for i in range(4)]
    h_back = [back[i].start(p.res[:, 2 * i:2 * i + 2, :], dram["spill_2"][:, 2 * i:2 * i + 2, :], [done, spilled]) for i in range(4)]
    o_rms = []
    h1, turn_tmp = [], A[2]
    h_moments = Moments(p, T[8], [T[9]], after=done)
    for m in range(8):
        def take_u(view, banks, tok, m=m):
            h1.append(p.tt(grid(p.res[:, m, :]), grid(p.res[:, m, :]), view, ALU.add, [tok, h_back[m // 2]]))
            return h1[m]

        def take_o(view, banks, tok, m=m):
            if m == 0:
                o_rms.append(rms_of(A[3], o_moments.token, 4 * P, A[0], A[1], done))
            e = p.tt(grid(turn_tmp), view, grid(A[0]), ALU.mult, [tok, o_rms, h1[m], p.dve.last()])
            h1[m] = p.tt(p.res[:, m, :], p.res[:, m, :], turn_tmp, ALU.add, [e])
            h_moments.square(p.res[:, m, :], h1[m])
            return e
        for first, take in ((0, take_u), (4, take_o)):
            p.product([block_of("w_out_2", first + k, m * P) for k in range(4)],
                      lambda k, first=first: p.x_hi[:, first + k, :], lambda k, first=first: p.x_lo[:, first + k, :],
                      THREE, m_ready[first:first + 4], take)
            p.drain()
    old = p.pe.last()
    n_ready = [p.split_scaled(p.res[:, k, :], p.column("ffn_norm_g_2", k), k, 0, WIDE, [h1[k], old]) for k in range(8)]
    banks = p.take_slot()
    moments_ready = h_moments.token
    t = p.ones_product(T[8], THREE, banks, moments_ready)
    sums = ps[:, banks[0]:banks[0] + 3, 0:348]
    switch = p.everything()
    ctx.close()
    keep.close()

    ctx = ExitStack()
    RING = 5
    h_hi = p.sbuf("h2_hi", [P, RING, S], F32R, ctx=ctx)
    h_lo = p.sbuf("h2_lo", [P, RING, S], F32R, ctx=ctx)
    up = p.sbuf("up_2", [P, 2, S + 2], ctx=ctx)
    conv = p.sbuf("up_conv_2", [P, 2, S], ctx=ctx)
    ffn_rms = p.sbuf("ffn_rms", [P, WIDE], ctx=ctx)
    scratch = up[:, :, :].rearrange("p a b -> p (a b)")[:, 0:WIDE]
    ffn_rms_ready = p.inverse_root(grid(ffn_rms[:, :]), grid(scratch), sums, D, EPS, [t, switch])
    p.free(banks, ffn_rms_ready)
    gains = p.sbuf("gains_3", [P, 8], ctx=ctx)
    h_used, h_ready = [switch] * RING, {}
    up_free, conv_free = [switch] * 2, [switch] * 2
    acc = list(h1)
    tri = lambda t: t.rearrange("p (a b) -> p a b", a=3)
    gain_ready = p.tt(gains[:, :], p.vec[:, VCOL["final_norm_g_2"]:VCOL["final_norm_g_2"] + 8],
                      p.vec[:, VCOL["pre_norm_g_3"]:VCOL["pre_norm_g_3"] + 8], ALU.mult, switch)

    def hidden(j):
        got = []
        for i in range(2):
            def take(view, banks, tok, i=i):
                e = p.tt(tri(up[:, i, :]), view, tri(ffn_rms[:, META - 2:META + S]), ALU.mult, [tok, up_free[i], ffn_rms_ready])
                chunk = i * FF2 + j
                w = lambda tap: p.column("ffn_conv_w_2", tap * 44 + chunk)
                c = p.ts(conv[:, i, :], up[:, i, 0:S], w(0), p.column("ffn_conv_b_2", chunk), ALU.mult, ALU.add, [e, conv_free[i]])
                c = p.stt(conv[:, i, :], up[:, i, 1:S + 1], w(1), conv[:, i, :], ALU.mult, ALU.add, [c])
                c = p.stt(conv[:, i, :], up[:, i, 2:S + 2], w(2), conv[:, i, :], ALU.mult, ALU.add, [c])
                up_free[i] = c
                if i == 0:
                    c = p.activation(conv[:, 0, :], conv[:, 0, :], ACT.Silu, [c])
                got.append(c)
                return e
            p.product([block_of("w_ffn_up_2", k, i * FF2 * P + j * P) for k in range(8)], hi, lo, FFN2, n_ready, take)
            p.drain()
        c = p.tt(conv[:, 0, :], conv[:, 0, :], conv[:, 1, :], ALU.mult, got)
        conv_free[1] = c
        c = p.split(conv[:, 0, :], j % RING, 0, S, [c, h_used[j % RING]], h_hi, h_lo)
        h_ready[j] = conv_free[0] = c

    m1, m2 = None, None
    x_ready = [None] * 8

    def project(ks, last):
        for m in range(8):
            def take(view, banks, tok, m=m):
                c = acc[m] = p.tt(real(m), real(m), view, ALU.add, [tok, acc[m], n_ready[m]])
                if last:
                    m1.square(real(m), c)
                    m2.square(real(m), c, scale=p.column("final_norm_g_2", m))
                    x_ready[m] = p.split_scaled(real(m), gains[:, m:m + 1], m, 0, S, [c, old, gain_ready])
                return c
            p.product([block_of("w_ffn_down_2", k, m * P) for k in ks],
                      lambda i: h_hi[:, ks[i] % RING, :], lambda i: h_lo[:, ks[i] % RING, :],
                      TWO, [h_ready[k] for k in ks], take)
            p.drain()
        for k in ks:
            h_used[k % RING] = p.pe.last()

    groups = [list(range(0, 2))] + [list(range(g, g + 4)) for g in range(2, FF2, 4)]
    done_to = 0
    for ks in groups:
        ahead = min(ks[-1] + 2, FF2)
        for j in range(done_to, ahead):
            hidden(j)
        done_to = ahead
        last = ks is groups[-1]
        if last:
            old = p.pe.last()
            idle = p.dve.last()
            m1 = Moments(p, conv[:, 0, :], [up[:, 0, 0:S]], after=idle)
            m2 = Moments(p, conv[:, 1, :], [up[:, 1, 0:S]], after=idle)
        project(ks, last)
    moments = [p.ones_product(conv[:, 0, :], TWO, [4, 5], m1.token), p.ones_product(conv[:, 1, :], TWO, [6, 7], m2.token)]
    switch = p.everything()
    ctx.close()
    return x_ready, moments, switch


def layer_3(p, x_ready, moments, switch, out):
    dram, ps = p.dram, p.ps
    hi, lo = p.x_parts()
    real = lambda k: p.res[:, k, META:META + S]
    grid = lambda t: t.rearrange("p (a b) -> p a b", a=2)
    chunks = lambda t: t.rearrange("p (c l) -> p c l", l=CHUNK)
    ctx = ExitStack()
    mix = p.sbuf("mix_3", [P, 8, S], ctx=ctx)
    work = p.sbuf("work_3", [P, 7, S], ctx=ctx)
    w_a2 = p.sbuf("w_a2", [16, 4, P], ctx=ctx)
    pair = p.sbuf("pair_scores", [P, 2, P], ctx=ctx)
    ends = p.sbuf("chunk_decay", [P, 16], ctx=ctx)
    M = [mix[:, i, :] for i in range(8)]
    W = [work[:, i, :] for i in range(7)]

    rms, tmp, rms2 = W[0], W[1], W[2]
    first = p.inverse_root(grid(rms), grid(tmp), ps[:, 4:6, :], D, EPS, [moments, switch])
    p.free([4, 5], first)
    c = p.tt(tmp, rms, rms, ALU.mult, [first])
    c = p.tt(grid(tmp), ps[:, 6:8, :], grid(tmp), ALU.mult, [c, moments])
    p.free([6, 7], c)
    c = p.inverse_root(rms2, W[3], tmp, D, EPS, [c, switch])
    scale_ready = p.tt(rms2, rms2, rms, ALU.mult, [c])
    x_in = [p.stt(real(k), real(k), p.column("final_norm_g_2", k), rms, ALU.mult, ALU.mult, [first, x_ready[k]]) for k in range(8)]
    spill = Dma(p.sp, p.sem("x3_spilled"))
    spilled = spill.start(dram["spill_3"][:, :, 0:S], p.res[:, :, META:META + S], x_in)
    w_a2_dma = Dma(p.sp, p.sem("w_a2_landed"))
    w_a2_ready = w_a2_dma.start(w_a2[:, :, :], dram["w_a2"].rearrange("r (h c) -> r h c", h=4), switch)
    free = [spilled, x_in, switch]
    T = [p.res[:, i, 0:S] for i in range(8)]

    def w_in(col, take, n=P):
        p.product([block_of("w_in_3", k, col if n == P else [(0, col, n)]) for k in range(8)], hi, lo, TWO, x_ready, take)

    def scaled(out, func, after, told):
        def take(view, banks, tok):
            e = p.tt(grid(out), view, grid(rms2), ALU.mult, [tok, scale_ready, after])
            told(p.activation(out, out, func, [e]) if func else e)
            return e
        return take

    w_s, b_s = T[6].rearrange("p (g t) -> p g t", g=8), T[7]
    s_dma = Dma(p.sp, p.sem("w_s_landed"))
    s_dma.start(w_s, dram["a_w_s"], free)
    landed = s_dma.start(b_s, dram["a_b_s"].broadcast_to([P, 8 * P]), free)
    total, mean, root = W[3], W[4], T[0]
    v_ready, summed = {}, [None]

    def told_v(g):
        def told(tok):
            v_ready[g] = tok
            if g:
                summed[0] = p.tt(total, M[0] if g == 1 else total, M[g], ALU.add, [v_ready[0], tok, summed[0], scale_ready])
        return told

    for g in range(8):
        w_in(OFF3["v"] + g * P, scaled(M[g], ACT.Gelu, switch, told_v(g)))
    p.drain()
    masked = p.tt(w_s, w_s, p.upper[:, :].unsqueeze(1).broadcast_to([P, 8, P]), ALU.mult, [landed, p.const])
    u_g, s_g, u_tok, s_tok, lr_tok = [W[5], W[6]], [T[1], T[2]], {}, {}, []
    gates_used = [free, free]

    def gate_products(g):
        r = g % 2
        w_in(OFF3["u"] + g * P, scaled(u_g[r], ACT.Gelu, gates_used[r], lambda t: u_tok.update({g: t})))
        w_in(OFF3["gate"] + g * P, scaled(s_g[r], ACT.Silu, gates_used[r], lambda t: s_tok.update({g: t})))

    lr = T[5]

    def take_lr(view, banks, tok):
        lr_tok.append(p.tt(grid(lr)[0:16], ps[0:16, banks[0]:banks[0] + 2, :], grid(rms2)[0:16], ALU.mult, [tok, scale_ready, free]))
        return lr_tok[0]

    w_in(OFF3["lr"], take_lr, 16)
    gate_products(0)
    gate_products(1)
    s = p.ones_product(total, TWO, [4, 5], summed[0])
    p.pump(4)
    v_done = [PerPiece([None] * 2) for _ in range(8)]

    def apply(g, i, cols, x, c):
        v_done[g][i] = p.activation(x, x, ACT.Identity, [c], bias=p.column("a_ln_b_3", g))

    layer_norm(p, M, v_ready, s, mean, root, W[1], [T[3], T[4]], D, EPS, "a_ln_g_3", apply, [free, p.dve.last()], fill=2)
    p.drain()
    v_t, sp_t = [W[3], W[4]], T[3]
    vt_used, spilled_a = [p.everything()] * 2, []
    spill_a = [Dma(p.sp, p.sem(f"a_spilled{i}")) for i in range(2)]
    for g in range(8):
        r = g % 2
        vt = v_t[r]
        t_ready = []
        for half in range(2):
            t = p.mm([(ps[:, 6 + half, i * P:(i + 1) * P], M[g][:, (4 * half + i) * P:(4 * half + i + 1) * P], p.ident[:, :], True, True)
                      for i in range(4)], [v_done[g][half], p.bank_free[6 + half]], transpose=True)
            e = p.copy(vt[:, half * 512:(half + 1) * 512], ps[:, 6 + half, :], [t, vt_used[r]])
            p.free([6 + half], e)
            t_ready.append(e)
        p.pump(4)
        t = p.mm([(ps[:, 4 + n // 4, (n % 4) * P:(n % 4 + 1) * P], vt[:, n * P:(n + 1) * P], w_s[:, g, :], True, True) for n in range(8)],
                 [t_ready, masked, p.bank_free[4], p.bank_free[5]])
        vt_used[r] = t
        bias = b_s[:, g * P:(g + 1) * P].unsqueeze(1).broadcast_to([P, 8, P])
        c = p.tt(sp_t.rearrange("p (n t) -> p n t", n=8), ps[:, 4:6, :].rearrange("p a (n t) -> p (a n) t", t=P), bias, ALU.add, [t, landed, p.dve.last(), vt_used])
        p.free([4, 5], c)
        c = p.tt(u_g[r], u_g[r], sp_t, ALU.mult, [c, u_tok[g]])
        c = p.tt(M[g], u_g[r], s_g[r], ALU.mult, [c, s_tok[g], t_ready])
        gates_used[r] = c
        spilled_a.append(spill_a[r].start(dram["spill_a"][:, g, 0:S], M[g], [c, spilled_a[g - 2] if g >= 2 else None]))
        p.drain()
        if g + 2 < 8:
            gate_products(g + 2)

    q_in, k_in = M[6], M[7]
    qb, kd, reset, qe, ke, kd_tok = T[0], T[1], T[2], T[3], T[4], T[6]
    v_f, v0, v1, b_t, e_t, g0, g1 = T[7], W[0], W[1], W[3], W[4], W[5], W[6]
    states = p.sbuf("states", [P, 4, 256], ctx=ctx)
    start = p.everything()
    z = [p.memset(pair[:, :, :], 0.0, switch)]
    c = p.memset(reset, 1.0, [start])
    z.append(p.memset(chunks(reset)[:, :, 0:1], 0.0, [c]))
    SCALE = P ** -0.5
    TAU = 1.0 / 16.0
    b_ready = []
    st = dict(q=[start, spilled_a], v_f=start, v0=start, v1=start, done=start, gates=start)
    got = {}

    def tell(name):
        return lambda tok: got.update({name: tok})

    def q_and_k(h):
        w_in(OFF3["q"] + h * P, scaled(q_in, None, st["q"], tell(("q", h))))
        w_in(OFF3["k"] + h * P, scaled(k_in, None, st["q"], tell(("k", h))))

    def v_product(h, i):
        w_in(OFF3["bv"] + (2 * h + i) * P, scaled(v_f, None, st["v_f"], tell(("v", h, i))))

    def gate_product(h, i, dst):
        w_in(OFF3["bgate"] + (2 * h + i) * P, scaled(dst, ACT.Silu, st["gates"], tell(("g", h, i))))

    def turn_v(h, i, dst):
        out = []
        for half in range(2):
            t = p.mm([(ps[:, 6 + half, n * P:(n + 1) * P], v_f[:, (4 * half + n) * P:(4 * half + n + 1) * P], p.ident[:, :], True, True)
                      for n in range(4)], [got["v", h, i], p.bank_free[6 + half]], transpose=True)
            c = p.copy(dst[:, half * 512:(half + 1) * 512], ps[:, 6 + half, :], [t, st["done"]])
            p.free([6 + half], c)
            out.append(c)
        st["v_f"] = t
        return out

    q_and_k(0)
    v_product(0, 0)
    p.drain()
    for h in range(H3):
        done = st["done"]
        ready = turn_v(h, 0, v0)
        v_product(h, 1)
        gate_product(h, 0, g0)
        gate_product(h, 1, g1)
        t = p.mm([(ps[:, 4 + i, :], w_a2[:, h, :], lr[0:16, i * 512:(i + 1) * 512], True, True) for i in range(2)],
                 [lr_tok, w_a2_ready, p.bank_free[4], p.bank_free[5]])
        x = p.ts(qe, ps[:, 4:6, :], p.column("b_a2_3", h), None, ALU.add, None, [t, done])
        p.free([4, 5], x)
        c = p.stt(e_t, qe, -1.0, qe, ALU.mult, ALU.max, [x, done])
        c = p.activation(e_t, e_t, ACT.Exp, [c], scale=-1.0)
        c = p.activation(e_t, e_t, ACT.Ln, [c], bias=p.tiny[:, 2:3])
        c = p.stt(e_t, qe, 0.0, e_t, ALU.min, ALU.subtract, [c])
        b = p.dve.do(lambda e: e.tensor_tensor_scan(b_t, reset, e_t, 0.0, ALU.mult, ALU.add), [c, z, done])
        ref = chunks(b_t)[:, :, CHUNK // 2 - 1:CHUNK // 2].broadcast_to([P, 16, CHUNK])
        end = chunks(b_t)[:, :, CHUNK - 1:CHUNK]
        decay = p.activation(ends[:, :], end.rearrange("p c l -> p (c l)"), ACT.Exp, [b, done], scale=TAU)
        d = p.tt(chunks(kd), chunks(b_t), ref, ALU.subtract, [b, done])
        c1 = p.activation(e_t, kd, ACT.Exp, [d], scale=TAU)
        c2 = p.activation(ke, kd, ACT.Exp, [d, done], scale=-TAU)
        c3 = p.activation(qb, b_t, ACT.Exp, [b, done], scale=TAU)
        d = p.tt(chunks(kd), end.broadcast_to([P, 16, CHUNK]), chunks(b_t), ALU.subtract, [c1, c2])
        c4 = p.activation(kd, kd, ACT.Exp, [d], scale=TAU)
        r1 = p.stt(qe, q_in, SCALE, e_t, ALU.mult, ALU.mult, [c1, got["q", h]])
        r2 = p.tt(ke, ke, k_in, ALU.mult, [c2, got["k", h]])
        r3 = p.stt(qb, q_in, SCALE, qb, ALU.mult, ALU.mult, [c3])
        r4 = p.tt(kd, kd, k_in, ALU.mult, [c4])
        st["q"] = r4
        p.drain()
        ready += [r1, r2, r3] + turn_v(h, 1, v1)
        for half in range(2):
            t = p.mm([(ps[:, 6 + half, n * P:(n + 1) * P], kd[:, (4 * half + n) * P:(4 * half + n + 1) * P], p.ident[:, :], True, True)
                      for n in range(4)], [r4, p.bank_free[6 + half]], transpose=True)
            c = p.copy(kd_tok[:, half * 512:(half + 1) * 512], ps[:, 6 + half, :], [t, done])
            p.free([6 + half], c)
            ready.append(c)
        if h + 1 < H3:
            q_and_k(h + 1)
            v_product(h + 1, 0)
        else:
            old = p.pe.last()
            operand = [p.split(M[k], k, 0, S, [b_ready[k], old]) for k in range(6)]
        state = lambda c: states[:, c % 4, :]
        s_ready, s_used, pair_used, o_last = {}, {}, [done, done], []

        def update(c):
            n, rows = c // 2, slice(64 * (c % 2), 64 * (c % 2) + 64)
            t = p.mm([(ps[:, 7, i * P:(i + 1) * P], kd_tok[rows, n * P:(n + 1) * P], v[rows, n * P:(n + 1) * P], True, True)
                      for i, v in enumerate((v0, v1))], [ready, p.bank_free[7]])
            if c == 0:
                s = p.dcopy(state(1), ps[:, 7, 0:256], [t, done])
            else:
                s = p.stt(state(c + 1), state(c), ends[:, c:c + 1], ps[:, 7, 0:256], ALU.mult, ALU.add,
                          [t, s_ready[c], decay, s_used.get(c - 3)])
            p.free([7], s)
            s_ready[c + 1] = s

        def masked_scores(n):
            bank = 4 + n % 2
            cols = slice(n * P, (n + 1) * P)
            t = p.mm([(ps[:, bank, 0:P], ke[:, cols], qe[:, cols], True, True)], [ready, p.bank_free[bank]])
            tri = pair[:, n % 2, :]
            c1 = p.tt(tri[0:64, 0:64], ps[0:64, bank, 0:64], p.upper[0:64, 0:64], ALU.mult, [t, z, pair_used[n % 2]])
            c2 = p.tt(tri[64:128, 64:128], ps[64:128, bank, 64:128], p.upper[64:128, 64:128], ALU.mult, [t, z])
            p.free([bank], c2)
            return [c1, c2]

        update(0)
        following = masked_scores(0)
        p.pump(3)
        for n in range(8):
            cols = slice(n * P, (n + 1) * P)
            tri = pair[:, n % 2, :]
            now = following
            if n < 7:
                update(2 * n + 1)
                following = masked_scores(n + 1)
            products = []
            for i, v in enumerate((v0, v1)):
                o = i * P
                products.append((ps[:, 6, o:o + P], v[:, cols], tri, True, False))
                if n:
                    products.append((ps[:, 6, o:o + 64], state(2 * n)[:, o:o + P], qb[:, n * P:n * P + 64], False, False))
                products.append((ps[:, 6, o + 64:o + P], state(2 * n + 1)[:, o:o + P], qb[:, n * P + 64:(n + 1) * P], False, True))
            t = p.mm(products, [now, s_ready.get(2 * n), s_ready[2 * n + 1], p.bank_free[6]])
            pair_used[n % 2] = s_used[2 * n] = s_used[2 * n + 1] = t
            e = p.copy(mix[:, 2 * h:2 * h + 2, cols], ps[:, 6, 0:256].rearrange("p (i t) -> p i t", i=2), [t, spilled_a, st["q"]])
            p.free([6], e)
            o_last.append(e)
            if n < 7:
                update(2 * n + 2)
            p.pump(2)
        pe_done = p.pe.last()
        rs, _ = p.norm([M[2 * h], M[2 * h + 1]], [o_last, o_last], TWO, 256, EPS, (b_t, e_t, qe), (ke, kd_tok), banks=(4, 5), after=pe_done, fill=10)
        for i, g in enumerate((g0, g1)):
            c = p.stt(M[2 * h + i], M[2 * h + i], p.column("b_norm_g_3", 2 * h + i), b_t, ALU.mult, ALU.mult, [rs])
            c = p.tt(M[2 * h + i], M[2 * h + i], g, ALU.mult, [c, got["g", h, i]])
            b_ready.append(c)
        p.drain()
        st["gates"] = c
        st["done"] = [c, p.pe.last(), p.act.last()]

    operand += [p.split(M[k], k, 0, S, [b_ready[k], old]) for k in (6, 7)]
    done = p.everything()
    a_back = [Dma(p.sp, p.sem(f"a_back{i}")) for i in range(4)]
    a_landed = [a_back[i].start(p.res[:, 2 * i:2 * i + 2, 0:S], dram["spill_a"][:, 2 * i:2 * i + 2, 0:S], [done, spilled_a]) for i in range(4)]
    switch = p.everything()
    ctx.close()
    ctx = ExitStack()
    a_plain = p.same_place("a_plain", [P, 2, 8, S])
    a_hi = p.sbuf("a_hi", [P, 8, S], F32R, ctx=ctx)
    a_lo = p.sbuf("a_lo", [P, 8, S], F32R, ctx=ctx)
    last = p.sbuf("last_scratch", [P, 2, 512], ctx=ctx)
    operand += [p.split(p.res[:, k, 0:S], k, 0, S, [a_landed[k // 2], switch], a_hi, a_lo) for k in range(8)]
    y = [p.res[:, k, 0:S] for k in range(8)]
    x_landed = [[], []]
    stores = [Dma(p.sp, p.sem(f"stored{k}")) for k in range(4)]
    tokens, stats = [], []
    total, square = last[:, 0, :], last[:, 1, :]

    def post_norm(i, fill):
        cols = slice(512 * i, 512 * i + 512)
        ready, t = stats[i]
        root = a_plain[:, 0, 2 * i, 0:512]
        rs = p.inverse_root(root, a_plain[:, 0, 2 * i + 1, 0:512], ps[:, 6 + i, :], D, EPS, [t])
        p.free([6 + i], rs)
        for k in range(8):
            x = y[k][:, cols]
            c = p.stt(x, x, p.column("post_norm_g_3", k), root, ALU.mult, ALU.mult, [rs, ready[k]])
            c = p.tt(x, x, p.x_plain[:, i, k, 0:512], ALU.add, [c, x_landed[i][k // 4]])
            tokens.append(stores[k % 4].start(out[k][:, cols], x, [c, tokens[-4] if len(tokens) >= 4 else None]))
            p.pump(fill)

    for i in range(2):
        cols = slice(512 * i, 512 * i + 512)
        m = Moments(p, total, [square], after=[switch, stats[0][1] if i else None])
        ready = []
        for k in range(8):
            def take(view, banks, tok, k=k, m=m, ready=ready, cols=cols):
                c = p.copy(y[k][:, cols], view[:, 0, :], [tok, operand[8 + k]])
                m.square(y[k][:, cols], c)
                ready.append(c)
                return c
            p.product([block_of("w_out_3", (8 + c) % 16, k * P) for c in range(16)],
                      lambda c: (p.x_hi if c < 8 else a_hi)[:, c % 8, :], lambda c: (p.x_lo if c < 8 else a_lo)[:, c % 8, :],
                      TWO[i:i + 1], operand, take)
        if i:
            p.pump(8)
            post_norm(0, 4)
        p.drain()
        t = p.mm([(ps[:, 6 + i, :], p.ones[:, :], total, True, True)], [m.token, p.bank_free[6 + i]])
        stats.append((ready, t))
        if i == 0:
            for j in range(2):
                for half in range(2):
                    dma = Dma(p.sp, p.sem(f"x3_back{j}{half}"))
                    k = slice(4 * half, 4 * half + 4)
                    x_landed[j].append(dma.start(p.x_plain[:, j, k, 0:512],
                                                 dram["spill_3"][:, k, 512 * j:512 * j + 512], [t, spilled]))
    post_norm(1, 0)
    p.sp.wait(tokens)
    ctx.close()


def run_layers(p, out):
    result = layer_1(p)
    result = layer_2(p, *result)
    layer_3(p, *result, out)
    assert len(p.blocks) == N_BLOCKS and not p.jobs, (len(p.blocks), N_BLOCKS)


def build(nc, dram, out):
    ctx = ExitStack()
    with ctx:
        p = Program(nc, ctx, dram)
        run_layers(p, out)
        with nc.Block() as block:
            @block.sync
            def _(e):
                p.sp.emit(e)

            @block.tensor
            def _(e):
                p.pe.emit(e)

            @block.vector
            def _(e):
                p.dve.emit(e)

            @block.scalar
            def _(e):
                p.act.emit(e)

            @block.gpsimd
            def _(e):
                p.pool.emit(e)
    return p.blocks


def weight_array(blocks, inputs):
    w = np.zeros((N_TILES, P, BLOCKS, P), np.float32)
    for i, (name, row, rows, cols) in enumerate(blocks):
        src = inputs[name][0]
        for to, start, n in cols:
            w[i // BLOCKS, 0:rows, i % BLOCKS, to:to + n] = src[row:row + rows, start:start + n]
    return w


def constant_arrays():
    head_row = np.zeros((H1, H1, P), np.float32)
    head_row[np.arange(H1), np.arange(H1)] = 1.0
    fix = np.ones((P, 4, 16), np.float32)
    for g in range(4):
        fix[:, g] = (2 << g) / np.minimum(np.arange(1, 17), 2 << g)
    freq = (np.float32(1.0) / np.float32(10000.0) ** (np.arange(0, ROPE, 2, dtype=np.float32) / np.float32(ROPE))).astype(np.float32)
    angle = (np.arange(WIDE, dtype=np.float32)[None, :] * freq[:, None]).astype(np.float32)
    rope = np.zeros((P, WIDE), np.float32)
    rope[64:80] = rope[80:96] = np.cos(angle)
    rope[96:112], rope[112:128] = -np.sin(angle), np.sin(angle)
    return {"identity": np.eye(P, dtype=np.float32), "upper": np.triu(np.ones((P, P), np.float32)),
            "head_row": head_row, "pool_fix": fix, "rope": rope}


def kernel(**inputs):
    import concourse.bacc as bacc
    from concourse.bass_utils import run_bass_kernel_spmd

    inputs = {k: np.asarray(v) for k, v in inputs.items()}
    nc = bacc.Bacc("TRN2", target_bir_lowering=False, num_devices=1)
    vectors = np.concatenate([inputs[name].reshape(-1, P) for name, _ in VECTORS]).T
    gate_bias = np.zeros((P, 1), np.float32)
    gate_bias[0:4, 0], gate_bias[32:36, 0] = inputs["b_gate"][0, :4], inputs["b_gate"][0, 4:]
    arrays = {
        "x": inputs["x"][0].T.reshape(DC, P, S),
        "vectors": vectors,
        "gate_bias": gate_bias,
        "w_pool": inputs["w_pool"][0].transpose(1, 0, 2),
        "meta": inputs["meta_tokens_2"].T.reshape(DC, P, META).transpose(1, 0, 2),
        "w_a2": inputs["w_a2_3"][0],
        "a_w_s": inputs["a_w_s_3"][0].transpose(2, 0, 1),
        "a_b_s": inputs["a_b_s_3"][0].reshape(1, 8 * P),
        **constant_arrays(),
    }
    arrays = {k: np.ascontiguousarray(v) for k, v in arrays.items()}
    dram = {k: nc.dram_tensor(f"{k}_dram", v.shape, mybir.dt.from_np(v.dtype), kind="ExternalInput").ap()
            for k, v in arrays.items()}
    dram["w"] = nc.dram_tensor("w_dram", (N_TILES, P, BLOCKS, P), F32, kind="ExternalInput").ap()
    for name in ("spill_2", "spill_3", "spill_a"):
        dram[name] = nc.dram_tensor(name, (P, DC, WIDE), F32).ap()
    out = nc.dram_tensor("out_dram", (DC, P, S), F32, kind="ExternalOutput").ap()
    blocks = build(nc, dram, out)
    arrays["w"] = weight_array(blocks, inputs)
    r = run_bass_kernel_spmd(nc, [{f"{k}_dram": v for k, v in arrays.items()}], core_ids=[0])
    return np.ascontiguousarray(r.results[0]["out_dram"].reshape(D, S).T)[None]
```
